# Optimizing a Trainium2 kernel written in Bass

```python
import math
import jax
import jax.numpy as jnp
from jax import lax
import numpy as np
import jax, jax.numpy as jnp

D_MODEL = 1024
BATCH = 1
SEQ = 256
DEPTH = 1

CHUNK = 64
Q_BLOCK = 128
EPS = 1e-6
NEG_INF = -1e30

N_ATTN_HEADS = 8
HEAD_DIM = D_MODEL // (2 * N_ATTN_HEADS)
V_HEAD_DIM = 2 * HEAD_DIM
QK_WIDTH = N_ATTN_HEADS * 2 * HEAD_DIM
ATTN_WIDTH = N_ATTN_HEADS * V_HEAD_DIM

D_RNN = (5 * D_MODEL) // 4
RNN_BLOCK = 64
N_RNN_BLOCKS = D_RNN // RNN_BLOCK
CONV_WIDTH = 4
RG_C = 8.0

N_BRANCH = 2
IN_SPLITS = (QK_WIDTH, 2 * QK_WIDTH, 2 * QK_WIDTH + ATTN_WIDTH,
             2 * QK_WIDTH + ATTN_WIDTH + D_RNN, 2 * QK_WIDTH + ATTN_WIDTH + 2 * D_RNN)
IN_COLS = 2 * QK_WIDTH + ATTN_WIDTH + 2 * D_RNN + N_BRANCH * D_MODEL

PEER_HEADS = 8
PEER_N_KEYS = 128
PEER_N_EXPERTS = PEER_N_KEYS ** 2
PEER_QDIM = 256
PEER_HALF = PEER_QDIM // 2
PEER_TOPK = 16
PEER_BLOCK = 128


def rms_norm(x, g):
    xf = x.astype(jnp.float32)
    y = xf * lax.rsqrt(jnp.mean(xf * xf, axis=-1, keepdims=True) + EPS)
    return (y * g.astype(jnp.float32)).astype(x.dtype)

def diff_attention(q, k, v, q_norm_g, k_norm_g, lambda_q1, lambda_k1, lambda_q2, lambda_k2,
                   subln_g, lam_init):
    b, s = q.shape[0], q.shape[1]
    n_blk = s // Q_BLOCK
    q = rms_norm(q, q_norm_g)
    k = rms_norm(k, k_norm_g)
    lam = (jnp.exp(jnp.sum(lambda_q1.astype(jnp.float32) * lambda_k1.astype(jnp.float32)))
           - jnp.exp(jnp.sum(lambda_q2.astype(jnp.float32) * lambda_k2.astype(jnp.float32)))
           + lam_init)
    scale = HEAD_DIM ** -0.5
    key_chunk = jnp.arange(s) // CHUNK
    q_blocks = q.reshape(b, n_blk, Q_BLOCK, N_ATTN_HEADS, 2, HEAD_DIM).transpose(1, 0, 2, 3, 4, 5)

    def one_block(args):
        q_blk, blk = args
        scores = jnp.einsum('bqhcd,bkhcd->bhcqk', q_blk, k).astype(jnp.float32) * scale
        q_chunk = (blk * Q_BLOCK + jnp.arange(Q_BLOCK)) // CHUNK
        visible = key_chunk[None, :] <= q_chunk[:, None]
        scores = jnp.where(visible, scores, NEG_INF)
        probs = jax.nn.softmax(scores, axis=-1)
        diff = probs[:, :, 0] - lam * probs[:, :, 1]
        return jnp.einsum('bhqk,bkhd->bqhd', diff.astype(v.dtype), v)

    o = lax.map(one_block, (q_blocks, jnp.arange(n_blk)))
    o = o.transpose(1, 0, 2, 3, 4).reshape(b, s, N_ATTN_HEADS, V_HEAD_DIM)
    o = rms_norm(o, subln_g) * (1.0 - lam_init)
    return o.reshape(b, s, ATTN_WIDTH)

def causal_depthwise_conv(x, w, bias):
    s = x.shape[1]
    xp = jnp.pad(x, ((0, 0), (CONV_WIDTH - 1, 0), (0, 0)))
    y = bias
    for tap in range(CONV_WIDTH):
        y = y + xp[:, tap:tap + s] * w[tap]
    return y

def rg_lru(x, w_a, b_a, w_x, b_x, rg_lambda):
    b, s, _ = x.shape
    xb = x.reshape(b, s, N_RNN_BLOCKS, RNN_BLOCK)
    gate_r = jax.nn.sigmoid(jnp.einsum('bsgi,gij->bsgj', xb, w_a).reshape(b, s, D_RNN) + b_a)
    gate_i = jax.nn.sigmoid(jnp.einsum('bsgi,gij->bsgj', xb, w_x).reshape(b, s, D_RNN) + b_x)
    log_a = -RG_C * gate_r.astype(jnp.float32) * jax.nn.softplus(-rg_lambda.astype(jnp.float32))
    a = jnp.exp(log_a)
    mult = jnp.sqrt(-jnp.expm1(2.0 * log_a))
    u = mult * (gate_i * x).astype(jnp.float32)

    def combine(left, right):
        a_l, u_l = left
        a_r, u_r = right
        return a_l * a_r, a_r * u_l + u_r

    _, h = lax.associative_scan(combine, (a, u), axis=1)
    return h.astype(x.dtype)

def peer_ffn(h, w_q, sub_keys, u_tab, v_tab):
    b, s, d = h.shape
    tokens = h.reshape((b * s) // PEER_BLOCK, PEER_BLOCK, d)

    def one_block(hb):
        q = (hb @ w_q).reshape(PEER_BLOCK, PEER_HEADS, 2, PEER_HALF)
        sc = jnp.einsum('thcd,hcnd->thcn', q, sub_keys).astype(jnp.float32)
        s1, i1 = lax.top_k(sc[:, :, 0], PEER_TOPK)
        s2, i2 = lax.top_k(sc[:, :, 1], PEER_TOPK)
        cand_s = (s1[..., :, None] + s2[..., None, :]).reshape(PEER_BLOCK, PEER_HEADS, PEER_TOPK * PEER_TOPK)
        cand_i = (i1[..., :, None] * PEER_N_KEYS + i2[..., None, :]).reshape(PEER_BLOCK, PEER_HEADS, PEER_TOPK * PEER_TOPK)
        top_s, pos = lax.top_k(cand_s, PEER_TOPK)
        idx = jnp.take_along_axis(cand_i, pos, axis=-1)
        g = jax.nn.softmax(top_s, axis=-1)
        u = u_tab[idx]
        act = jax.nn.gelu(jnp.einsum('thkd,td->thk', u, hb))
        wts = (g * act.astype(jnp.float32)).astype(hb.dtype)
        v = v_tab[idx]
        return jnp.einsum('thk,thkd->td', wts, v)

    out = lax.map(one_block, tokens)
    return out.reshape(b, s, d)

def hybrid_block(x, lam_init, norm1_g, w_in, b_gate, q_norm_g, k_norm_g, lambda_q1, lambda_k1,
                 lambda_q2, lambda_k2, subln_g, conv_w, conv_b, w_rg_a, b_rg_a, w_rg_x, b_rg_x,
                 rg_lambda, w_br_attn, w_br_rnn, w_out, norm2_g, w_peer_q, peer_sub_keys,
                 peer_u, peer_v):
    b, s, _ = x.shape
    h = rms_norm(x, norm1_g)
    z = h @ w_in
    q, k, v, xr, yr, gate_logits = jnp.split(z, IN_SPLITS, axis=-1)
    q = q.reshape(b, s, N_ATTN_HEADS, 2, HEAD_DIM)
    k = k.reshape(b, s, N_ATTN_HEADS, 2, HEAD_DIM)
    v = v.reshape(b, s, N_ATTN_HEADS, V_HEAD_DIM)
    attn = diff_attention(q, k, v, q_norm_g, k_norm_g, lambda_q1, lambda_k1, lambda_q2,
                          lambda_k2, subln_g, lam_init)
    rnn = rg_lru(causal_depthwise_conv(xr, conv_w, conv_b), w_rg_a, b_rg_a, w_rg_x, b_rg_x,
                 rg_lambda) * jax.nn.gelu(yr)
    gates = jax.nn.sigmoid(gate_logits + b_gate).reshape(b, s, N_BRANCH, D_MODEL)
    merged = gates[:, :, 0] * (attn @ w_br_attn) + gates[:, :, 1] * (rnn @ w_br_rnn)
    x = x + merged @ w_out
    x = x + peer_ffn(rms_norm(x, norm2_g), w_peer_q, peer_sub_keys, peer_u, peer_v)
    return x

def first_inputs(seed: int = 0) -> dict:
    key = jax.random.key(seed)
    ks = jax.random.split(key, 26)
    L = DEPTH

    def nrm(k, shape, scale):
        return jax.random.normal(k, shape, jnp.float32) * scale

    a0 = jax.random.uniform(ks[17], (L, D_RNN), jnp.float32, 0.9, 0.999)
    return {
        'x': nrm(ks[0], (BATCH, SEQ, D_MODEL), 1.0),
        'norm1_g': 1.0 + nrm(ks[1], (L, D_MODEL), 0.02),
        'w_in': nrm(ks[2], (L, D_MODEL, IN_COLS), D_MODEL ** -0.5),
        'b_gate': nrm(ks[3], (L, N_BRANCH * D_MODEL), 0.02),
        'q_norm_g': 1.0 + nrm(ks[4], (L, HEAD_DIM), 0.02),
        'k_norm_g': 1.0 + nrm(ks[5], (L, HEAD_DIM), 0.02),
        'lambda_q1': nrm(ks[6], (L, HEAD_DIM), 0.1),
        'lambda_k1': nrm(ks[7], (L, HEAD_DIM), 0.1),
        'lambda_q2': nrm(ks[8], (L, HEAD_DIM), 0.1),
        'lambda_k2': nrm(ks[9], (L, HEAD_DIM), 0.1),
        'subln_g': 1.0 + nrm(ks[10], (L, V_HEAD_DIM), 0.02),
        'conv_w': nrm(ks[11], (L, CONV_WIDTH, D_RNN), CONV_WIDTH ** -0.5),
        'conv_b': nrm(ks[12], (L, D_RNN), 0.02),
        'w_rg_a': nrm(ks[13], (L, N_RNN_BLOCKS, RNN_BLOCK, RNN_BLOCK), RNN_BLOCK ** -0.5),
        'b_rg_a': nrm(ks[14], (L, D_RNN), 0.02),
        'w_rg_x': nrm(ks[15], (L, N_RNN_BLOCKS, RNN_BLOCK, RNN_BLOCK), RNN_BLOCK ** -0.5),
        'b_rg_x': nrm(ks[16], (L, D_RNN), 0.02),
        'rg_lambda': jnp.log(a0) - jnp.log1p(-a0),
        'w_br_attn': nrm(ks[18], (L, ATTN_WIDTH, D_MODEL), ATTN_WIDTH ** -0.5),
        'w_br_rnn': nrm(ks[19], (L, D_RNN, D_MODEL), D_RNN ** -0.5),
        'w_out': nrm(ks[20], (L, D_MODEL, D_MODEL), D_MODEL ** -0.5),
        'norm2_g': 1.0 + nrm(ks[21], (L, D_MODEL), 0.02),
        'w_peer_q': nrm(ks[22], (L, D_MODEL, PEER_HEADS * PEER_QDIM), D_MODEL ** -0.5),
        'peer_sub_keys': nrm(ks[23], (L, PEER_HEADS, 2, PEER_N_KEYS, PEER_HALF), PEER_HALF ** -0.5),
        'peer_u': nrm(ks[24], (L, PEER_N_EXPERTS, D_MODEL), D_MODEL ** -0.5),
        'peer_v': nrm(ks[25], (L, PEER_N_EXPERTS, D_MODEL), PEER_HEADS ** -0.5),
    }

def first_block(x, norm1_g, w_in, b_gate, q_norm_g, k_norm_g, lambda_q1, lambda_k1, lambda_q2,
              lambda_k2, subln_g, conv_w, conv_b, w_rg_a, b_rg_a, w_rg_x, b_rg_x, rg_lambda,
              w_br_attn, w_br_rnn, w_out, norm2_g, w_peer_q, peer_sub_keys, peer_u, peer_v):
    for layer in range(DEPTH):
        lam_init = 0.8 - 0.6 * math.exp(-0.3 * layer)
        x = hybrid_block(x, lam_init, norm1_g[layer], w_in[layer], b_gate[layer], q_norm_g[layer],
                         k_norm_g[layer], lambda_q1[layer], lambda_k1[layer], lambda_q2[layer],
                         lambda_k2[layer], subln_g[layer], conv_w[layer], conv_b[layer],
                         w_rg_a[layer], b_rg_a[layer], w_rg_x[layer], b_rg_x[layer],
                         rg_lambda[layer], w_br_attn[layer], w_br_rnn[layer], w_out[layer],
                         norm2_g[layer], w_peer_q[layer], peer_sub_keys[layer], peer_u[layer],
                         peer_v[layer])
    return x


N_HEADS = 8
HEAD_DIM_2 = 64
ATTN_WIDTH_2 = N_HEADS * HEAD_DIM_2
CONV_WIDTH_2 = D_MODEL // 2
CONV_KERNEL = 31
N_EXPERTS = 32
TOP_K = 4
D_EXPERT = D_MODEL
SWIGLU_LIMIT = 7.0
SWIGLU_ALPHA = 1.702
MOE_BLOCK = 128
RMS_EPS = 1e-5
LN_EPS = 1e-5
N_MOD = 6
COL_SIZES = (CONV_WIDTH_2, CONV_WIDTH_2,
             ATTN_WIDTH_2, ATTN_WIDTH_2, ATTN_WIDTH_2,
             N_HEADS,
             D_MODEL, D_MODEL)
IN_COLS_2 = sum(COL_SIZES)


def rms_norm_2(x, g):
    xf = x.astype(jnp.float32)
    y = xf * lax.rsqrt(jnp.mean(xf * xf, axis=-1, keepdims=True) + RMS_EPS)
    return (y * g.astype(jnp.float32)).astype(x.dtype)

def layer_norm(x, g, b):
    xf = x.astype(jnp.float32)
    mu = jnp.mean(xf, axis=-1, keepdims=True)
    var = jnp.mean(jnp.square(xf - mu), axis=-1, keepdims=True)
    y = (xf - mu) * lax.rsqrt(var + LN_EPS)
    return (y * g.astype(jnp.float32) + b.astype(jnp.float32)).astype(x.dtype)

def conv_module(u_val, u_gate, conv_w, conv_b, ln_g, ln_b, w_proj):
    a = u_val * jax.nn.sigmoid(u_gate)
    a = lax.conv_general_dilated(
        a, conv_w[:, None, :].astype(a.dtype), window_strides=(1,),
        padding=[(CONV_KERNEL - 1, 0)],
        dimension_numbers=('NWC', 'WIO', 'NWC'),
        feature_group_count=CONV_WIDTH_2) + conv_b
    a = jax.nn.silu(layer_norm(a, ln_g, ln_b))
    return a @ w_proj

def forgetting_attention(q, k, v, f_logit):
    B, S = q.shape[0], q.shape[1]
    n_blocks = S // Q_BLOCK
    log_f = jax.nn.log_sigmoid(f_logit.astype(jnp.float32))
    F = jnp.cumsum(log_f, axis=1).transpose(0, 2, 1)
    kh = k.transpose(0, 2, 1, 3)
    vh = v.transpose(0, 2, 1, 3)
    q_blocks = q.transpose(0, 2, 1, 3).reshape(B, N_HEADS, n_blocks, Q_BLOCK, HEAD_DIM_2).transpose(2, 0, 1, 3, 4)
    F_blocks = F.reshape(B, N_HEADS, n_blocks, Q_BLOCK).transpose(2, 0, 1, 3)
    k_pos = jnp.arange(S)
    scale = HEAD_DIM_2 ** -0.5

    def one_block(args):
        qi, Fi, bi = args
        q_pos = bi * Q_BLOCK + jnp.arange(Q_BLOCK)
        s = jnp.einsum('bhqd,bhkd->bhqk', qi, kh).astype(jnp.float32) * scale
        s = s + Fi[..., :, None] - F[:, :, None, :]
        s = jnp.where(k_pos[None, :] <= q_pos[:, None], s, -jnp.inf)
        p = jax.nn.softmax(s, axis=-1)
        return jnp.einsum('bhqk,bhkd->bhqd', p.astype(vh.dtype), vh)

    out = lax.map(one_block, (q_blocks, F_blocks, jnp.arange(n_blocks)))
    return out.transpose(1, 0, 3, 2, 4).reshape(B, S, ATTN_WIDTH_2)

def moe_ffn(h, w_router, b_router, w1, b1, w2, b2):
    B, S, D = h.shape
    T = B * S
    A = T * TOP_K
    hf = h.reshape(T, D)
    logits = (hf @ w_router + b_router).astype(jnp.float32)
    top_v, top_e = lax.top_k(logits, TOP_K)
    gates = jax.nn.softmax(top_v, axis=-1)

    flat_e = top_e.reshape(A).astype(jnp.int32)
    flat_tok = (jnp.arange(A, dtype=jnp.int32) // TOP_K)
    flat_gate = gates.reshape(A)
    order = jnp.argsort(flat_e)
    se, stok, sg = flat_e[order], flat_tok[order], flat_gate[order]
    counts = jnp.bincount(flat_e, length=N_EXPERTS)
    padded = (counts + MOE_BLOCK - 1) // MOE_BLOCK * MOE_BLOCK
    pend = jnp.cumsum(padded)
    pstart = pend - padded
    ustart = jnp.cumsum(counts) - counts
    dest = pstart[se] + jnp.arange(A, dtype=jnp.int32) - ustart[se]
    P = A + N_EXPERTS * MOE_BLOCK
    n_blocks = P // MOE_BLOCK
    tok_buf = jnp.zeros((P,), jnp.int32).at[dest].set(stok)
    gate_buf = jnp.zeros((P,), jnp.float32).at[dest].set(sg)
    block_e = jnp.clip(jnp.searchsorted(pend, jnp.arange(n_blocks) * MOE_BLOCK, side='right'), 0, N_EXPERTS - 1)
    xb = hf[tok_buf].reshape(n_blocks, MOE_BLOCK, D)

    def expert_block(args):
        xi, e = args
        hc = xi @ w1[e] + b1[e]
        g, u = hc[:, :D_EXPERT], hc[:, D_EXPERT:]
        g = jnp.minimum(g, SWIGLU_LIMIT)
        u = jnp.clip(u, -SWIGLU_LIMIT, SWIGLU_LIMIT)
        hm = (u + 1.0) * (g * jax.nn.sigmoid(SWIGLU_ALPHA * g))
        return hm @ w2[e] + b2[e]

    yb = lax.map(expert_block, (xb, block_e)).reshape(P, D)
    y = jax.ops.segment_sum(yb.astype(jnp.float32) * gate_buf[:, None], tok_buf, num_segments=T)
    return y.astype(h.dtype).reshape(B, S, D)

def second_inputs(seed: int = 0) -> dict:
    key = jax.random.key(seed)
    ks = jax.random.split(key, 24)
    f32 = jnp.float32
    L, D = DEPTH, D_MODEL

    def nrm(k, shape, fan_in, mult=1.0):
        return jax.random.normal(k, shape, f32) * (mult * fan_in ** -0.5)

    return {
        "x": jax.random.normal(ks[0], (BATCH, SEQ, D), f32),
        "c": jax.random.normal(ks[1], (BATCH, D), f32),
        "w_ada": nrm(ks[2], (L, D, N_MOD * D), D, 0.5),
        "b_ada": 0.02 * jax.random.normal(ks[3], (L, N_MOD * D), f32),
        "norm1_g": 1.0 + 0.05 * jax.random.normal(ks[4], (L, D), f32),
        "w_in": nrm(ks[5], (L, D, IN_COLS_2), D),
        "b_forget": jax.random.uniform(ks[6], (L, N_HEADS), f32, 1.0, 4.0),
        "conv_w": nrm(ks[7], (L, CONV_KERNEL, CONV_WIDTH_2), CONV_KERNEL),
        "conv_b": 0.02 * jax.random.normal(ks[8], (L, CONV_WIDTH_2), f32),
        "conv_ln_g": 1.0 + 0.05 * jax.random.normal(ks[9], (L, CONV_WIDTH_2), f32),
        "conv_ln_b": 0.02 * jax.random.normal(ks[10], (L, CONV_WIDTH_2), f32),
        "w_conv_out": nrm(ks[11], (L, CONV_WIDTH_2, D), CONV_WIDTH_2),
        "w_attn_out": nrm(ks[12], (L, ATTN_WIDTH_2, D), ATTN_WIDTH_2),
        "w_out": nrm(ks[13], (L, D, D), D),
        "norm2_g": 1.0 + 0.05 * jax.random.normal(ks[14], (L, D), f32),
        "w_router": nrm(ks[15], (L, D, N_EXPERTS), D),
        "b_router": 0.01 * jax.random.normal(ks[16], (L, N_EXPERTS), f32),
        "w_exp_in": nrm(ks[17], (L, N_EXPERTS, D, 2 * D_EXPERT), D),
        "b_exp_in": 0.02 * jax.random.normal(ks[18], (L, N_EXPERTS, 2 * D_EXPERT), f32),
        "w_exp_out": nrm(ks[19], (L, N_EXPERTS, D_EXPERT, D), D_EXPERT),
        "b_exp_out": 0.02 * jax.random.normal(ks[20], (L, N_EXPERTS, D), f32),
        "final_g": 1.0 + 0.05 * jax.random.normal(ks[21], (D,), f32),
    }

def second_block(x, c, w_ada, b_ada, norm1_g, w_in, b_forget, conv_w, conv_b, conv_ln_g, conv_ln_b,
              w_conv_out, w_attn_out, w_out, norm2_g, w_router, b_router, w_exp_in, b_exp_in,
              w_exp_out, b_exp_out, final_g):
    B, S, D = x.shape
    offs = np.cumsum(COL_SIZES)[:-1].tolist()
    for l in range(DEPTH):
        mod = (jax.nn.silu(c) @ w_ada[l] + b_ada[l]).reshape(B, N_MOD, D)
        sh1, sc1, g1, sh2, sc2, g2 = (mod[:, i, None, :] for i in range(N_MOD))

        h = rms_norm_2(x, norm1_g[l]) * (1.0 + sc1) + sh1
        z = h @ w_in[l]
        u_val, u_gate, q, k, v, f_logit, gate_c, gate_a = jnp.split(z, offs, axis=-1)
        conv_out = conv_module(u_val, u_gate, conv_w[l], conv_b[l], conv_ln_g[l], conv_ln_b[l], w_conv_out[l])
        attn = forgetting_attention(q.reshape(B, S, N_HEADS, HEAD_DIM_2),
                                    k.reshape(B, S, N_HEADS, HEAD_DIM_2),
                                    v.reshape(B, S, N_HEADS, HEAD_DIM_2),
                                    f_logit + b_forget[l])
        attn_out = attn @ w_attn_out[l]
        mixed = jax.nn.sigmoid(gate_c) * conv_out + jax.nn.sigmoid(gate_a) * attn_out
        x = x + g1 * (mixed @ w_out[l])

        h2 = rms_norm_2(x, norm2_g[l]) * (1.0 + sc2) + sh2
        x = x + g2 * moe_ffn(h2, w_router[l], b_router[l], w_exp_in[l], b_exp_in[l], w_exp_out[l], b_exp_out[l])
    return rms_norm_2(x, final_g)


def setup_inputs(seed=0):
    out = dict(first_inputs(seed))
    for name, value in second_inputs(seed + 1).items():
        if name != "x":
            out[name + "_2"] = value
    return out


def reference(
    x, norm1_g, w_in, b_gate, q_norm_g, k_norm_g, lambda_q1, lambda_k1, lambda_q2, lambda_k2,
    subln_g, conv_w, conv_b, w_rg_a, b_rg_a, w_rg_x, b_rg_x, rg_lambda, w_br_attn, w_br_rnn,
    w_out, norm2_g, w_peer_q, peer_sub_keys, peer_u, peer_v, c_2, w_ada_2, b_ada_2, norm1_g_2,
    w_in_2, b_forget_2, conv_w_2, conv_b_2, conv_ln_g_2, conv_ln_b_2, w_conv_out_2,
    w_attn_out_2, w_out_2, norm2_g_2, w_router_2, b_router_2, w_exp_in_2, b_exp_in_2,
    w_exp_out_2, b_exp_out_2, final_g_2,
):
    x = first_block(
        x, norm1_g, w_in, b_gate, q_norm_g, k_norm_g, lambda_q1, lambda_k1, lambda_q2,
        lambda_k2, subln_g, conv_w, conv_b, w_rg_a, b_rg_a, w_rg_x, b_rg_x, rg_lambda,
        w_br_attn, w_br_rnn, w_out, norm2_g, w_peer_q, peer_sub_keys, peer_u, peer_v,
    )
    return second_block(
        x, c_2, w_ada_2, b_ada_2, norm1_g_2, w_in_2, b_forget_2, conv_w_2, conv_b_2,
        conv_ln_g_2, conv_ln_b_2, w_conv_out_2, w_attn_out_2, w_out_2, norm2_g_2, w_router_2,
        b_router_2, w_exp_in_2, b_exp_in_2, w_exp_out_2, b_exp_out_2, final_g_2,
    )


_drawn_inputs = setup_inputs


def setup_inputs(seed=0):
    import zlib

    import numpy as np

    out = dict(_drawn_inputs(seed))
    spreads = {}
    factors = {'b_gate': 4.122,
     'q_norm_g': 2.845,
     'lambda_k2': 5.844,
     'b_rg_a': 7.416,
     'b_rg_x': 6.939,
     'b_ada_2': 2.706,
     'norm1_g_2': 7.014,
     'conv_b_2': 23.303,
     'conv_ln_g_2': 7.241,
     'conv_ln_b_2': 36.44,
     'b_router_2': 24.138,
     'b_exp_in_2': 27.671,
     'b_exp_out_2': 34.357,
     'norm2_g_2': 3.971}
    for name, (base, spread) in spreads.items():
        noise = np.random.default_rng([zlib.crc32(name.encode()), seed]).standard_normal(out[name].shape)
        drawn = base * np.exp(spread * noise) if base else spread * noise
        out[name] = jnp.asarray(drawn.astype(out[name].dtype))
    for name, factor in factors.items():
        out[name] = (out[name] * factor).astype(out[name].dtype)
    return out
```

```python
from contextlib import ExitStack

import numpy as np

import concourse.bass as bass
from concourse import mybir

F32 = mybir.dt.float32
U32 = mybir.dt.uint32
ALU = mybir.AluOpType
ACT = mybir.ActivationFunctionType
AX = mybir.AxisListType.X

P = 128
T = 256
TT = T // P
D = 1024
KD = D // P
EPS1 = 1e-6
EPS2 = 1e-5
NEG = -1e30
LAM_INIT = 0.2

HA, DH = 8, 64
DR = 1280
CR = DR // P
TAPS1 = 4
PH, PK, TOPK = 8, 128, 16
N_EXPERTS_PEER = PK * PK
HB = 8
CW = 512
KC = CW // P
TAPS2 = 31
E, FE = 32, 1024
LIMIT, ALPHA = 7.0, 1.702

SLOT = 4096
RING = 5
N_BANKS = 8

COLS = {}


def _column(name, n):
    start = sum(c for _, c in COLS.values())
    COLS[name] = (start, n)


for _name, _n in (("norm1_g", KD), ("b_gate", 2 * KD), ("q_norm_g", 1), ("k_norm_g", 1), ("subln_g", 1),
                  ("conv_w", CR * TAPS1), ("conv_b", CR), ("b_rg_a", CR), ("b_rg_x", CR), ("rg_lambda", CR),
                  ("norm2_g", KD), ("b_ada", 6 * KD), ("norm1_g_2", KD), ("conv_w_2", KC * TAPS2),
                  ("conv_b_2", KC), ("conv_ln_g", KC), ("conv_ln_b", KC), ("norm2_g_2", KD), ("b_forget", 1)):
    _column(_name, _n)
N_COLS = sum(c for _, c in COLS.values())



def plan_first():
    s = [("ss1",)]
    late = []
    projections = ([("xr", i) for i in range(CR // 2)] + [("yr", 0)] + [("q", i) for i in range(4)]
                   + [("k", i) for i in range(4)] + [("v", i) for i in range(4)])
    for n, p in enumerate(projections):
        s.append(p)
        for when, steps in [x for x in late if x[0] <= n]:
            s.extend(steps)
        late = [x for x in late if x[0] > n]
        if p[0] == "xr":
            late.append((n + 2, [("rg", 2 * p[1]), ("rg", 2 * p[1] + 1)]))
        if p[0] in "qk":
            late.append((n + 1, [("ss" + p[0], p[1])]))
    assert not late
    slots = [("yr", i) for i in range(1, 5)] + [("gate", i) for i in range(KD)]
    for n, p in enumerate(slots):
        s.append(p)
        if 3 <= n < HA + 3:
            s.append(("osum", n - 3))
        if 2 <= n < HA + 2:
            s.append(("o", n - 2))
        if 1 <= n < HA + 1:
            s.append(("dT", n - 1))
        if n < HA:
            s += [("s0", n), ("s1", n)]
    s += [("brr", i) for i in range(4)] + [("bra", i) for i in range(4)] + [("wo", i) for i in range(4)]
    s.append(("ss2",))
    s += [("h2r", i) for i in range(4)]
    s += [("pq", i) for i in range(8)]
    s += [("key", i) for i in range(8)]
    return s


def plan_second():
    s = [("x2T", i) for i in range(4)] + [("ss3",)]
    s += [("ug", i) for i in range(2)] + [("uv", i) for i in range(2)] + [("f",)]
    s += [("q", i) for i in range(2)] + [("k", i) for i in range(2)] + [("v", i) for i in range(2)]
    for n in range(KD):
        s.append(("gate", n))
        if n >= 2:
            s.append(("o", n - 2))
        if n >= 1:
            s.append(("dT", n - 1))
        s.append(("s", n))
    s += [("o", HB - 2), ("dT", HB - 1), ("mean",), ("o", HB - 1), ("var",)]
    s += [("bra", i) for i in range(4)] + [("brc", i) for i in range(4)] + [("wo", i) for i in range(4)]
    s.append(("ss4",))
    s += [("route", i) for i in range(TT)]
    s += [("x3r", i) for i in range(4)] + [("g2r", i) for i in range(2)]
    s += [("gT",)] + [("gbc", i) for i in range(E // 2)]
    return s


def plan_units():
    w = lambda i: ("w_in", i, SLOT)
    ada = lambda i: ("w_ada", i, SLOT)
    first = [w(6), w(7), w(8), ada(0), w(0), ada(1), w(1), ada(2), w(2), ada(3), w(3), ada(4), w(4), ada(5),
             w(5), ada(6), w(9), ada(7), w(10), ada(8), w(11), ada(9), w(12), ada(10), w(13), ada(11), w(14)]
    first += [("w_br_rnn", i, CR * 256) for i in range(4)] + [("w_br_attn", i, SLOT) for i in range(2)]
    first += [("w_out", i, SLOT) for i in range(2)] + [("w_peer_q", i, SLOT) for i in range(4)]
    first += [("sub_keys", 0, 2 * PH * PK)]
    second = [("w_in_2", i, SLOT) for i in (1, 0, 2, 3, 4, 5, 6, 7, 8)]
    second += [("w_attn_out_2", 0, SLOT), ("w_conv_out_2", 0, SLOT)] + [("w_out_2", i, SLOT) for i in range(2)]
    return first, second


class Jobs:

    def __init__(self, plan, full, free, before=None):
        self.number = {step: n for n, step in enumerate(plan)}
        self.full, self.free = full, free
        self.base = [before.base[b] + before.jobs(b) if before else 0 for b in range(N_BANKS)]

    def jobs(self, b):
        return sum(n % N_BANKS == b for n in self.number.values())

    def bank(self, *job):
        return self.number[job] % N_BANKS

    def claim(self, pe, *job):
        n = self.number[job]
        if n >= N_BANKS:
            pe.wait_ge(self.free[n % N_BANKS], self.base[n % N_BANKS] + n // N_BANKS)

    def filled(self, eng, *job):
        n = self.number[job]
        eng.wait_ge(self.full[n % N_BANKS], self.base[n % N_BANKS] + n // N_BANKS + 1)

    def all_free(self, eng):
        for b in range(N_BANKS):
            eng.wait_ge(self.free[b], self.base[b] + self.jobs(b))


class Own:

    def __init__(self, eng, sem):
        self.eng, self.sem, self.n, self.loop = eng, sem, 0, None

    def mark(self, ins):
        ins.then_inc(self.sem, 1)
        self.n += 1

    def settle(self):
        self.eng.wait_ge(self.sem, self.n if self.loop is None else self.loop + self.n)

    def __call__(self, ins):
        self.mark(ins)
        self.settle()

    def enter(self, i, per):
        self.start, self.per = self.n, per
        self.loop = i * per

    def leave(self, count):
        assert self.n - self.start == self.per, (self.n - self.start, self.per)
        self.n, self.loop = self.start + self.per * count, None


def build_program(nc, a, out):
    first_units, second_units = plan_units()
    units = first_units + second_units
    unit_at = {(name, i): n for n, (name, i, _) in enumerate(units)}
    n_first = len(first_units)

    with ExitStack() as ctx:
        def sem(name):
            return ctx.enter_context(nc.semaphore(name))

        ring = ctx.enter_context(nc.sbuf_tensor("ring", [P, 6 * SLOT], F32))
        arena_words = 27400
        arena = ctx.enter_context(nc.sbuf_tensor("arena", [P, arena_words], F32))
        ps = ctx.enter_context(nc.psum_tensor("ps", [P, N_BANKS, 512], F32))
        at = {"fixed": 0}

        def carve(region, *shape):
            n = int(np.prod(shape))
            start = at[region]
            at[region] = start + n
            assert at[region] <= arena_words, (region, at[region])
            v = arena[:, start:start + n]
            if len(shape) == 2:
                v = v.rearrange("p (a b) -> p a b", b=shape[1])
            if len(shape) == 3:
                v = v.rearrange("p (a b c) -> p a b c", b=shape[1], c=shape[2])
            return v

        ident = carve("fixed", P)
        ones = carve("fixed", P)
        cols = carve("fixed", N_COLS)
        eps = carve("fixed", 2)
        xT = carve("fixed", KD, T)
        hT = carve("fixed", KD, T)
        rstd = carve("fixed", T)
        mod = carve("fixed", 6 * KD)
        scale1, scale2 = carve("fixed", KD), carve("fixed", KD)
        iota_i, iota16 = carve("fixed", TOPK), carve("fixed", TOPK)

        def col(name, i=0, n=1):
            s = COLS[name][0] + i
            return cols[:, s:s + n]

        at["A"] = at["fixed"]
        qT = carve("A", KD, T)
        kT = carve("A", KD, T)
        v_rows = carve("A", TT, D)
        rnnT = carve("A", CR, T)
        w_gates = carve("A", 2, CR, P)
        c_row = carve("A", D)
        xr = [carve("A", 2, T + TAPS1 - 1) for _ in range(2)]
        xc = [carve("A", 2, T) for _ in range(3)]
        ri = carve("A", 2, 2, T)
        decay, e_w, poly, gelu_y = (carve("A", 2, T) for _ in range(4))
        blocks = carve("A", P)
        probs = [carve("A", 2, 3 * P) for _ in range(2)]
        dT = [carve("A", 3 * P) for _ in range(2)]
        sq = carve("A", 2, T)
        inv = carve("A", 2, T)
        osq = carve("A", T)
        oinv = carve("A", T)
        lams = carve("A", 4, DH)
        small = carve("A", 40)
        sp = carve("A", 6, CR)
        x_sq = rnnT
        gates = ring[:, 5 * SLOT:6 * SLOT].rearrange("p (a b) -> p a b", b=T)

        at["P"] = at["fixed"]
        h2_rows = carve("P", TT, D)
        qpT = carve("P", 2 * PH, T)
        scores = carve("P", TT, 2 * PH, PK)
        cand = carve("P", PH, TOPK * TOPK)
        hot = carve("P", PH * TOPK, TOPK)
        top = carve("P", 2 * PH, TOPK)
        top_i = carve("P", 2 * PH, TOPK)
        top_f = carve("P", 2 * PH, TOPK)
        top_s = carve("P", PH, TOPK)
        pos = carve("P", PH, TOPK)
        half_pos = carve("P", PH, TOPK)
        half_f = carve("P", PH, TOPK)
        i1_of, i2_of = carve("P", PH, TOPK), carve("P", PH, TOPK)
        soft = carve("P", 2 * PH)
        peer_idx = carve("P", TT, PH * TOPK)
        peer_g = carve("P", TT, PH * TOPK)
        idx_now = carve("P", 2, TOPK)
        dots = carve("P", 2, TOPK)
        wts = carve("P", 2, TOPK)
        x2_rows = h2_rows
        diag = qpT.rearrange("p (g k) t -> p g k t", g=2).rearrange("p g k t -> p g (k t)").rearrange(
            "p g (k t) -> p g k t", t=P)
        u_rows = [ring[:, i * D:(i + 1) * D] for i in range(8)]
        v_gath = [ring[:, (8 + i) * D:(9 + i) * D] for i in range(16)]

        at["B"] = at["fixed"] + TT * D
        qz = carve("B", HB, T)
        kv = carve("B", KD, T)
        kB = kv[:, 0:KC, :]
        vB = kv[:, KC:KD, :].rearrange("p (a b) t -> p a (b t)", a=TT)
        attnB = carve("B", KC, T)
        pad = carve("B", KC, T + TAPS2 - 1)
        conv = carve("B", KC, T)
        sigB = carve("B", KC, T)
        sqB = carve("B", KC, T)
        mixed = carve("B", KD, T)
        pB = [carve("B", 3 * P) for _ in range(2)]
        pTB = [carve("B", 3 * P) for _ in range(2)]
        cmask = carve("B", P)
        w_f, w_r = carve("B", KD, DH), carve("B", KD, E)
        fx = carve("B", 4, T)
        f_right = carve("B", T)
        f_left = carve("B", HB, T)
        smallB = carve("B", 24)
        meanB, invB = carve("B", T), carve("B", T)
        xsqB = kv
        b_route = carve("B", E)
        b1 = carve("B", E, 2 * KD)
        b2 = carve("B", D)

        at["M"] = at["fixed"]
        gate_bc = carve("M", E, T)
        hm = carve("M", KD, T)
        x3_rows = carve("M", TT, D)
        g2_row = carve("M", D)
        final_row = carve("M", D)
        g_act = [carve("M", T) for _ in range(2)]
        u_act = [carve("M", T) for _ in range(2)]
        sg_act = [carve("M", T) for _ in range(2)]
        logits = carve("M", E + 4)
        logits_r = carve("M", E + 4)
        m8 = carve("M", 8)
        chosen = carve("M", E)
        gate_rows = carve("M", TT, E)
        gT = carve("M", T)
        smallM = carve("M", 8)
        y_rows = gate_bc.rearrange("p e t -> p (e t)")[:, 0:TT * D].rearrange("p (a b) -> p a b", b=D)
        gdiag = ring[:, 0:E * T].rearrange("p (e t) -> p e t", t=T)
        g2_diag = ring[:, 2 * SLOT:2 * SLOT + KD * P].rearrange("p (c j) -> p c j", j=P)
        w1_unit = [ring[:, n * SLOT:(n + 1) * SLOT].rearrange("p (c s j) -> p c s j", c=KD, s=2) for n in range(4)]
        w2_unit = [ring[:, n * SLOT:(n + 1) * SLOT].rearrange("p (c j) -> p c j", j=D) for n in (4, 5)]

        s_par = sem("params_loaded")
        s_x = sem("x_loaded")
        s_wg = sem("gate_weights_loaded")
        s_const, s_iota = sem("constants_ready"), sem("iota_ready")
        full = [sem(f"bank_full_{b}") for b in range(N_BANKS)]
        free = [sem(f"bank_free_{b}") for b in range(N_BANKS)]
        r_full = [sem(f"unit_loaded_{b}") for b in range(RING)]
        r_free = [sem(f"unit_used_{b}") for b in range(RING)]
        s_v, s_a, s_p = sem("vector_own"), sem("scalar_own"), sem("pool_own")
        A = Jobs(plan_first(), full, free)
        B = Jobs(plan_second(), full, free, before=A)

        def unit(name, i):
            n = unit_at[(name, i)]
            s = n % RING
            return ring[:, s * SLOT:s * SLOT + units[n][2]]

        def unit_loaded(eng, name, i):
            n = unit_at[(name, i)]
            eng.wait_ge(r_full[n % RING], 16 * (n // RING + 1))

        def unit_used(name, i):
            return r_free[unit_at[(name, i)] % RING]

        s_sq = sem("squares_ready")
        s_root = sem("root_ready")
        s_h = sem("h_ready")
        s_xr = sem("xr_ready")
        s_xc = sem("xc_ready")
        s_ri = sem("rnn_gates_ready")
        s_rnn_free = sem("rnn_gates_used")
        s_dec = sem("decay_exponent_ready")
        s_expw = sem("decay_ready")
        s_poly = sem("mult_squared_ready")
        s_mult = sem("mult_ready")
        s_gel = sem("gelu_y_ready")
        s_gel_free = sem("rnn_pair_done")
        s_qsq = sem("qk_squares_ready")
        s_qroot = sem("qk_root_ready")
        s_qroot_free = sem("qk_ready")
        s_vr = sem("v_rows_ready")
        s_gate = sem("branch_gates_ready")
        s_nm = sem("negative_max_ready")
        s_exp = sem("exponentials_ready")
        s_diff = sem("probabilities_ready")
        s_dT = sem("transposed_probs_ready")
        s_osq = sem("head_squares_ready")
        s_oroot = sem("head_root_ready")
        s_o = sem("head_output_ready")
        s_mrg = sem("merged_ready")
        s_x1 = sem("residual_ready")
        s_silu = sem("silu_c_ready")
        s_sp = sem("lambda_exp_ready")
        s_spw = sem("lambda_in_ready")
        s_h2r = sem("h2_rows_ready")
        s_pq = sem("peer_queries_ready")
        s_ps = sem("peer_scores_ready")
        s_out = sem("output_stored")
        s_soft_in = sem("peer_top_ready")
        s_soft = sem("peer_exp_ready")
        s_route = sem("peer_routes_ready")
        s_idx = sem("peer_start")
        s_dot = sem("u_rows_used")
        s_dots = sem("dots_ready")
        s_act = sem("gelu_dots_ready")
        s_wts = sem("expert_weights_ready")
        s_diag = sem("diagonals_ready")
        s_pv = sem("v_rows_used")
        u_full = [sem(f"u_row_loaded_{k}") for k in range(8)]
        v_full = [sem(f"v_row_loaded_{k}") for k in range(16)]
        s_x2r = sem("x2_rows_ready")
        s_x2 = sem("x2_ready")
        s_smallw = sem("small_weights_loaded")
        s_poolB = sem("second_constants_ready")
        s_sqB, s_rootB = sem("squares_ready_2"), sem("root_ready_2")
        s_hB = sem("h_ready_2")
        s_sig = sem("glu_gate_ready")
        s_fe, s_fl, s_fm = sem("forget_exp_in"), sem("forget_log_ready"), sem("forget_matrices_ready")
        s_qkv = sem("qkv_ready")
        s_gateB = sem("branch_gates_ready_2")
        s_mxB, s_exB, s_prB = sem("negative_max_ready_2"), sem("exponentials_ready_2"), sem("probs_ready_2")
        s_pTB, s_oB = sem("transposed_probs_ready_2"), sem("head_output_ready_2")
        s_conv, s_cen, s_csq = sem("conv_ready"), sem("centred_ready"), sem("centred_squares_ready")
        s_croot, s_cn, s_silu2 = sem("conv_root_ready"), sem("conv_normed_ready"), sem("conv_silu_ready")
        s_mix, s_x3 = sem("mixed_ready"), sem("x3_ready")
        s_rmax, s_rexp, s_gr = sem("router_max_ready"), sem("router_exp_ready"), sem("gate_rows_ready")
        s_gd, s_gbc, s_x3r = sem("gate_diagonals_ready"), sem("gates_broadcast"), sem("x3_rows_ready")
        s_g2d = sem("g2_diagonals_ready")
        w_full = [sem(f"expert_unit_loaded_{n}") for n in range(6)]
        s_z = sem("expert_z_filled")
        z_free = [sem(f"expert_z_free_{n}") for n in range(4)]
        s_g, s_sg = sem("expert_gate_ready"), sem("expert_sigmoid_ready")
        s_hm = sem("expert_hidden_ready")
        s_hu = sem("expert_hidden_used")
        s_fin = sem("experts_done")
        s_y, s_yroot, s_yn = sem("y_ready"), sem("y_root_ready"), sem("y_normed")
        s_row = sem("rows_loaded")

        block = ctx.enter_context(nc.Block())

        @block.sync
        def _(sp):
            sp.dma_start(xT, a["xT"]).then_inc(s_x, 16)
            sp.dma_start(cols, a["cols"]).then_inc(s_par, 16)
            sp.dma_start(w_gates, a["w_rg"]).then_inc(s_wg, 16)
            for i, name in enumerate(("lambda_q1", "lambda_k1", "lambda_q2", "lambda_k2")):
                sp.dma_start(lams[:, i, :], a[name].partition_broadcast(P)).then_inc(s_par, 16)
            sp.dma_start(c_row, a["c_2"].partition_broadcast(P)).then_inc(s_par, 16)
            for n, (name, i, words) in enumerate(units[:n_first]):
                if n >= RING:
                    sp.wait_ge(r_free[n % RING], n // RING)
                sp.dma_start(unit(name, i), a[name][i]).then_inc(r_full[n % RING], 16)
            sp.wait_ge(s_dot, 8 + TT * PH * TOPK)
            sp.wait_ge(s_pv, 17 + TT * PH * TOPK)
            for name, dst in (("w_f", w_f), ("w_router", w_r), ("b_exp_in", b1)):
                sp.dma_start(dst, a[name]).then_inc(s_smallw, 16)
            sp.dma_start(b_route, a["b_router"].partition_broadcast(P)).then_inc(s_smallw, 16)
            sp.wait_ge(s_poolB, 1)
            sp.dma_start(b2[0:E, :], a["b_exp_out"]).then_inc(s_smallw, 16)
            for n in range(n_first, len(units)):
                name, i, words = units[n]
                if n >= n_first + RING:
                    sp.wait_ge(r_free[n % RING], n // RING)
                sp.dma_start(unit(name, i), a[name][i]).then_inc(r_full[n % RING], 16)
            sp.wait_ge(s_gbc, E // 2)
            sp.wait_ge(s_x3r, 6)
            order = (0, 1, 2, 4, 3, 5)
            for n in order:
                sp.dma_start(ring[:, n * SLOT:(n + 1) * SLOT], a["w_exp"][0, n]).then_inc(w_full[n], 16)
            sp.dma_start(final_row, a["final_g"].partition_broadcast(P)).then_inc(s_row, 16)
            with sp.Fori(1, E) as e:
                for n in order:
                    if n < 4:
                        sp.wait_ge(s_z, (e - 1) * KD + 2 * n + 2)
                    else:
                        sp.wait_ge(s_hu, (e - 1) * KD + 4 * (n - 4) + 5)
                    sp.dma_start(ring[:, n * SLOT:(n + 1) * SLOT],
                                 a["w_exp"][bass.ds(e, 1), n].rearrange("e p w -> (e p) w")).then_inc(w_full[n], 16)
            sp.wait_ge(s_yn, TT)
            sp.dma_start(out.rearrange("(a p) d -> p a d", p=P), y_rows).then_inc(s_out, 16)
            sp.wait_ge(s_out, 16)

        @block.gpsimd
        def _(pool):
            own = Own(pool, s_p)
            own.mark(pool.memset(ident, 0.0))
            own.mark(pool.memset(blocks, 0.0))
            own.mark(pool.memset(ones, 1.0))
            own.mark(pool.memset(eps[:, 0:1], EPS1))
            own.mark(pool.memset(eps[:, 1:2], EPS2))
            own.settle()
            own(pool.affine_select(out=ident, in_=ident, compare_op=ALU.not_equal, fill=1.0, base=0,
                                   pattern=[[-1, P]], channel_multiplier=1))
            own(pool.memset(blocks[0:DH, 0:DH], 1.0))
            own(pool.memset(blocks[DH:P, DH:P], 1.0))
            for i in range(2):
                own.mark(pool.memset(xr[i][:, :, 0:TAPS1 - 1], 0.0))
            own.settle()
            pool.sem_inc(s_const, 1)
            own(pool.iota(iota_i.bitcast(mybir.dt.int32), pattern=[[1, TOPK]], base=0, channel_multiplier=0))
            own(pool.tensor_copy(iota16, iota_i.bitcast(mybir.dt.int32)))
            pool.sem_inc(s_iota, 1)

            A.all_free(pool)
            for s in range(RING):
                pool.wait_ge(r_free[s], len([n for n in range(n_first) if n % RING == s]))
            pool.wait_ge(s_mrg, 4)
            for tile in range(TT):
                pool.wait_ge(s_route, tile + 1)
                per = 2 * (1 + 2 * TOPK)
                with pool.Fori(0, PH // 2) as i:
                    own.enter(i, per)
                    for par in range(2):
                        g = tile * PH + par
                        pool.wait_ge(s_pv, i * (2 * TOPK) + TOPK * g + 1)
                        own(pool.tensor_copy(idx_now[:, par, :].bitcast(U32),
                                             peer_idx[:, tile, bass.ds(i * (2 * TOPK) + par * TOPK, TOPK)]
                                             .bitcast(U32)))
                        for k in range(TOPK):
                            own.mark(pool.wait_ge(s_dot, i * (2 * TOPK) + TOPK * g + k + 1))
                            pool.indirect_dma_start(
                                out=u_rows[k % 8], out_offset=None, in_=a["peer_u"],
                                in_offset=bass.IndirectOffsetOnAxis(ap=idx_now[:, par, k:k + 1].bitcast(U32), axis=0)
                            ).then_inc(u_full[k % 8], 16)
                        for k in range(TOPK):
                            own.mark(pool.wait_ge(s_pv, i * (2 * TOPK) + TOPK * g + k + 2))
                            pool.indirect_dma_start(
                                out=v_gath[k], out_offset=None, in_=a["peer_v"],
                                in_offset=bass.IndirectOffsetOnAxis(ap=idx_now[:, par, k:k + 1].bitcast(U32), axis=0)
                            ).then_inc(v_full[k], 16)
                own.leave(PH // 2)

            pool.wait_ge(s_dot, 8 + TT * PH * TOPK)
            pool.wait_ge(s_pv, 17 + TT * PH * TOPK)
            for dst in (qz, f_left, pad[:, :, 0:TAPS2 - 1], b2, cmask):
                own.mark(pool.memset(dst, 0.0))
            own.mark(pool.memset(f_right, 1.0))
            own.settle()
            own(pool.affine_select(out=cmask, in_=cmask, compare_op=ALU.is_ge, fill=NEG, base=0,
                                   pattern=[[-1, P]], channel_multiplier=1))
            pool.sem_inc(s_poolB, 1)

        @block.tensor
        def _(pe):
            def mm(o, l, r, start, stop):
                return pe.matmul(o, l, r, start=start, stop=stop)

            def project(J, job, b, w, m, src, nk, half):
                for c in range(nk):
                    last = mm(ps[:, b, half * T:(half + 1) * T], w[:, c, m * P:(m + 1) * P], src[:, c, :],
                              c == 0, c == nk - 1)
                return last

            pe.wait_ge(s_const, 1)
            inc = None
            seen = {}
            for job in plan_first():
                kind, i = job[0], job[1] if len(job) > 1 else 0
                b = A.bank(*job)
                seen[kind] = seen.get(kind, 0) + 1
                if kind in ("xr", "yr", "q", "k", "gate"):
                    first = {"q": 0, "k": 8, "xr": 24, "yr": 34, "gate": 44}[kind] + 2 * i
                    u = first // 4
                    w = unit("w_in", u).rearrange("p (c n) -> p c n", c=KD)
                    unit_loaded(pe, "w_in", u)
                    if kind == "xr" and i == 0:
                        pe.wait_ge(s_h, KD)
                    A.claim(pe, *job)
                    project(A, job, b, w, first % 4, hT, KD, 0)
                    last = project(A, job, b, w, first % 4 + 1, hT, KD, 1)
                    last.then_inc(full[b], 1)
                    if first % 4 == 2:
                        pe.wait_ge(full[b], A.number[job] // N_BANKS + 1).then_inc(unit_used("w_in", u), 1)
                elif kind == "v":
                    u = 4 + i // 2
                    w = unit("w_in", u).rearrange("p (c n) -> p c n", c=KD)
                    unit_loaded(pe, "w_in", u)
                    A.claim(pe, *job)
                    for c in range(KD):
                        last = mm(ps[:, b, :], hT[:, c, (i % 2) * P:(i % 2 + 1) * P], w[:, c, :], c == 0, c == KD - 1)
                    last.then_inc(full[b], 1)
                    if i % 2 == 1:
                        pe.wait_ge(full[b], A.number[job] // N_BANKS + 1).then_inc(unit_used("w_in", u), 1)
                elif kind in ("ss1", "ss2"):
                    pe.wait_ge(s_sq, 1 if kind == "ss1" else 2)
                    A.claim(pe, *job)
                    for c in range(KD):
                        last = mm(ps[:, b, 0:T], ones, x_sq[:, c, :], c == 0, c == KD - 1)
                    last.then_inc(full[b], 1)
                elif kind == "rg":
                    if i % 2 == 0:
                        pe.wait_ge(s_xc, i // 2 + 1)
                    if i == 0:
                        pe.wait_ge(s_wg, 16)
                    A.claim(pe, *job)
                    for g in range(2):
                        last = mm(ps[:, b, g * T:(g + 1) * T], w_gates[:, g, i, :], xc[i // 2 % 3][:, i % 2, :],
                                  True, True)
                    last.then_inc(full[b], 1)
                elif kind in ("ssq", "ssk"):
                    n = i + (4 if kind == "ssk" else 0)
                    pe.wait_ge(s_qsq, n + 1)
                    A.claim(pe, *job)
                    mm(ps[:, b, :], blocks, sq.rearrange("p a b -> p (a b)"), True, True).then_inc(full[b], 1)
                elif kind in ("s0", "s1"):
                    if i == 0:
                        pe.wait_ge(s_qroot_free, 8)
                    A.claim(pe, *job)
                    h = slice(0, DH) if kind == "s0" else slice(DH, P)
                    mm(ps[:, b, 0:T], qT[h, i, P:T], kT[h, i, :], True, True)
                    mm(ps[:, b, T:3 * P], qT[h, i, 0:P], kT[h, i, 0:P], True, True).then_inc(full[b], 1)
                elif kind == "dT":
                    pe.wait_ge(s_diff, i + 1)
                    A.claim(pe, *job)
                    pe.transpose(ps[:, b, 0:P], probs[i % 2][:, 0, T:3 * P], ident)
                    pe.transpose(ps[:, b, P:2 * P], probs[i % 2][:, 0, 0:P], ident)
                    pe.transpose(ps[:, b, 2 * P:3 * P], probs[i % 2][:, 0, P:T], ident).then_inc(full[b], 1)
                elif kind == "o":
                    pe.wait_ge(s_dT, i + 1)
                    if i == 0:
                        pe.wait_ge(s_vr, 4)
                    A.claim(pe, *job)
                    mm(ps[:, b, 0:T], v_rows[:, 0, i * P:(i + 1) * P], dT[i % 2][:, 0:T], True, False)
                    mm(ps[:, b, P:T], v_rows[:, 1, i * P:(i + 1) * P], dT[i % 2][:, T:3 * P], False, True)\
                        .then_inc(full[b], 1)
                elif kind == "osum":
                    pe.wait_ge(s_osq, i + 1)
                    A.claim(pe, *job)
                    mm(ps[:, b, 0:T], ones, osq, True, True).then_inc(full[b], 1)
                elif kind == "brr":
                    if i == 0:
                        pe.wait_ge(s_gel_free, CR // 2)
                    unit_loaded(pe, "w_br_rnn", i)
                    w = unit("w_br_rnn", i).rearrange("p (c n) -> p c n", c=CR)
                    A.claim(pe, *job)
                    project(A, job, b, w, 0, rnnT, CR, 0)
                    project(A, job, b, w, 1, rnnT, CR, 1).then_inc(full[b], 1)
                    pe.wait_ge(full[b], A.number[job] // N_BANKS + 1).then_inc(unit_used("w_br_rnn", i), 1)
                elif kind in ("bra", "wo"):
                    name, src = ("w_br_attn", qT) if kind == "bra" else ("w_out", kT)
                    if i == 0:
                        if kind == "bra":
                            pe.wait_ge(s_o, HA)
                        else:
                            pe.wait_ge(s_mrg, 4)
                    unit_loaded(pe, name, i // 2)
                    w = unit(name, i // 2).rearrange("p (c n) -> p c n", c=KD)
                    A.claim(pe, *job)
                    project(A, job, b, w, 2 * (i % 2), src, KD, 0)
                    project(A, job, b, w, 2 * (i % 2) + 1, src, KD, 1).then_inc(full[b], 1)
                    if i % 2 == 1:
                        pe.wait_ge(full[b], A.number[job] // N_BANKS + 1).then_inc(unit_used(name, i // 2), 1)
                elif kind == "h2r":
                    if i == 0:
                        pe.wait_ge(s_h, 2 * KD)
                    A.claim(pe, *job)
                    for j in range(4):
                        last = pe.transpose(ps[:, b, j * P:(j + 1) * P],
                                            hT[:, 4 * (i % 2) + j, (i // 2) * P:(i // 2 + 1) * P], ident)
                    last.then_inc(full[b], 1)
                elif kind == "pq":
                    unit_loaded(pe, "w_peer_q", i // 2)
                    w = unit("w_peer_q", i // 2).rearrange("p (c n) -> p c n", c=KD)
                    A.claim(pe, *job)
                    project(A, job, b, w, 2 * (i % 2), hT, KD, 0)
                    project(A, job, b, w, 2 * (i % 2) + 1, hT, KD, 1).then_inc(full[b], 1)
                    if i % 2 == 1:
                        pe.wait_ge(full[b], A.number[job] // N_BANKS + 1).then_inc(unit_used("w_peer_q", i // 2), 1)
                elif kind == "key":
                    if i == 0:
                        unit_loaded(pe, "sub_keys", 0)
                        pe.wait_ge(s_pq, 8)
                    A.claim(pe, *job)
                    keys = unit("sub_keys", 0).rearrange("p (c n) -> p c n", n=PK)
                    for j in range(4):
                        hc = 4 * (i % 4) + j
                        last = mm(ps[:, b, j * PK:(j + 1) * PK], qpT[:, hc, (i // 4) * P:(i // 4 + 1) * P],
                                  keys[:, hc, :], True, True)
                    last.then_inc(full[b], 1)
                    if i == 7:
                        pe.wait_ge(full[b], A.number[job] // N_BANKS + 1).then_inc(unit_used("sub_keys", 0), 1)
                else:
                    raise ValueError(job)

            def add(o, l, r, start=False):
                return pe.matmul(o, l, r, start=start, stop=False, skip_group_check=True)

            A.all_free(pe)
            pe.sem_inc(s_pv, 17)
            for tile in range(TT):
                for c in range(KD):
                    add(ps[:, 2 * tile + c // 4, (c % 4) * P:(c % 4 + 1) * P], xT[:, c, tile * P:(tile + 1) * P],
                        ident, start=(c % 4 == 0))
                with pe.Fori(0, PH // 2) as i:
                    for par in range(2):
                        g = tile * PH + par
                        pe.wait_ge(s_diag, i * 2 + g + 1)
                        for k in range(TOPK):
                            pe.wait_ge(v_full[k], i * 32 + 16 * (g + 1))
                            add(ps[:, 2 * tile, :], diag[:, par, k, :], v_gath[k][:, 0:512])
                            add(ps[:, 2 * tile + 1, :], diag[:, par, k, :], v_gath[k][:, 512:D]).then_inc(s_pv, 1)

            for job in plan_second():
                kind, i = job[0], job[1] if len(job) > 1 else 0
                b = B.bank(*job)

                def release(name, u):
                    pe.wait_ge(full[b], B.base[b] + B.number[job] // N_BANKS + 1).then_inc(unit_used(name, u), 1)

                if kind == "x2T":
                    if i == 0:
                        pe.wait_ge(s_x2r, TT)
                    B.claim(pe, *job)
                    for j in range(2):
                        for t in range(TT):
                            last = pe.transpose(ps[:, b, j * T + t * P:j * T + (t + 1) * P],
                                                x2_rows[:, t, (2 * i + j) * P:(2 * i + j + 1) * P], ident)
                    last.then_inc(full[b], 1)
                elif kind in ("ss3", "ss4"):
                    pe.wait_ge(s_sqB, 1 if kind == "ss3" else 2)
                    B.claim(pe, *job)
                    for c in range(KD):
                        last = mm(ps[:, b, 0:T], ones, xsqB[:, c, :], c == 0, c == KD - 1)
                    last.then_inc(full[b], 1)
                elif kind in ("ug", "uv", "q", "k", "gate"):
                    u = {"ug": 1, "uv": 0, "q": 2, "k": 3, "gate": 5}[kind] + i // 2
                    w = unit("w_in_2", u).rearrange("p (c n) -> p c n", c=KD)
                    unit_loaded(pe, "w_in_2", u)
                    if kind == "ug" and i == 0:
                        pe.wait_ge(s_hB, 1)
                    B.claim(pe, *job)
                    project(B, job, b, w, 2 * (i % 2), hT, KD, 0)
                    project(B, job, b, w, 2 * (i % 2) + 1, hT, KD, 1).then_inc(full[b], 1)
                    if i % 2 == 1:
                        release("w_in_2", u)
                elif kind == "v":
                    w = unit("w_in_2", 4).rearrange("p (c n) -> p c n", c=KD)
                    unit_loaded(pe, "w_in_2", 4)
                    B.claim(pe, *job)
                    for c in range(KD):
                        last = mm(ps[:, b, :], hT[:, c, i * P:(i + 1) * P], w[:, c, :], c == 0, c == KD - 1)
                    last.then_inc(full[b], 1)
                    if i == 1:
                        release("w_in_2", 4)
                elif kind == "f":
                    pe.wait_ge(s_smallw, 16 * 5)
                    B.claim(pe, *job)
                    for c in range(KD):
                        last = mm(ps[0:DH, b, 0:T], w_f[:, c, :], hT[:, c, :], c == 0, c == KD - 1)
                    last.then_inc(full[b], 1)
                elif kind == "s":
                    if i == 0:
                        pe.wait_ge(s_qkv, 6)
                        pe.wait_ge(s_fm, 1)
                    B.claim(pe, *job)
                    mm(ps[:, b, 0:T], qz[:, i, P:T], kB[:, i // 2, :], True, False)
                    mm(ps[:, b, 0:T], f_left[:, i, P:T], f_right, False, True)
                    mm(ps[:, b, T:3 * P], qz[:, i, 0:P], kB[:, i // 2, 0:P], True, False)
                    mm(ps[:, b, T:3 * P], f_left[:, i, 0:P], f_right[:, 0:P], False, True).then_inc(full[b], 1)
                elif kind == "dT":
                    pe.wait_ge(s_prB, i + 1)
                    B.claim(pe, *job)
                    pe.transpose(ps[:, b, 0:P], pB[i % 2][:, T:3 * P], ident)
                    pe.transpose(ps[:, b, P:2 * P], pB[i % 2][:, 0:P], ident)
                    pe.transpose(ps[:, b, 2 * P:3 * P], pB[i % 2][:, P:T], ident).then_inc(full[b], 1)
                elif kind == "o":
                    pe.wait_ge(s_pTB, i + 1)
                    B.claim(pe, *job)
                    c = slice(i // 2 * P, (i // 2 + 1) * P)
                    mm(ps[:, b, 0:T], vB[:, 0, c], pTB[i % 2][:, 0:T], True, False)
                    mm(ps[:, b, P:T], vB[:, 1, c], pTB[i % 2][:, T:3 * P], False, True).then_inc(full[b], 1)
                elif kind in ("mean", "var"):
                    if kind == "mean":
                        pe.wait_ge(s_conv, 1)
                    else:
                        pe.wait_ge(s_csq, 1)
                    B.claim(pe, *job)
                    for c in range(KC):
                        last = mm(ps[:, b, 0:T], ones, (conv if kind == "mean" else sqB)[:, c, :], c == 0, c == KC - 1)
                    last.then_inc(full[b], 1)
                elif kind in ("bra", "brc"):
                    name, src = ("w_attn_out_2", attnB) if kind == "bra" else ("w_conv_out_2", conv)
                    unit_loaded(pe, name, 0)
                    if i == 0:
                        if kind == "bra":
                            pe.wait_ge(s_oB, HB)
                        else:
                            pe.wait_ge(s_silu2, 1)
                    w = unit(name, 0).rearrange("p (c n) -> p c n", c=KC)
                    B.claim(pe, *job)
                    project(B, job, b, w, 2 * i, src, KC, 0)
                    project(B, job, b, w, 2 * i + 1, src, KC, 1).then_inc(full[b], 1)
                    if i == 3:
                        release(name, 0)
                elif kind == "wo":
                    if i == 0:
                        pe.wait_ge(s_mix, 4)
                    unit_loaded(pe, "w_out_2", i // 2)
                    w = unit("w_out_2", i // 2).rearrange("p (c n) -> p c n", c=KD)
                    B.claim(pe, *job)
                    project(B, job, b, w, 2 * (i % 2), mixed, KD, 0)
                    project(B, job, b, w, 2 * (i % 2) + 1, mixed, KD, 1).then_inc(full[b], 1)
                    if i % 2 == 1:
                        release("w_out_2", i // 2)
                elif kind == "route":
                    if i == 0:
                        pe.wait_ge(s_hB, 2)
                    B.claim(pe, *job)
                    for c in range(KD):
                        last = mm(ps[:, b, 0:E], hT[:, c, i * P:(i + 1) * P], w_r[:, c, :], c == 0, c == KD - 1)
                    last.then_inc(full[b], 1)
                elif kind == "gT":
                    pe.wait_ge(s_gr, TT)
                    B.claim(pe, *job)
                    for t in range(TT):
                        last = pe.transpose(ps[0:E, b, t * P:(t + 1) * P], gate_rows[:, t, :], ident)
                    last.then_inc(full[b], 1)
                elif kind == "gbc":
                    if i == 0:
                        pe.wait_ge(s_gd, 1)
                    B.claim(pe, *job)
                    mm(ps[:, b, :], ones[0:E, :], gdiag[0:E, 2 * i:2 * i + 2, :].rearrange("p e t -> p (e t)"),
                       True, True).then_inc(full[b], 1)
                elif kind == "x3r":
                    B.claim(pe, *job)
                    for j in range(4):
                        last = pe.transpose(ps[:, b, j * P:(j + 1) * P],
                                            xT[:, 4 * (i % 2) + j, (i // 2) * P:(i // 2 + 1) * P], ident)
                    last.then_inc(full[b], 1)
                elif kind == "g2r":
                    if i == 0:
                        pe.wait_ge(s_g2d, 1)
                    B.claim(pe, *job)
                    mm(ps[:, b, :], ones, g2_diag[:, 4 * i:4 * i + 4, :].rearrange("p c j -> p (c j)"),
                       True, True).then_inc(full[b], 1)
                else:
                    raise ValueError(job)

            B.all_free(pe)
            pe.sem_inc(s_hu, 1)
            for t in range(TT):
                for half in range(2):
                    add(ps[:, 2 * t + half, :], gT[:, t * P:(t + 1) * P], b2[:, half * 512:(half + 1) * 512],
                        start=True)
            with pe.Fori(0, E) as e:
                def hidden(m):
                    if m % 2 == 0:
                        pe.wait_ge(w_full[m // 2], e * 16 + 16)
                    pe.wait_ge(z_free[m % 4], e * 2 + m // 4 + 1)
                    for s in range(2):
                        for c in range(KD):
                            last = mm(ps[:, 4 + m % 4, s * T:(s + 1) * T],
                                      w1_unit[m // 2][:, c, s, (m % 2) * P:(m % 2 + 1) * P], hT[:, c, :],
                                      c == 0, c == KD - 1)
                    last.then_inc(s_z, 1)

                def down(k):
                    if k % 4 == 0:
                        pe.wait_ge(w_full[4 + k // 4], e * 16 + 16)
                    pe.wait_ge(s_hm, e * KD + k + 1)
                    for t in range(TT):
                        for half in range(2):
                            last = add(ps[:, 2 * t + half, :], hm[:, k, t * P:(t + 1) * P],
                                       w2_unit[k // 4][:, k % 4, half * 512:(half + 1) * 512])
                    last.then_inc(s_hu, 1)

                for m in range(6):
                    hidden(m)
                for k in range(4):
                    down(k)
                hidden(6)
                hidden(7)
                for k in range(4, 8):
                    down(k)

        @block.scalar
        def _(act):
            own = Own(act, s_a)
            fn = act.activation
            act.wait_ge(s_x, 16)
            fn(x_sq[:, 0:KD, :], xT, ACT.Square).then_inc(s_sq, 1)
            act.wait_ge(s_const, 1)
            act.wait_ge(s_par, 16 * 6)
            fn(c_row, c_row, ACT.Silu).then_inc(s_silu, 1)
            act.wait_ge(s_spw, 1)
            fn(sp[:, 1, :], sp[:, 0, :], ACT.Exp)
            fn(small[:, 2:4], small[:, 0:2], ACT.Exp).then_inc(s_sp, 1)
            qn = 0
            for job in plan_first():
                kind, i = job[0], job[1] if len(job) > 1 else 0
                b = A.bank(*job)
                bank = ps[:, b, :]
                pair = bank.rearrange("p (a b) -> p a b", b=T)
                if kind in ("ss1", "ss2"):
                    A.filled(act, *job)
                    own(fn(rstd, ps[:, b, 0:T], ACT.Sqrt, bias=eps[:, 0:1], scale=1.0 / D))
                    act.sem_inc(free[b], 1)
                    act.sem_inc(s_root, 1)
                elif kind == "xr":
                    A.filled(act, *job)
                    if i >= 2:
                        act.wait_ge(s_xc, i - 1)
                    own(act.copy(xr[i % 2][:, :, TAPS1 - 1:], pair))
                    act.sem_inc(free[b], 1)
                    act.sem_inc(s_xr, 1)
                elif kind == "rg":
                    A.filled(act, *job)
                    if i % 2 == 0 and i >= 2:
                        act.wait_ge(s_rnn_free, i // 2)
                    own.mark(fn(ri[:, 0, i % 2, :], ps[:, b, 0:T], ACT.Sigmoid, bias=col("b_rg_a", i)))
                    own(fn(ri[:, 1, i % 2, :], ps[:, b, T:2 * T], ACT.Sigmoid, bias=col("b_rg_x", i)))
                    act.sem_inc(free[b], 1)
                    if i % 2 == 1:
                        act.sem_inc(s_ri, 1)
                        act.wait_ge(s_dec, i // 2 + 1)
                        fn(e_w, decay, ACT.Exp, scale=-0.5).then_inc(s_expw, 1)
                        act.wait_ge(s_poly, i // 2 + 1)
                        fn(poly, poly, ACT.Sqrt).then_inc(s_mult, 1)
                elif kind == "yr":
                    A.filled(act, *job)
                    if i >= 1:
                        act.wait_ge(s_gel_free, i)
                    own(fn(gelu_y, pair, ACT.Gelu_apprx_tanh))
                    act.sem_inc(free[b], 1)
                    act.sem_inc(s_gel, 1)
                elif kind in ("q", "k"):
                    A.filled(act, *job)
                    n = i + (4 if kind == "k" else 0)
                    if n >= 1:
                        A.filled(act, "ssq" if n - 1 < 4 else "ssk", (n - 1) % 4)
                    fn(sq, pair, ACT.Square).then_inc(s_qsq, 1)
                elif kind in ("ssq", "ssk"):
                    A.filled(act, *job)
                    n = i + (4 if kind == "ssk" else 0)
                    if n >= 1:
                        act.wait_ge(s_qroot_free, n)
                    own(fn(inv, pair, ACT.Sqrt, bias=eps[:, 0:1], scale=1.0 / DH))
                    act.sem_inc(free[b], 1)
                    act.sem_inc(s_qroot, 1)
                elif kind == "v":
                    A.filled(act, *job)
                    own(act.copy(v_rows[:, i % 2, (i // 2) * 512:(i // 2 + 1) * 512], bank))
                    act.sem_inc(free[b], 1)
                    act.sem_inc(s_vr, 1)
                elif kind == "gate":
                    A.filled(act, *job)
                    own.mark(fn(gates[:, 2 * i, :], ps[:, b, 0:T], ACT.Sigmoid, bias=col("b_gate", 2 * i)))
                    own(fn(gates[:, 2 * i + 1, :], ps[:, b, T:2 * T], ACT.Sigmoid, bias=col("b_gate", 2 * i + 1)))
                    act.sem_inc(free[b], 1)
                    act.sem_inc(s_gate, 1)
                elif kind == "s1":
                    act.wait_ge(s_nm, i + 1)
                    if i >= 2:
                        A.filled(act, "dT", i - 2)
                    nm = small[:, 8 + 8 * (i % 2):12 + 8 * (i % 2)]
                    z = small[:, 12 + 8 * (i % 2):16 + 8 * (i % 2)]
                    b0 = A.bank("s0", i)
                    for c, bc in ((0, b0), (1, b)):
                        for t, keys in ((0, slice(0, T)), (1, slice(T, 3 * P))):
                            own.mark(fn(probs[i % 2][:, c, keys], ps[:, bc, keys], ACT.Exp,
                                        bias=nm[:, 2 * t + c:2 * t + c + 1], scale=DH ** -0.5,
                                        accum_out=z[:, 2 * t + c:2 * t + c + 1]))
                    own.settle()
                    act.sem_inc(free[b], 1)
                    act.sem_inc(free[b0], 1)
                    act.sem_inc(s_exp, 1)
                elif kind == "o":
                    A.filled(act, *job)
                    if i >= 1:
                        A.filled(act, "osum", i - 1)
                    fn(osq, ps[:, b, 0:T], ACT.Square).then_inc(s_osq, 1)
                elif kind == "osum":
                    A.filled(act, *job)
                    if i >= 1:
                        act.wait_ge(s_o, i)
                    own(fn(oinv, ps[:, b, 0:T], ACT.Sqrt, bias=eps[:, 0:1], scale=1.0 / P))
                    act.sem_inc(free[b], 1)
                    act.sem_inc(s_oroot, 1)
                elif kind == "wo":
                    if i == 3:
                        act.wait_ge(s_x1, 4)
                        fn(x_sq[:, 0:KD, :], xT, ACT.Square).then_inc(s_sq, 1)
                elif kind == "h2r":
                    A.filled(act, *job)
                    own(act.copy(h2_rows[:, i // 2, (i % 2) * 512:(i % 2 + 1) * 512], bank))
                    act.sem_inc(free[b], 1)
                    act.sem_inc(s_h2r, 1)
                elif kind == "pq":
                    A.filled(act, *job)
                    own(act.copy(qpT[:, 2 * i:2 * i + 2, :], pair))
                    act.sem_inc(free[b], 1)
                    act.sem_inc(s_pq, 1)
                elif kind == "key":
                    A.filled(act, *job)
                    own(act.copy(scores[:, i // 4, 4 * (i % 4):4 * (i % 4) + 4, :],
                                 bank.rearrange("p (a b) -> p a b", b=PK)))
                    act.sem_inc(free[b], 1)
                    act.sem_inc(s_ps, 1)
            for tile in range(TT):
                act.wait_ge(s_soft_in, tile + 1)
                fn(top_s, top_s, ACT.Exp).then_inc(s_soft, 1)
            for tile in range(TT):
                with act.Fori(0, PH // 2) as i:
                    for par in range(2):
                        g = tile * PH + par
                        act.wait_ge(s_dots, i * 2 + g + 1)
                        fn(dots[:, par, :], dots[:, par, :], ACT.Gelu_apprx_tanh).then_inc(s_act, 1)
                        act.wait_ge(s_wts, i * 2 + g + 1)
                        act.wait_ge(s_pv, i * (2 * TOPK) + TOPK * g + 1)
                        for k in range(TOPK):
                            last = fn(diag[:, par, k, :], ident, ACT.Copy, scale=wts[:, par, k:k + 1])
                        last.then_inc(s_diag, 1)
                act.wait_ge(s_pv, 17 + (tile + 1) * PH * TOPK)
                for half in range(2):
                    last = act.copy(x2_rows[:, tile, half * 512:(half + 1) * 512], ps[:, 2 * tile + half, :])
                last.then_inc(s_x2r, 1)

            for job in plan_second():
                kind, i = job[0], job[1] if len(job) > 1 else 0
                b = B.bank(*job)
                bank = ps[:, b, :]
                pair = bank.rearrange("p (a b) -> p a b", b=T)
                if kind == "x2T":
                    B.filled(act, *job)
                    own(act.copy(xT[:, 2 * i:2 * i + 2, :], pair))
                    act.sem_inc(free[b], 1)
                    act.sem_inc(s_x2, 1)
                    if i == 3:
                        fn(xsqB, xT, ACT.Square).then_inc(s_sqB, 1)
                elif kind in ("ss3", "ss4"):
                    B.filled(act, *job)
                    own(fn(rstd, ps[:, b, 0:T], ACT.Sqrt, bias=eps[:, 1:2], scale=1.0 / D))
                    act.sem_inc(free[b], 1)
                    act.sem_inc(s_rootB, 1)
                elif kind == "ug":
                    B.filled(act, *job)
                    own(fn(sigB[:, 2 * i:2 * i + 2, :], pair, ACT.Sigmoid))
                    act.sem_inc(free[b], 1)
                    act.sem_inc(s_sig, 1)
                elif kind == "f":
                    act.wait_ge(s_fe, 1)
                    own(fn(fx[0:DH, 2, :], fx[0:DH, 1, :], ACT.Exp))
                    own(fn(fx[0:DH, 2, :], fx[0:DH, 2, :], ACT.Ln, bias=1.0))
                    act.sem_inc(s_fl, 1)
                elif kind == "q":
                    B.filled(act, *job)
                    if i == 0:
                        act.wait_ge(s_poolB, 1)
                    z4 = qz.rearrange("p (c s) t -> p c s t", s=2)
                    own.mark(act.copy(z4[0:DH, 2 * i:2 * i + 2, 0, :], pair[0:DH]))
                    own(act.copy(z4[DH:P, 2 * i:2 * i + 2, 1, :], pair[DH:P]))
                    act.sem_inc(free[b], 1)
                    act.sem_inc(s_qkv, 1)
                elif kind == "k":
                    B.filled(act, *job)
                    own(act.copy(kB[:, 2 * i:2 * i + 2, :], pair))
                    act.sem_inc(free[b], 1)
                    act.sem_inc(s_qkv, 1)
                elif kind == "v":
                    B.filled(act, *job)
                    own(act.copy(vB[:, i, :], bank))
                    act.sem_inc(free[b], 1)
                    act.sem_inc(s_qkv, 1)
                elif kind == "gate":
                    B.filled(act, *job)
                    own(fn(gates[:, 2 * i:2 * i + 2, :], pair, ACT.Sigmoid))
                    act.sem_inc(free[b], 1)
                    act.sem_inc(s_gateB, 1)
                elif kind == "s":
                    act.wait_ge(s_mxB, i + 1)
                    if i >= 2:
                        B.filled(act, "dT", i - 2)
                    nm = smallB[:, 2 * (i % 2):2 * (i % 2) + 2]
                    z = smallB[:, 4 + 2 * (i % 2):6 + 2 * (i % 2)]
                    for t, keys in ((0, slice(0, T)), (1, slice(T, 3 * P))):
                        own.mark(fn(pB[i % 2][:, keys], ps[:, b, keys], ACT.Exp, bias=nm[:, t:t + 1],
                                    scale=DH ** -0.5, accum_out=z[:, t:t + 1]))
                    own.settle()
                    act.sem_inc(free[b], 1)
                    act.sem_inc(s_exB, 1)
                elif kind == "o":
                    B.filled(act, *job)
                    h = slice(0, DH) if i % 2 == 0 else slice(DH, P)
                    own(act.copy(attnB[h, i // 2, :], ps[h, b, 0:T]))
                    act.sem_inc(free[b], 1)
                    act.sem_inc(s_oB, 1)
                elif kind == "mean":
                    act.wait_ge(s_cen, 1)
                    fn(sqB, conv, ACT.Square).then_inc(s_csq, 1)
                elif kind == "var":
                    B.filled(act, *job)
                    own(fn(invB, ps[:, b, 0:T], ACT.Sqrt, bias=eps[:, 1:2], scale=1.0 / CW))
                    act.sem_inc(free[b], 1)
                    act.sem_inc(s_croot, 1)
                    act.wait_ge(s_cn, 1)
                    for c in range(KC):
                        last = fn(conv[:, c, :], conv[:, c, :], ACT.Silu, bias=col("conv_ln_b", c),
                                  scale=col("conv_ln_g", c))
                    last.then_inc(s_silu2, 1)
                elif kind == "wo" and i == 3:
                    act.wait_ge(s_x3, 4)
                    fn(xsqB, xT, ACT.Square).then_inc(s_sqB, 1)
                elif kind == "route":
                    act.wait_ge(s_rmax, i + 1)
                    fn(chosen, logits[:, 0:E], ACT.Exp, bias=smallM[:, 0:1]).then_inc(s_rexp, 1)
                elif kind == "gbc":
                    B.filled(act, *job)
                    own(act.copy(gate_bc[:, 2 * i:2 * i + 2, :], pair))
                    act.sem_inc(free[b], 1)
                    act.sem_inc(s_gbc, 1)
                elif kind == "x3r":
                    B.filled(act, *job)
                    own(act.copy(x3_rows[:, i // 2, (i % 2) * 512:(i % 2 + 1) * 512], bank))
                    act.sem_inc(free[b], 1)
                    act.sem_inc(s_x3r, 1)
                elif kind == "g2r":
                    B.filled(act, *job)
                    own(act.copy(g2_row[:, i * 512:(i + 1) * 512], bank))
                    act.sem_inc(free[b], 1)
                    act.sem_inc(s_x3r, 1)

            with act.Fori(0, E) as e:
                for m in range(KD):
                    act.wait_ge(s_g, e * KD + m + 1)
                    fn(sg_act[m % 2], g_act[m % 2], ACT.Sigmoid, scale=ALPHA).then_inc(s_sg, 1)
            act.wait_ge(s_y, 1)
            fn(smallM[:, 2:4], smallM[:, 2:4], ACT.Sqrt, bias=eps[:, 1:2], scale=1.0 / D).then_inc(s_yroot, 1)

        @block.vector
        def _(dve):
            own = Own(dve, s_v)
            ts, tt, stt = dve.tensor_scalar, dve.tensor_tensor, dve.scalar_tensor_tensor

            dve.wait_ge(s_par, 16 * 6)
            dve.wait_ge(s_const, 1)
            for i in range(2):
                own.mark(dve.tensor_tensor_reduce(lams[:, 2 * i, :], lams[:, 2 * i, :], lams[:, 2 * i + 1, :], 1.0,
                                                  0.0, ALU.mult, ALU.add, small[:, i:i + 1]))
            lam_r = col("rg_lambda", 0, CR)
            own(ts(sp[:, 2, :], lam_r, -1.0, None, ALU.mult))
            own(tt(sp[:, 0, :], sp[:, 2, :], lam_r, ALU.min))
            dve.sem_inc(s_spw, 1)
            dve.wait_ge(s_sp, 1)
            own(tt(small[:, 4:5], small[:, 2:3], small[:, 3:4], ALU.subtract))
            own(ts(small[:, 4:5], small[:, 4:5], LAM_INIT, None, ALU.add))
            lam = small[:, 4:5]
            own(ts(small[:, 5:6], col("subln_g"), 1.0 - LAM_INIT, None, ALU.mult))
            sub_g = small[:, 5:6]
            y, s_, s2, acc = sp[:, 1, :], sp[:, 3, :], sp[:, 4, :], sp[:, 5, :]
            own(ts(s_, y, 2.0, None, ALU.add))
            own(dve.reciprocal(s_, s_))
            own(tt(s_, s_, y, ALU.mult))
            own(tt(s2, s_, s_, ALU.mult))
            own(ts(acc, s2, 1.0 / 17, 1.0 / 15, ALU.mult, ALU.add))
            for k in (13, 11, 9, 7, 5, 3, 1):
                own(tt(acc, acc, s2, ALU.mult))
                own(ts(acc, acc, 1.0 / k, None, ALU.add))
            own(tt(acc, acc, s_, ALU.mult))
            own(ts(sp[:, 2, :], sp[:, 2, :], 0.0, None, ALU.max))
            own(stt(acc, acc, 2.0, sp[:, 2, :], ALU.mult, ALU.add))
            own(ts(acc, acc, 16.0, None, ALU.mult))
            decay_rate = acc

            def ada(n):
                unit_loaded(dve, "w_ada", n)
                w = unit("w_ada", n).rearrange("p (c n) -> p c n", n=D)
                if n == 0:
                    dve.wait_ge(s_silu, 1)
                for j in range(4):
                    m = 4 * n + j
                    own.mark(dve.tensor_tensor_reduce(w[:, j, :], w[:, j, :], c_row, 1.0, 0.0, ALU.mult, ALU.add,
                                                      mod[:, m:m + 1]))
                own.settle()
                dve.sem_inc(unit_used("w_ada", n), 1)

            def norm_h(coef):
                own(dve.reciprocal(rstd, rstd))
                for c in range(KD):
                    stt(hT[:, c, :], xT[:, c, :], coef(c), rstd, ALU.mult, ALU.mult).then_inc(s_h, 1)

            ada_at = {("q", 0): 0, ("q", 2): 1, ("k", 0): 2, ("k", 2): 3, ("v", 0): 4, ("v", 2): 5,
                      ("yr", 1): 6, ("yr", 3): 7, ("gate", 0): 8, ("gate", 2): 9, ("gate", 4): 10, ("gate", 6): 11}
            for job in plan_first():
                kind, i = job[0], job[1] if len(job) > 1 else 0
                b = A.bank(*job)
                bank = ps[:, b, :]
                pair = bank.rearrange("p (a b) -> p a b", b=T)
                if job in ada_at:
                    ada(ada_at[job])
                if kind == "ss1":
                    dve.wait_ge(s_x, 16)
                    dve.wait_ge(s_root, 1)
                    norm_h(lambda c: col("norm1_g", c))
                elif kind == "ss2":
                    dve.wait_ge(s_root, 2)
                    dve.wait_ge(full[A.bank("gate", 7)], A.number[("gate", 7)] // N_BANKS + 1)
                    norm_h(lambda c: col("norm2_g", c))
                elif kind == "xr":
                    dve.wait_ge(s_xr, i + 1)
                    if i >= 3:
                        A.filled(dve, "rg", 2 * (i - 3) + 1)
                    for tap in range(TAPS1):
                        for j in range(2):
                            c = 2 * i + j
                            src = xr[i % 2][:, j, tap:tap + T]
                            w = col("conv_w", c * TAPS1 + tap)
                            if tap == 0:
                                own.mark(ts(xc[i % 3][:, j, :], src, w, col("conv_b", c), ALU.mult, ALU.add))
                            else:
                                own.mark(stt(xc[i % 3][:, j, :], src, w, xc[i % 3][:, j, :], ALU.mult, ALU.add))
                        own.settle()
                    dve.sem_inc(s_xc, 1)
                elif kind == "rg" and i % 2 == 1:
                    n = i // 2
                    dve.wait_ge(s_ri, n + 1)
                    for j in range(2):
                        own.mark(ts(decay[:, j, :], ri[:, 0, j, :], decay_rate[:, 2 * n + j:2 * n + j + 1], None,
                                    ALU.mult))
                    own.settle()
                    dve.sem_inc(s_dec, 1)
                    coef = [1.0, -1.0 / 2, 1.0 / 6, -1.0 / 24, 1.0 / 120, -1.0 / 720]
                    own(ts(poly, decay, coef[5], None, ALU.mult))
                    for k in (4, 3, 2, 1, 0):
                        own(stt(poly, poly, coef[k], decay, ALU.add, ALU.mult))
                    own(tt(ri[:, 1], ri[:, 1], xc[n % 3], ALU.mult))
                    mask = ri[:, 0].bitcast(U32)
                    own(ts(mask, decay, 0.25, None, ALU.is_gt))
                    dve.wait_ge(s_expw, n + 1)
                    own(tt(decay, e_w, e_w, ALU.mult))
                    own(ts(decay, decay, -1.0, 1.0, ALU.mult, ALU.add))
                    own(dve.copy_predicated(poly, mask, decay))
                    own(ts(poly, poly, 1e-34, None, ALU.max))
                    dve.sem_inc(s_poly, 1)
                    dve.wait_ge(s_mult, n + 1)
                    own(tt(decay, poly, ri[:, 1], ALU.mult))
                    dve.sem_inc(s_rnn_free, 1)
                    for j in range(2):
                        own.mark(dve.tensor_tensor_scan(rnnT[:, 2 * n + j, :], e_w[:, j, :], decay[:, j, :], 0.0,
                                                        ALU.mult, ALU.add))
                    own.settle()
                elif kind == "yr":
                    dve.wait_ge(s_gel, i + 1)
                    own(tt(rnnT[:, 2 * i:2 * i + 2, :], rnnT[:, 2 * i:2 * i + 2, :], gelu_y, ALU.mult))
                    dve.sem_inc(s_gel_free, 1)
                elif kind in ("ssq", "ssk"):
                    n = i + (4 if kind == "ssk" else 0)
                    dst = (qT if kind == "ssq" else kT)[:, 2 * i:2 * i + 2, :]
                    bz = A.bank(kind[2], i)
                    dve.wait_ge(s_qroot, n + 1)
                    own(dve.reciprocal(inv, inv))
                    own(stt(dst, ps[:, bz, :].rearrange("p (a b) -> p a b", b=T), col(kind[2] + "_norm_g"), inv,
                            ALU.mult, ALU.mult))
                    dve.sem_inc(free[bz], 1)
                    dve.sem_inc(s_qroot_free, 1)
                elif kind == "s1":
                    b0 = A.bank("s0", i)
                    nm = small[:, 8 + 8 * (i % 2):12 + 8 * (i % 2)]
                    z = small[:, 12 + 8 * (i % 2):16 + 8 * (i % 2)]
                    A.filled(dve, "s0", i)
                    A.filled(dve, *job)
                    for bc in (b0, b):
                        diagonal = ps[:, bc, P:3 * P].rearrange("p (a b) -> p a b", b=P)
                        own.mark(dve.memset(diagonal[0:DH, :, DH:P], NEG))
                    own.settle()
                    for c, bc in ((0, b0), (1, b)):
                        own.mark(dve.tensor_reduce(nm[:, c:c + 1], ps[:, bc, 0:T], AX, ALU.max))
                        own.mark(dve.tensor_reduce(nm[:, 2 + c:3 + c], ps[:, bc, T:3 * P], AX, ALU.max))
                    own.settle()
                    own(ts(nm, nm, -DH ** -0.5, None, ALU.mult))
                    dve.sem_inc(s_nm, 1)
                    dve.wait_ge(s_exp, i + 1)
                    own(dve.reciprocal(z, z))
                    zl = small[:, 24 + 2 * (i % 2):26 + 2 * (i % 2)]
                    own.mark(ts(zl[:, 0:1], z[:, 1:2], lam, None, ALU.mult))
                    own(ts(zl[:, 1:2], z[:, 3:4], lam, None, ALU.mult))
                    buf = probs[i % 2]
                    halves = ((slice(0, T), z[:, 0:1], zl[:, 0:1]), (slice(T, 3 * P), z[:, 2:3], zl[:, 1:2]))
                    for keys, _, l in halves:
                        own.mark(ts(buf[:, 1, keys], buf[:, 1, keys], l, None, ALU.mult))
                    own.settle()
                    for keys, r, _ in halves:
                        own.mark(stt(buf[:, 0, keys], buf[:, 0, keys], r, buf[:, 1, keys], ALU.mult, ALU.subtract))
                    own.settle()
                    dve.sem_inc(s_diff, 1)
                elif kind == "dT":
                    A.filled(dve, *job)
                    if i >= 2:
                        A.filled(dve, "o", i - 2)
                    own(dve.tensor_copy(dT[i % 2], ps[:, b, 0:3 * P]))
                    dve.sem_inc(free[b], 1)
                    dve.sem_inc(s_dT, 1)
                elif kind == "osum":
                    bo = A.bank("o", i)
                    dve.wait_ge(s_oroot, i + 1)
                    own(dve.reciprocal(oinv, oinv))
                    own(stt(qT[:, i, :], ps[:, bo, 0:T], sub_g, oinv, ALU.mult, ALU.mult))
                    dve.sem_inc(free[bo], 1)
                    dve.sem_inc(s_o, 1)
                elif kind in ("brr", "bra"):
                    if i == 0:
                        dve.wait_ge(s_gate, KD)
                    g = 2 * i + (KD if kind == "brr" else 0)
                    dst = kT[:, 2 * i:2 * i + 2, :]
                    A.filled(dve, *job)
                    if kind == "brr":
                        own(tt(dst, pair, gates[:, g:g + 2, :], ALU.mult))
                        dve.sem_inc(free[b], 1)
                    else:
                        own(tt(sq, pair, gates[:, g:g + 2, :], ALU.mult))
                        dve.sem_inc(free[b], 1)
                        own(tt(dst, dst, sq, ALU.add))
                        dve.sem_inc(s_mrg, 1)
                elif kind == "wo":
                    A.filled(dve, *job)
                    own(tt(xT[:, 2 * i:2 * i + 2, :], pair, xT[:, 2 * i:2 * i + 2, :], ALU.add))
                    dve.sem_inc(free[b], 1)
                    dve.sem_inc(s_x1, 1)

            own(tt(mod, mod, col("b_ada", 0, 6 * KD), ALU.add))
            own.mark(stt(scale1, mod[:, KD:2 * KD], 1.0, col("norm1_g_2", 0, KD), ALU.add, ALU.mult))
            own(stt(scale2, mod[:, 4 * KD:5 * KD], 1.0, col("norm2_g_2", 0, KD), ALU.add, ALU.mult))

            def top16(values, best, where, n):
                for half in range(2):
                    s = slice(8 * half, 8 * half + 8)
                    for r in range(n):
                        own.mark(dve.max(best[:, r, s], values[:, r, :]))
                    own.settle()
                    for r in range(n):
                        own.mark(dve.max_index(where[:, r, s], best[:, r, s], values[:, r, :]))
                    own.settle()
                    if half == 0:
                        for r in range(n):
                            own.mark(dve.match_replace(values[:, r, :], best[:, r, s], values[:, r, :], -3e38))
                        own.settle()

            dve.wait_ge(s_iota, 1)
            for tile in range(TT):
                dve.wait_ge(s_ps, 4 * (tile + 1))
                top16(scores[:, tile], top, top_i.bitcast(U32), 2 * PH)
                own.mark(dve.tensor_copy(top_f, top_i.bitcast(U32)))
                of = top.rearrange("p (h c) k -> p h c k", c=2)
                fi = top_f.rearrange("p (h c) k -> p h c k", c=2)
                four = [P, PH, TOPK, TOPK]
                own(tt(cand.rearrange("p h (x y) -> p h x y", y=TOPK), of[:, :, 0, :].unsqueeze(3).to_broadcast(four),
                       of[:, :, 1, :].unsqueeze(2).to_broadcast(four), ALU.add))
                top16(cand, top_s, pos.bitcast(U32), PH)
                own(dve.tensor_copy(soft[:, 0:PH], top_s[:, :, 0]))
                own(tt(top_s, top_s, soft[:, 0:PH].unsqueeze(2).to_broadcast([P, PH, TOPK]), ALU.subtract))
                dve.sem_inc(s_soft_in, 1)
                hot4 = hot.rearrange("p (h k) x -> p h k x", k=TOPK)
                for op, arg, c, dst in ((ALU.logical_shift_right, 4, 0, i1_of), (ALU.bitwise_and, 15, 1, i2_of)):
                    own(ts(half_pos.bitcast(U32), pos.bitcast(U32), arg, None, op))
                    own(dve.tensor_copy(half_f, half_pos.bitcast(U32)))
                    own(tt(hot4, half_f.unsqueeze(3).to_broadcast(four),
                           iota16.unsqueeze(1).unsqueeze(1).to_broadcast(four), ALU.is_equal))
                    own(tt(hot4, hot4, fi[:, :, c, :].unsqueeze(2).to_broadcast(four), ALU.mult))
                    own(dve.tensor_reduce(dst, hot4, AX, ALU.add))
                own(stt(i1_of, i1_of, float(PK), i2_of, ALU.mult, ALU.add))
                own(dve.tensor_copy(peer_idx[:, tile, :].bitcast(U32), i1_of.rearrange("p h k -> p (h k)")))
                dve.wait_ge(s_soft, tile + 1)
                own(dve.tensor_reduce(soft[:, 0:PH], top_s, AX, ALU.add))
                own(dve.reciprocal(soft[:, 0:PH], soft[:, 0:PH]))
                own(tt(peer_g[:, tile, :].rearrange("p (h k) -> p h k", k=TOPK), top_s,
                       soft[:, 0:PH].unsqueeze(2).to_broadcast([P, PH, TOPK]), ALU.mult))
                dve.sem_inc(s_route, 1)

            dve.sem_inc(s_dot, 8)
            for tile in range(TT):
                dve.wait_ge(s_h2r, 2 * (tile + 1))
                with dve.Fori(0, PH // 2) as i:
                    for par in range(2):
                        g = tile * PH + par
                        for k in range(TOPK):
                            dve.wait_ge(u_full[k % 8], i * 64 + 16 * (2 * g + k // 8 + 1))
                            dve.tensor_tensor_reduce(u_rows[k % 8], u_rows[k % 8], h2_rows[:, tile, :], 1.0, 0.0,
                                                     ALU.mult, ALU.add, dots[:, par, k:k + 1]).then_inc(s_dot, 1)
                        dve.wait_ge(s_dot, i * 32 + TOPK * (g + 1) + 8)
                        dve.sem_inc(s_dots, 1)
                        dve.wait_ge(s_act, i * 2 + g + 1)
                        tt(wts[:, par, :], dots[:, par, :],
                           peer_g[:, tile, bass.ds(i * (2 * TOPK) + par * TOPK, TOPK)], ALU.mult).then_inc(s_wts, 1)

            def norm_hB(scale, shift):
                own(dve.reciprocal(rstd, rstd))
                for c in range(KD):
                    own.mark(stt(hT[:, c, :], xT[:, c, :], scale[:, c:c + 1], rstd, ALU.mult, ALU.mult))
                own.settle()
                for c in range(KD):
                    own.mark(ts(hT[:, c, :], hT[:, c, :], mod[:, shift + c:shift + c + 1], None, ALU.add))
                own.settle()
                dve.sem_inc(s_hB, 1)

            taps = [(tap, c) for tap in range(TAPS2) for c in range(KC)]
            for job in plan_second():
                kind, i = job[0], job[1] if len(job) > 1 else 0
                b = B.bank(*job)
                bank = ps[:, b, :]
                pair = bank.rearrange("p (a b) -> p a b", b=T)
                if kind == "ss3":
                    dve.wait_ge(s_x2, 4)
                    dve.wait_ge(s_rootB, 1)
                    norm_hB(scale1, 0)
                elif kind == "ss4":
                    dve.wait_ge(s_rootB, 2)
                    norm_hB(scale2, 3 * KD)
                elif kind == "uv":
                    B.filled(dve, *job)
                    dve.wait_ge(s_sig, i + 1)
                    own(tt(pad[:, 2 * i:2 * i + 2, TAPS2 - 1:], pair, sigB[:, 2 * i:2 * i + 2, :], ALU.mult))
                    dve.sem_inc(free[b], 1)
                elif kind == "f":
                    B.filled(dve, *job)
                    x, y, l, w = (fx[0:DH, j, :] for j in range(4))
                    own(ts(x, ps[0:DH, b, 0:T], col("b_forget")[0:DH], None, ALU.add))
                    dve.sem_inc(free[b], 1)
                    own(ts(y, x, -1.0, None, ALU.mult))
                    own(tt(y, x, y, ALU.min))
                    dve.sem_inc(s_fe, 1)
                    own(ts(x, x, 0.0, None, ALU.min))
                    dve.wait_ge(s_fl, 1)
                    own(tt(x, x, l, ALU.subtract))
                    own(dve.memset(w, 1.0))
                    own(dve.tensor_tensor_scan(y, w, x, 0.0, ALU.mult, ALU.add))
                    own(ts(y, y, DH ** 0.5, None, ALU.mult))
                    dve.wait_ge(s_poolB, 1)
                    own.mark(ts(f_right[0:32, :], y[0:32, :], -1.0, None, ALU.mult))
                    own.mark(dve.tensor_copy(f_left[0:32], ident[0:32, 0:HB].unsqueeze(2).to_broadcast([32, HB, T])))
                    own.mark(tt(f_left[32:64], fx[32:64, 1, :].unsqueeze(1).to_broadcast([32, HB, T]),
                                ident[32:64, 32:32 + HB].unsqueeze(2).to_broadcast([32, HB, T]), ALU.mult))
                    own.settle()
                    dve.sem_inc(s_fm, 1)
                elif kind == "s":
                    nm = smallB[:, 2 * (i % 2):2 * (i % 2) + 2]
                    z = smallB[:, 4 + 2 * (i % 2):6 + 2 * (i % 2)]
                    B.filled(dve, *job)
                    diagonal = ps[:, b, P:3 * P].rearrange("p (a b) -> p a b", b=P)
                    own(tt(diagonal, diagonal, cmask.unsqueeze(1).to_broadcast([P, 2, P]), ALU.add))
                    own.mark(dve.tensor_reduce(nm[:, 0:1], ps[:, b, 0:T], AX, ALU.max))
                    own(dve.tensor_reduce(nm[:, 1:2], ps[:, b, T:3 * P], AX, ALU.max))
                    own(ts(nm, nm, -DH ** -0.5, None, ALU.mult))
                    dve.sem_inc(s_mxB, 1)
                    for tap, c in taps[16 * i:16 * i + 16]:
                        src = pad[:, c, tap:tap + T]
                        w = col("conv_w_2", c * TAPS2 + tap)
                        if tap == 0:
                            own.mark(ts(conv[:, c, :], src, w, col("conv_b_2", c), ALU.mult, ALU.add))
                        else:
                            own.mark(stt(conv[:, c, :], src, w, conv[:, c, :], ALU.mult, ALU.add))
                        if c == KC - 1:
                            own.settle()
                    if i == HB - 1:
                        dve.sem_inc(s_conv, 1)
                    dve.wait_ge(s_exB, i + 1)
                    own(dve.reciprocal(z, z))
                    for t, keys in ((0, slice(0, T)), (1, slice(T, 3 * P))):
                        own.mark(ts(pB[i % 2][:, keys], pB[i % 2][:, keys], z[:, t:t + 1], None, ALU.mult))
                    own.settle()
                    dve.sem_inc(s_prB, 1)
                elif kind == "dT":
                    B.filled(dve, *job)
                    if i >= 2:
                        B.filled(dve, "o", i - 2)
                    own(dve.tensor_copy(pTB[i % 2], ps[:, b, 0:3 * P]))
                    dve.sem_inc(free[b], 1)
                    dve.sem_inc(s_pTB, 1)
                elif kind == "mean":
                    B.filled(dve, *job)
                    own(ts(meanB, ps[:, b, 0:T], 1.0 / CW, None, ALU.mult))
                    dve.sem_inc(free[b], 1)
                    own(tt(conv, conv, meanB.unsqueeze(1).to_broadcast([P, KC, T]), ALU.subtract))
                    dve.sem_inc(s_cen, 1)
                elif kind == "var":
                    dve.wait_ge(s_croot, 1)
                    dve.wait_ge(s_csq, 1)
                    own(dve.reciprocal(invB, invB))
                    own(tt(conv, conv, invB.unsqueeze(1).to_broadcast([P, KC, T]), ALU.mult))
                    dve.sem_inc(s_cn, 1)
                elif kind in ("bra", "brc"):
                    if i == 0:
                        dve.wait_ge(s_gateB, KD)
                    g = 2 * i + (KD if kind == "bra" else 0)
                    dst = mixed[:, 2 * i:2 * i + 2, :]
                    B.filled(dve, *job)
                    if kind == "bra":
                        own(tt(dst, pair, gates[:, g:g + 2, :], ALU.mult))
                        dve.sem_inc(free[b], 1)
                    else:
                        own(tt(sigB[:, 0:2, :], pair, gates[:, g:g + 2, :], ALU.mult))
                        dve.sem_inc(free[b], 1)
                        own(tt(dst, dst, sigB[:, 0:2, :], ALU.add))
                        dve.sem_inc(s_mix, 1)
                elif kind == "wo":
                    B.filled(dve, *job)
                    for j in range(2):
                        c = 2 * i + j
                        own.mark(stt(xT[:, c, :], ps[:, b, j * T:(j + 1) * T], mod[:, 2 * KD + c:2 * KD + c + 1],
                                     xT[:, c, :], ALU.mult, ALU.add))
                    own.settle()
                    dve.sem_inc(free[b], 1)
                    dve.sem_inc(s_x3, 1)
                    if i == 3:
                        for s in range(RING):
                            dve.wait_ge(r_free[s], len([n for n in range(len(units)) if n % RING == s]))
                        own(tt(g2_diag, ident.unsqueeze(1).to_broadcast([P, KD, P]),
                               mod[:, 5 * KD:6 * KD].unsqueeze(2).to_broadcast([P, KD, P]), ALU.mult))
                        dve.sem_inc(s_g2d, 1)
                elif kind == "route":
                    B.filled(dve, *job)
                    own.mark(dve.memset(logits[:, E:E + 4], 3e38))
                    own(tt(logits[:, 0:E], ps[:, b, 0:E], b_route, ALU.add))
                    dve.sem_inc(free[b], 1)
                    own(dve.max(m8, logits))
                    own(dve.match_replace(logits_r, m8, logits, -3e38))
                    own(ts(smallM[:, 0:1], m8[:, 4:5], -1.0, None, ALU.mult))
                    dve.sem_inc(s_rmax, 1)
                    dve.wait_ge(s_rexp, i + 1)
                    own(tt(logits_r[:, 0:E], logits_r[:, 0:E], logits[:, 0:E], ALU.not_equal))
                    own(tt(chosen, chosen, logits_r[:, 0:E], ALU.mult))
                    own(dve.tensor_reduce(smallM[:, 1:2], chosen, AX, ALU.add))
                    own(dve.reciprocal(smallM[:, 1:2], smallM[:, 1:2]))
                    own(ts(gate_rows[:, i, :], chosen, smallM[:, 1:2], None, ALU.mult))
                    dve.sem_inc(s_gr, 1)
                elif kind == "gT":
                    B.filled(dve, *job)
                    own(dve.memset(gT, 0.0))
                    own(dve.tensor_copy(gT[0:E, :], ps[0:E, b, 0:T]))
                    dve.sem_inc(free[b], 1)
                    own(tt(gdiag[0:E], gT[0:E, :].unsqueeze(1).to_broadcast([E, E, T]),
                           ident[0:E, 0:E].unsqueeze(2).to_broadcast([E, E, T]), ALU.mult))
                    dve.sem_inc(s_gd, 1)

            for n in range(4):
                dve.sem_inc(z_free[n], 1)
            dve.wait_ge(s_smallw, 16 * 5)
            dve.wait_ge(s_gbc, E // 2)
            with dve.Fori(0, E) as e:
                own.enter(e, 4 * KD)
                for m in range(KD):
                    b, g, u = 4 + m % 4, g_act[m % 2], u_act[m % 2]
                    dve.wait_ge(s_z, e * KD + m + 1)
                    if m >= 2:
                        dve.wait_ge(s_sg, e * KD + m - 1)
                    ts(g, ps[:, b, 0:T], b1[:, bass.ds(e, 1), m], LIMIT, ALU.add, ALU.min).then_inc(s_g, 1)
                    own(ts(u, ps[:, b, T:2 * T], b1[:, bass.ds(e, 1), KD + m], LIMIT, ALU.add, ALU.min))
                    dve.sem_inc(z_free[m % 4], 1)
                    own(ts(u, u, -LIMIT, 1.0, ALU.max, ALU.add))
                    dve.wait_ge(s_g, e * KD + m + 1)
                    own(tt(u, u, g, ALU.mult))
                    own(tt(u, u, gate_bc[:, bass.ds(e, 1), :].rearrange("p e t -> p (e t)"), ALU.mult))
                    dve.wait_ge(s_sg, e * KD + m + 1)
                    dve.wait_ge(s_hu, e * KD + 1)
                    tt(hm[:, m, :], u, sg_act[m % 2], ALU.mult).then_inc(s_hm, 1)
                own.leave(E)

            dve.wait_ge(s_hu, E * KD + 1)
            dve.wait_ge(s_row, 16)
            for t in range(TT):
                for half in range(2):
                    h = slice(half * 512, (half + 1) * 512)
                    own(tt(y_rows[:, t, h], ps[:, 2 * t + half, :], g2_row[:, h], ALU.mult))
                own(tt(y_rows[:, t, :], y_rows[:, t, :], x3_rows[:, t, :], ALU.add))
                own(dve.tensor_tensor_reduce(x3_rows[:, t, :], y_rows[:, t, :], y_rows[:, t, :], 1.0, 0.0, ALU.mult,
                                             ALU.add, smallM[:, 2 + t:3 + t]))
            dve.sem_inc(s_y, 1)
            dve.wait_ge(s_yroot, 1)
            own(dve.reciprocal(smallM[:, 2:4], smallM[:, 2:4]))
            for t in range(TT):
                stt(y_rows[:, t, :], y_rows[:, t, :], smallM[:, 2 + t:3 + t], final_row, ALU.mult, ALU.mult)\
                    .then_inc(s_yn, 1)


def _units(w, columns):
    k, n = w.shape
    return np.ascontiguousarray(w.reshape(k // P, P, n // columns, columns).transpose(2, 1, 0, 3)).reshape(
        n // columns, P, k // P * columns)


def _chunks(v):
    return v.reshape(-1, P).T


def _layout(i):
    a = {}
    a["xT"] = np.ascontiguousarray(i["x"][0].T.reshape(KD, P, T).transpose(1, 0, 2))
    w_in = i["w_in"][0]
    a["w_in"] = _units(w_in, 512)
    a["w_br_rnn"] = _units(i["w_br_rnn"][0], 256)
    for name in ("w_br_attn", "w_out", "w_peer_q"):
        a[name] = _units(i[name][0], 512)
    a["sub_keys"] = np.ascontiguousarray(i["peer_sub_keys"][0].reshape(2 * PH, PK, P).transpose(2, 0, 1)).reshape(
        1, P, 2 * PH * PK)
    a["w_ada"] = np.ascontiguousarray(i["w_ada_2"][0].T.reshape(12, 4, P, D).transpose(0, 2, 1, 3)).reshape(
        12, P, 4 * D)
    a["peer_u"], a["peer_v"] = i["peer_u"][0], i["peer_v"][0]
    w = i["w_in_2"][0]
    a["w_in_2"] = np.concatenate([_units(w[:, 0:2560], 512), _units(w[:, 2568:], 512)])
    w_f = np.zeros((P, KD, DH), np.float32)
    for s in (0, 32):
        w_f[:, :, s:s + HB] = w[:, 2560:2568].reshape(KD, P, HB).transpose(1, 0, 2)
    a["w_f"] = w_f
    a["w_router"] = np.ascontiguousarray(i["w_router_2"][0].reshape(KD, P, E).transpose(1, 0, 2))
    a["w_attn_out_2"] = _units(i["w_attn_out_2"][0], D)
    a["w_conv_out_2"] = _units(i["w_conv_out_2"][0], D)
    a["w_out_2"] = _units(i["w_out_2"][0], 512)
    a["b_router"] = i["b_router_2"][0]
    a["b_exp_in"] = np.ascontiguousarray(i["b_exp_in_2"][0].reshape(E, 2 * KD, P).transpose(2, 0, 1))
    a["b_exp_out"] = i["b_exp_out_2"][0]
    a["final_g"] = i["final_g_2"]
    a["w_exp"] = w_exp = np.empty((E, 6, P, SLOT), np.float32)
    up = i["w_exp_in_2"][0].reshape(E, KD, P, 2, 4, T)
    w_exp[:, 0:4] = up.transpose(0, 4, 2, 1, 3, 5).reshape(E, 4, P, SLOT)
    w_exp[:, 4:6] = i["w_exp_out_2"][0].reshape(E, 2, 4, P, D).transpose(0, 1, 3, 2, 4).reshape(E, 2, P, SLOT)
    gates = np.zeros((P, 2, CR, P), np.float32)
    for g, name in enumerate(("w_rg_a", "w_rg_x")):
        w = i[name][0].reshape(CR, 2, DH, DH)
        for s in range(2):
            gates[s * DH:(s + 1) * DH, g, :, s * DH:(s + 1) * DH] = w[:, s].transpose(1, 0, 2)
    a["w_rg"] = gates
    for name in ("lambda_q1", "lambda_k1", "lambda_q2", "lambda_k2"):
        a[name] = i[name][0]
    a["c_2"] = i["c_2"][0]
    cols = np.zeros((P, N_COLS), np.float32)

    def put(name, v):
        s, n = COLS[name]
        cols[0:v.shape[0], s:s + n] = v

    for name, key in (("norm1_g", "norm1_g"), ("b_gate", "b_gate"), ("conv_b", "conv_b"), ("b_rg_a", "b_rg_a"),
                      ("b_rg_x", "b_rg_x"), ("rg_lambda", "rg_lambda"), ("norm2_g", "norm2_g"), ("b_ada", "b_ada_2"),
                      ("norm1_g_2", "norm1_g_2"), ("conv_b_2", "conv_b_2"), ("conv_ln_g", "conv_ln_g_2"),
                      ("conv_ln_b", "conv_ln_b_2"), ("norm2_g_2", "norm2_g_2"), ("subln_g", "subln_g")):
        put(name, _chunks(i[key][0]))
    for name in ("q_norm_g", "k_norm_g"):
        put(name, np.concatenate([i[name][0], i[name][0]])[:, None])
    put("conv_w", i["conv_w"][0].reshape(TAPS1, CR, P).transpose(2, 1, 0).reshape(P, CR * TAPS1))
    put("conv_w_2", i["conv_w_2"][0].reshape(TAPS2, KC, P).transpose(2, 1, 0).reshape(P, KC * TAPS2))
    put("b_forget", i["b_forget_2"][0][:, None])
    cols[32:32 + HB, COLS["b_forget"][0]] = i["b_forget_2"][0]
    a["cols"] = cols
    return a


def kernel(**inputs):
    import concourse.bacc as bacc
    from concourse.bass_utils import run_bass_kernel_spmd

    nc = bacc.Bacc("TRN2", target_bir_lowering=False, num_devices=1)
    arrays, aps = {}, {}
    for name, v in _layout(inputs).items():
        arrays[f"in_{name}"] = v
        aps[name] = nc.dram_tensor(f"in_{name}", v.shape, F32, kind="ExternalInput").ap()
    out = nc.dram_tensor("out", (T, D), F32, kind="ExternalOutput").ap()
    build_program(nc, aps, out)
    r = run_bass_kernel_spmd(nc, [arrays], core_ids=[0])
    return r.results[0]["out"].reshape(1, T, D)
```

```python
from contextlib import ExitStack

import numpy as np

import concourse.bass as bass
from concourse import mybir

F32 = mybir.dt.float32
U32 = mybir.dt.uint32
ALU = mybir.AluOpType
ACT = mybir.ActivationFunctionType
AX = mybir.AxisListType.X

P = 128
T = 256
TT = T // P
D = 1024
KD = D // P
EPS1 = 1e-6
EPS2 = 1e-5
NEG = -1e30
LAM_INIT = 0.2

HA, DH = 8, 64
DR = 1280
CR = DR // P
TAPS1 = 4
PH, PK, TOPK = 8, 128, 16
N_EXPERTS_PEER = PK * PK
HB = 8
CW = 512
KC = CW // P
TAPS2 = 31
E, FE = 32, 1024
LIMIT, ALPHA = 7.0, 1.702

SLOT = 4096
RING = 5
N_BANKS = 8

COLS = {}


def _column(name, n):
    start = sum(c for _, c in COLS.values())
    COLS[name] = (start, n)


for _name, _n in (("norm1_g", KD), ("b_gate", 2 * KD), ("q_norm_g", 1), ("k_norm_g", 1), ("subln_g", 1),
                  ("conv_w", CR * TAPS1), ("conv_b", CR), ("b_rg_a", CR), ("b_rg_x", CR), ("rg_lambda", CR),
                  ("norm2_g", KD), ("b_ada", 6 * KD), ("norm1_g_2", KD), ("conv_w_2", KC * TAPS2),
                  ("conv_b_2", KC), ("conv_ln_g", KC), ("conv_ln_b", KC), ("norm2_g_2", KD), ("b_forget", 1)):
    _column(_name, _n)
N_COLS = sum(c for _, c in COLS.values())



def plan_first():
    s = [("ss1",)]
    late = []
    projections = ([("xr", i) for i in range(CR // 2)] + [("yr", 0)] + [("q", i) for i in range(4)]
                   + [("k", i) for i in range(4)] + [("v", i) for i in range(4)])
    for n, p in enumerate(projections):
        s.append(p)
        for when, steps in [x for x in late if x[0] <= n]:
            s.extend(steps)
        late = [x for x in late if x[0] > n]
        if p[0] == "xr":
            late.append((n + 2, [("rg", 2 * p[1]), ("rg", 2 * p[1] + 1)]))
        if p[0] in "qk":
            late.append((n + 1, [("ss" + p[0], p[1])]))
    assert not late
    slots = [("yr", i) for i in range(1, 5)] + [("gate", i) for i in range(KD)]
    for n, p in enumerate(slots):
        s.append(p)
        if 3 <= n < HA + 3:
            s.append(("osum", n - 3))
        if 2 <= n < HA + 2:
            s.append(("o", n - 2))
        if 1 <= n < HA + 1:
            s.append(("dT", n - 1))
        if n < HA:
            s += [("s0", n), ("s1", n)]
    s += [("brr", i) for i in range(4)] + [("bra", i) for i in range(4)] + [("wo", i) for i in range(4)]
    s.append(("ss2",))
    s += [("h2r", i) for i in range(4)]
    s += [("pq", i) for i in range(8)]
    s += [("key", i) for i in range(8)]
    return s


def plan_second():
    s = [("x2T", i) for i in range(4)] + [("ss3",)]
    s += [("ug", i) for i in range(2)] + [("uv", i) for i in range(2)] + [("f",)]
    s += [("q", i) for i in range(2)] + [("k", i) for i in range(2)] + [("v", i) for i in range(2)]
    for n in range(KD):
        s.append(("gate", n))
        if n >= 2:
            s.append(("o", n - 2))
        if n >= 1:
            s.append(("dT", n - 1))
        s.append(("s", n))
    s += [("o", HB - 2), ("dT", HB - 1), ("mean",), ("o", HB - 1), ("var",)]
    s += [("bra", i) for i in range(4)] + [("brc", i) for i in range(4)] + [("wo", i) for i in range(4)]
    s.append(("ss4",))
    s += [("route", i) for i in range(TT)]
    s += [("x3r", i) for i in range(4)] + [("g2r", i) for i in range(2)]
    s += [("h3r", i) for i in range(4)] + [("rank",), ("gT",), ("xg", 0), ("xg", 1)]
    return s


EXPERT_JOBS = (("Zg0", 4), ("Zu0", 5), ("Zg1", 6), ("Tg0", 7), ("Tu0", 4), ("Zu1", 5), ("Tg1", 6), ("S", 7),
               ("G0", 7), ("G1", 4), ("Tu1", 5), ("D0", 6), ("D1", 7))
EXPERT_BANK = dict(EXPERT_JOBS)


class ExpertJobs:

    def __init__(self, full, free):
        self.full, self.free = full, free
        self.uses = {b: [j for j, x in EXPERT_JOBS if x == b] for b in (4, 5, 6, 7)}

    def claim(self, pe, q, job):
        b = EXPERT_BANK[job]
        pe.wait_ge(self.free[b - 4], q * len(self.uses[b]) + self.uses[b].index(job) + 1)

    def filled(self, eng, q, job):
        b = EXPERT_BANK[job]
        eng.wait_ge(self.full[b - 4], q * len(self.uses[b]) + self.uses[b].index(job) + 1)


def plan_units():
    w = lambda i: ("w_in", i, SLOT)
    ada = lambda i: ("w_ada", i, SLOT)
    first = [w(6), w(7), w(8), ada(0), w(0), ada(1), w(1), ada(2), w(2), ada(3), w(3), ada(4), w(4), ada(5),
             w(5), ada(6), w(9), ada(7), w(10), ada(8), w(11), ada(9), w(12), ada(10), w(13), ada(11), w(14)]
    first += [("w_br_rnn", i, CR * 256) for i in range(4)] + [("w_br_attn", i, SLOT) for i in range(2)]
    first += [("w_out", i, SLOT) for i in range(2)] + [("w_peer_q", i, SLOT) for i in range(4)]
    first += [("sub_keys", 0, 2 * PH * PK)]
    second = [("w_in_2", i, SLOT) for i in (1, 0, 2, 3, 4, 5, 6, 7, 8)]
    second += [("w_attn_out_2", 0, SLOT), ("w_conv_out_2", 0, SLOT)] + [("w_out_2", i, SLOT) for i in range(2)]
    return first, second


class Jobs:

    def __init__(self, plan, full, free, before=None):
        self.number = {step: n for n, step in enumerate(plan)}
        self.full, self.free = full, free
        self.base = [before.base[b] + before.jobs(b) if before else 0 for b in range(N_BANKS)]

    def jobs(self, b):
        return sum(n % N_BANKS == b for n in self.number.values())

    def bank(self, *job):
        return self.number[job] % N_BANKS

    def claim(self, pe, *job):
        n = self.number[job]
        if n >= N_BANKS:
            pe.wait_ge(self.free[n % N_BANKS], self.base[n % N_BANKS] + n // N_BANKS)

    def filled(self, eng, *job):
        n = self.number[job]
        eng.wait_ge(self.full[n % N_BANKS], self.base[n % N_BANKS] + n // N_BANKS + 1)

    def all_free(self, eng):
        for b in range(N_BANKS):
            eng.wait_ge(self.free[b], self.base[b] + self.jobs(b))


class Own:

    def __init__(self, eng, sem):
        self.eng, self.sem, self.n, self.loop = eng, sem, 0, None

    def mark(self, ins):
        ins.then_inc(self.sem, 1)
        self.n += 1

    def settle(self):
        self.eng.wait_ge(self.sem, self.n if self.loop is None else self.loop + self.n)

    def __call__(self, ins):
        self.mark(ins)
        self.settle()

    def enter(self, i, per):
        self.start, self.per = self.n, per
        self.loop = i * per

    def leave_open(self):
        assert self.n - self.start == self.per, (self.n - self.start, self.per)
        self.loop = None

    def leave(self, count):
        assert self.n - self.start == self.per, (self.n - self.start, self.per)
        self.n, self.loop = self.start + self.per * count, None


def build_program(nc, a, out):
    first_units, second_units = plan_units()
    units = first_units + second_units
    unit_at = {(name, i): n for n, (name, i, _) in enumerate(units)}
    n_first = len(first_units)

    with ExitStack() as ctx:
        def sem(name):
            return ctx.enter_context(nc.semaphore(name))

        ring = ctx.enter_context(nc.sbuf_tensor("ring", [P, 6 * SLOT], F32))
        arena_words = 27400
        arena = ctx.enter_context(nc.sbuf_tensor("arena", [P, arena_words], F32))
        ps = ctx.enter_context(nc.psum_tensor("ps", [P, N_BANKS, 512], F32))
        at = {"fixed": 0}

        def carve(region, *shape):
            n = int(np.prod(shape))
            start = at[region]
            at[region] = start + n
            assert at[region] <= arena_words, (region, at[region])
            v = arena[:, start:start + n]
            if len(shape) == 2:
                v = v.rearrange("p (a b) -> p a b", b=shape[1])
            if len(shape) == 3:
                v = v.rearrange("p (a b c) -> p a b c", b=shape[1], c=shape[2])
            return v

        ident = carve("fixed", P)
        ones = carve("fixed", P)
        cols = carve("fixed", N_COLS)
        eps = carve("fixed", 2)
        xT = carve("fixed", KD, T)
        hT = carve("fixed", KD, T)
        rstd = carve("fixed", T)
        mod = carve("fixed", 6 * KD)
        scale1, scale2 = carve("fixed", KD), carve("fixed", KD)
        iota_i, iota16 = carve("fixed", TOPK), carve("fixed", TOPK)

        def col(name, i=0, n=1):
            s = COLS[name][0] + i
            return cols[:, s:s + n]

        at["A"] = at["fixed"]
        qT = carve("A", KD, T)
        kT = carve("A", KD, T)
        v_rows = carve("A", TT, D)
        rnnT = carve("A", CR, T)
        w_gates = carve("A", 2, CR, P)
        c_row = carve("A", D)
        xr = [carve("A", 2, T + TAPS1 - 1) for _ in range(2)]
        xc = [carve("A", 2, T) for _ in range(3)]
        ri = carve("A", 2, 2, T)
        decay, e_w, poly, gelu_y = (carve("A", 2, T) for _ in range(4))
        blocks = carve("A", P)
        probs = [carve("A", 2, 3 * P) for _ in range(2)]
        dT = [carve("A", 3 * P) for _ in range(2)]
        sq = carve("A", 2, T)
        inv = carve("A", 2, T)
        osq = carve("A", T)
        oinv = carve("A", T)
        lams = carve("A", 4, DH)
        small = carve("A", 40)
        sp = carve("A", 6, CR)
        x_sq = rnnT
        gates = ring[:, 5 * SLOT:6 * SLOT].rearrange("p (a b) -> p a b", b=T)

        at["P"] = at["fixed"]
        h2_rows = carve("P", TT, D)
        qpT = carve("P", 2 * PH, T)
        scores = carve("P", TT, 2 * PH, PK)
        cand = carve("P", PH, TOPK * TOPK)
        hot = carve("P", PH * TOPK, TOPK)
        top = carve("P", 2 * PH, TOPK)
        top_i = carve("P", 2 * PH, TOPK)
        top_f = carve("P", 2 * PH, TOPK)
        top_s = carve("P", PH, TOPK)
        pos = carve("P", PH, TOPK)
        half_pos = carve("P", PH, TOPK)
        half_f = carve("P", PH, TOPK)
        i1_of, i2_of = carve("P", PH, TOPK), carve("P", PH, TOPK)
        soft = carve("P", 2 * PH)
        peer_idx = carve("P", TT, PH * TOPK)
        peer_g = carve("P", TT, PH * TOPK)
        idx_now = carve("P", 2, TOPK)
        dots = carve("P", 2, TOPK)
        wts = carve("P", 2, TOPK)
        x2_rows = h2_rows
        diag = qpT.rearrange("p (g k) t -> p g k t", g=2).rearrange("p g k t -> p g (k t)").rearrange(
            "p g (k t) -> p g k t", t=P)
        u_rows = [ring[:, i * D:(i + 1) * D] for i in range(8)]
        v_gath = [ring[:, (8 + i) * D:(9 + i) * D] for i in range(16)]

        at["B"] = at["fixed"] + TT * D
        qz = carve("B", HB, T)
        kv = carve("B", KD, T)
        kB = kv[:, 0:KC, :]
        vB = kv[:, KC:KD, :].rearrange("p (a b) t -> p a (b t)", a=TT)
        attnB = carve("B", KC, T)
        pad = carve("B", KC, T + TAPS2 - 1)
        conv = carve("B", KC, T)
        sigB = carve("B", KC, T)
        sqB = carve("B", KC, T)
        mixed = carve("B", KD, T)
        pB = [carve("B", 3 * P) for _ in range(2)]
        pTB = [carve("B", 3 * P) for _ in range(2)]
        cmask = carve("B", P)
        w_f = carve("B", KD, DH)
        fx = carve("B", 4, T)
        f_right = carve("B", T)
        f_left = carve("B", HB, T)
        smallB = carve("B", 24)
        meanB, invB = carve("B", T), carve("B", T)
        xsqB = kv
        kept = arena_words - (KD * E + E + E * 2 * KD + D)
        assert at["B"] <= kept, (at["B"], kept)
        at["K"] = kept
        w_r = carve("K", KD, E)
        b_route = carve("K", E)
        b1 = carve("K", E, 2 * KD)
        b2 = carve("K", D)

        at["M"] = at["fixed"]
        h3_rows = carve("M", TT, D)
        x3_rows = carve("M", TT, D)
        xg = carve("M", KD, P)
        z_sb = carve("M", 4, 512)
        hm = carve("M", KD, P)
        yg = carve("M", D)
        g_act = [carve("M", 4, P) for _ in range(2)]
        u_act = [carve("M", 4, P) for _ in range(2)]
        sg_act = [carve("M", 4, P) for _ in range(2)]
        sel = carve("M", TT, P)
        selg = carve("M", TT, P)
        selgT = carve("M", T)
        g2_row = carve("M", D)
        final_row = carve("M", D)
        slot_of = carve("M", TT, 2 * E + 1)
        gate_of = carve("M", TT, 2 * E + 1)
        before = carve("M", P)
        iota_row = carve("M", P)
        iota_row_i = carve("M", P)
        logits = carve("M", E + 4)
        logits_r = carve("M", E + 4)
        m8 = carve("M", 8)
        chosen = carve("M", E)
        gate_rows = carve("M", TT, E)
        picked = carve("M", TT, E)
        gT = carve("M", T)
        smallM = carve("M", 8)
        passes_i = carve("M", 2)
        assert at["M"] <= kept, (at["M"], kept)
        y_rows = ring[:, 0:TT * D].rearrange("p (a b) -> p a b", b=D)
        g2_diag = ring[:, 2 * SLOT:2 * SLOT + KD * P].rearrange("p (c j) -> p c j", j=P)
        w1_unit = [ring[:, n * SLOT:(n + 1) * SLOT].rearrange("p (c j) -> p c j", c=KD) for n in range(4)]
        w2_unit = [ring[:, n * SLOT:(n + 1) * SLOT].rearrange("p (c j) -> p c j", j=D) for n in (4, 5)]

        s_par = sem("params_loaded")
        s_x = sem("x_loaded")
        s_wg = sem("gate_weights_loaded")
        s_const, s_iota = sem("constants_ready"), sem("iota_ready")
        full = [sem(f"bank_full_{b}") for b in range(N_BANKS)]
        free = [sem(f"bank_free_{b}") for b in range(N_BANKS)]
        r_full = [sem(f"unit_loaded_{b}") for b in range(RING)]
        r_free = [sem(f"unit_used_{b}") for b in range(RING)]
        s_vend = sem("vector_own_end")
        s_v, s_a, s_p = sem("vector_own"), sem("scalar_own"), sem("pool_own")
        A = Jobs(plan_first(), full, free)
        B = Jobs(plan_second(), full, free, before=A)

        def unit(name, i):
            n = unit_at[(name, i)]
            s = n % RING
            return ring[:, s * SLOT:s * SLOT + units[n][2]]

        def unit_loaded(eng, name, i):
            n = unit_at[(name, i)]
            eng.wait_ge(r_full[n % RING], 16 * (n // RING + 1))

        def unit_used(name, i):
            return r_free[unit_at[(name, i)] % RING]

        s_sq = sem("squares_ready")
        s_root = sem("root_ready")
        s_h = sem("h_ready")
        s_xr = sem("xr_ready")
        s_xc = sem("xc_ready")
        s_ri = sem("rnn_gates_ready")
        s_rnn_free = sem("rnn_gates_used")
        s_dec = sem("decay_exponent_ready")
        s_expw = sem("decay_ready")
        s_poly = sem("mult_squared_ready")
        s_mult = sem("mult_ready")
        s_gel = sem("gelu_y_ready")
        s_gel_free = sem("rnn_pair_done")
        s_qsq = sem("qk_squares_ready")
        s_qroot = sem("qk_root_ready")
        s_qroot_free = sem("qk_ready")
        s_vr = sem("v_rows_ready")
        s_gate = sem("branch_gates_ready")
        s_nm = sem("negative_max_ready")
        s_exp = sem("exponentials_ready")
        s_diff = sem("probabilities_ready")
        s_dT = sem("transposed_probs_ready")
        s_osq = sem("head_squares_ready")
        s_oroot = sem("head_root_ready")
        s_o = sem("head_output_ready")
        s_mrg = sem("merged_ready")
        s_x1 = sem("residual_ready")
        s_silu = sem("silu_c_ready")
        s_sp = sem("lambda_exp_ready")
        s_spw = sem("lambda_in_ready")
        s_h2r = sem("h2_rows_ready")
        s_pq = sem("peer_queries_ready")
        s_ps = sem("peer_scores_ready")
        s_out = sem("output_stored")
        s_soft_in = sem("peer_top_ready")
        s_soft = sem("peer_exp_ready")
        s_route = sem("peer_routes_ready")
        s_idx = sem("peer_start")
        s_dot = sem("u_rows_used")
        s_dots = sem("dots_ready")
        s_act = sem("gelu_dots_ready")
        s_wts = sem("expert_weights_ready")
        s_diag = sem("diagonals_ready")
        s_pv = sem("v_rows_used")
        u_full = [sem(f"u_row_loaded_{k}") for k in range(8)]
        v_full = [sem(f"v_row_loaded_{k}") for k in range(16)]
        s_x2r = sem("x2_rows_ready")
        s_x2 = sem("x2_ready")
        s_smallw = sem("small_weights_loaded")
        s_poolB = sem("second_constants_ready")
        s_sig = sem("glu_gate_ready")
        s_fe, s_fl, s_fm = sem("forget_exp_in"), sem("forget_log_ready"), sem("forget_matrices_ready")
        s_qkv = sem("qkv_ready")
        s_conv, s_cen, s_csq = sem("conv_ready"), sem("centred_ready"), sem("centred_squares_ready")
        s_croot, s_cn, s_silu2 = sem("conv_root_ready"), sem("conv_normed_ready"), sem("conv_silu_ready")
        s_rmax, s_rexp, s_gr = sem("router_max_ready"), sem("router_exp_ready"), sem("gate_rows_ready")
        s_x3r, s_h3r = sem("x3_rows_ready"), sem("h3_rows_ready")
        s_pick, s_slots, s_gT = sem("picked_ready"), sem("slots_ready"), sem("gates_transposed")
        s_poolM = sem("expert_constants_ready")
        s_g2d = sem("g2_diagonals_ready")
        w_full = [sem(f"expert_unit_loaded_{n}") for n in range(6)]
        x_full = [sem(f"expert_bank_full_{b}") for b in range(4, 8)]
        x_free = [sem(f"expert_bank_free_{b}") for b in range(4, 8)]
        X = ExpertJobs(x_full, x_free)
        s_sel = sem("selection_ready")
        s_selg = sem("gated_selection_ready")
        s_selgT = sem("gated_selection_transposed")
        s_xg = sem("expert_tokens_ready")
        s_zc = sem("z_copied")
        s_g, s_sg = sem("expert_gate_ready"), sem("expert_sigmoid_ready")
        s_hm = sem("expert_hidden_ready")
        s_yg = sem("expert_rows_ready")
        s_fin = sem("experts_done")
        s_y, s_yroot, s_yn = sem("y_ready"), sem("y_root_ready"), sem("y_normed")
        s_row = sem("rows_loaded")

        block = ctx.enter_context(nc.Block())

        @block.sync
        def _(sp):
            sp.dma_start(xT, a["xT"]).then_inc(s_x, 16)
            sp.dma_start(cols, a["cols"]).then_inc(s_par, 16)
            sp.dma_start(w_gates, a["w_rg"]).then_inc(s_wg, 16)
            for i, name in enumerate(("lambda_q1", "lambda_k1", "lambda_q2", "lambda_k2")):
                sp.dma_start(lams[:, i, :], a[name].partition_broadcast(P)).then_inc(s_par, 16)
            sp.dma_start(c_row, a["c_2"].partition_broadcast(P)).then_inc(s_par, 16)
            for n, (name, i, words) in enumerate(units[:n_first]):
                if n >= RING:
                    sp.wait_ge(r_free[n % RING], n // RING)
                sp.dma_start(unit(name, i), a[name][i]).then_inc(r_full[n % RING], 16)
            sp.wait_ge(s_dot, 8 + TT * PH * TOPK)
            sp.wait_ge(s_pv, 17 + TT * PH * TOPK)
            for name, dst in (("w_f", w_f), ("w_router", w_r), ("b_exp_in", b1)):
                sp.dma_start(dst, a[name]).then_inc(s_smallw, 16)
            sp.dma_start(b_route, a["b_router"].partition_broadcast(P)).then_inc(s_smallw, 16)
            sp.wait_ge(s_poolB, 1)
            sp.dma_start(b2[0:E, :], a["b_exp_out"]).then_inc(s_smallw, 16)
            for n in range(n_first, len(units)):
                name, i, words = units[n]
                if n >= n_first + RING:
                    sp.wait_ge(r_free[n % RING], n // RING)
                sp.dma_start(unit(name, i), a[name][i]).then_inc(r_full[n % RING], 16)
            sp.wait_ge(s_x3r, 6)
            sp.wait_ge(s_mrg, 4 + 4)
            sp.dma_start(final_row, a["final_g"].partition_broadcast(P)).then_inc(s_row, 16)

            def load(e, n):
                sp.dma_start(ring[:, n * SLOT:(n + 1) * SLOT],
                             a["w_exp"][bass.ds(e, 1), n].rearrange("e p w -> (e p) w")).then_inc(w_full[n], 16)

            sp.wait_ge(s_slots, 1)
            passes = sp.value_load(passes_i[0:1, 0:1].bitcast(mybir.dt.int32), min_val=1, max_val=2)
            with sp.Fori(0, passes) as p:
                sp.wait_ge(s_yg, p * (2 * E) + 1)
                for n in range(6):
                    load(0, n)
                with sp.Fori(1, E) as e:
                    q = p * E + e - 1
                    for n, job in enumerate(("Zg0", "Zu0", "Zg1", "Zu1", "D0", "D1")):
                        X.filled(sp, q, job)
                        load(e, n)
            sp.wait_ge(s_yn, TT)
            sp.dma_start(out.rearrange("(a p) d -> p a d", p=P), y_rows).then_inc(s_out, 16)
            sp.wait_ge(s_out, 16)

        @block.gpsimd
        def _(pool):
            own = Own(pool, s_p)
            own.mark(pool.memset(ident, 0.0))
            own.mark(pool.memset(blocks, 0.0))
            own.mark(pool.memset(ones, 1.0))
            own.mark(pool.memset(eps[:, 0:1], EPS1))
            own.mark(pool.memset(eps[:, 1:2], EPS2))
            own.settle()
            own(pool.affine_select(out=ident, in_=ident, compare_op=ALU.not_equal, fill=1.0, base=0,
                                   pattern=[[-1, P]], channel_multiplier=1))
            own(pool.memset(blocks[0:DH, 0:DH], 1.0))
            own(pool.memset(blocks[DH:P, DH:P], 1.0))
            for i in range(2):
                own.mark(pool.memset(xr[i][:, :, 0:TAPS1 - 1], 0.0))
            own.settle()
            pool.sem_inc(s_const, 1)
            own(pool.iota(iota_i.bitcast(mybir.dt.int32), pattern=[[1, TOPK]], base=0, channel_multiplier=0))
            own(pool.tensor_copy(iota16, iota_i.bitcast(mybir.dt.int32)))
            pool.sem_inc(s_iota, 1)

            A.all_free(pool)
            for s in range(RING):
                pool.wait_ge(r_free[s], len([n for n in range(n_first) if n % RING == s]))
            pool.wait_ge(s_mrg, 4)
            for tile in range(TT):
                pool.wait_ge(s_route, tile + 1)
                per = 2 * (1 + 2 * TOPK)
                with pool.Fori(0, PH // 2) as i:
                    own.enter(i, per)
                    for par in range(2):
                        g = tile * PH + par
                        pool.wait_ge(s_pv, i * (2 * TOPK) + TOPK * g + 1)
                        own(pool.tensor_copy(idx_now[:, par, :].bitcast(U32),
                                             peer_idx[:, tile, bass.ds(i * (2 * TOPK) + par * TOPK, TOPK)]
                                             .bitcast(U32)))
                        for k in range(TOPK):
                            own.mark(pool.wait_ge(s_dot, i * (2 * TOPK) + TOPK * g + k + 1))
                            pool.indirect_dma_start(
                                out=u_rows[k % 8], out_offset=None, in_=a["peer_u"],
                                in_offset=bass.IndirectOffsetOnAxis(ap=idx_now[:, par, k:k + 1].bitcast(U32), axis=0)
                            ).then_inc(u_full[k % 8], 16)
                        for k in range(TOPK):
                            own.mark(pool.wait_ge(s_pv, i * (2 * TOPK) + TOPK * g + k + 2))
                            pool.indirect_dma_start(
                                out=v_gath[k], out_offset=None, in_=a["peer_v"],
                                in_offset=bass.IndirectOffsetOnAxis(ap=idx_now[:, par, k:k + 1].bitcast(U32), axis=0)
                            ).then_inc(v_full[k], 16)
                own.leave(PH // 2)

            pool.wait_ge(s_dot, 8 + TT * PH * TOPK)
            pool.wait_ge(s_pv, 17 + TT * PH * TOPK)
            for dst in (qz, f_left, pad[:, :, 0:TAPS2 - 1], b2, cmask):
                own.mark(pool.memset(dst, 0.0))
            own.mark(pool.memset(f_right, 1.0))
            own.settle()
            own(pool.affine_select(out=cmask, in_=cmask, compare_op=ALU.is_ge, fill=NEG, base=0,
                                   pattern=[[-1, P]], channel_multiplier=1))
            pool.sem_inc(s_poolB, 1)
            pool.wait_ge(s_x1, 4 + 4)
            own.mark(pool.memset(before, 1.0))
            own.mark(pool.memset(slot_of, -1.0))
            own.mark(pool.memset(gate_of, 0.0))
            own.mark(pool.memset(selgT, 0.0))
            own.mark(pool.memset(yg, 0.0))
            own.mark(pool.memset(gT, 0.0))
            own.mark(pool.iota(iota_row_i.bitcast(mybir.dt.int32), pattern=[[1, P]], base=0, channel_multiplier=0))
            own.settle()
            own(pool.affine_select(out=before, in_=before, compare_op=ALU.is_gt, fill=0.0, base=0,
                                   pattern=[[1, P]], channel_multiplier=-1))
            own(pool.tensor_copy(iota_row, iota_row_i.bitcast(mybir.dt.int32)))
            pool.sem_inc(s_poolM, 1)

        @block.tensor
        def _(pe):
            def mm(o, l, r, start, stop):
                return pe.matmul(o, l, r, start=start, stop=stop)

            def project(J, job, b, w, m, src, nk, half):
                for c in range(nk):
                    last = mm(ps[:, b, half * T:(half + 1) * T], w[:, c, m * P:(m + 1) * P], src[:, c, :],
                              c == 0, c == nk - 1)
                return last

            pe.wait_ge(s_const, 1)
            inc = None
            seen = {}
            for job in plan_first():
                kind, i = job[0], job[1] if len(job) > 1 else 0
                b = A.bank(*job)
                seen[kind] = seen.get(kind, 0) + 1
                if kind in ("xr", "yr", "q", "k", "gate"):
                    first = {"q": 0, "k": 8, "xr": 24, "yr": 34, "gate": 44}[kind] + 2 * i
                    u = first // 4
                    w = unit("w_in", u).rearrange("p (c n) -> p c n", c=KD)
                    unit_loaded(pe, "w_in", u)
                    if kind == "xr" and i == 0:
                        pe.wait_ge(s_h, KD)
                    A.claim(pe, *job)
                    project(A, job, b, w, first % 4, hT, KD, 0)
                    last = project(A, job, b, w, first % 4 + 1, hT, KD, 1)
                    last.then_inc(full[b], 1)
                    if first % 4 == 2:
                        pe.wait_ge(full[b], A.number[job] // N_BANKS + 1).then_inc(unit_used("w_in", u), 1)
                elif kind == "v":
                    u = 4 + i // 2
                    w = unit("w_in", u).rearrange("p (c n) -> p c n", c=KD)
                    unit_loaded(pe, "w_in", u)
                    A.claim(pe, *job)
                    for c in range(KD):
                        last = mm(ps[:, b, :], hT[:, c, (i % 2) * P:(i % 2 + 1) * P], w[:, c, :], c == 0, c == KD - 1)
                    last.then_inc(full[b], 1)
                    if i % 2 == 1:
                        pe.wait_ge(full[b], A.number[job] // N_BANKS + 1).then_inc(unit_used("w_in", u), 1)
                elif kind in ("ss1", "ss2"):
                    pe.wait_ge(s_sq, 1 if kind == "ss1" else 2)
                    A.claim(pe, *job)
                    for c in range(KD):
                        last = mm(ps[:, b, 0:T], ones, x_sq[:, c, :], c == 0, c == KD - 1)
                    last.then_inc(full[b], 1)
                elif kind == "rg":
                    if i % 2 == 0:
                        pe.wait_ge(s_xc, i // 2 + 1)
                    if i == 0:
                        pe.wait_ge(s_wg, 16)
                    A.claim(pe, *job)
                    for g in range(2):
                        last = mm(ps[:, b, g * T:(g + 1) * T], w_gates[:, g, i, :], xc[i // 2 % 3][:, i % 2, :],
                                  True, True)
                    last.then_inc(full[b], 1)
                elif kind in ("ssq", "ssk"):
                    n = i + (4 if kind == "ssk" else 0)
                    pe.wait_ge(s_qsq, n + 1)
                    A.claim(pe, *job)
                    mm(ps[:, b, :], blocks, sq.rearrange("p a b -> p (a b)"), True, True).then_inc(full[b], 1)
                elif kind in ("s0", "s1"):
                    if i == 0:
                        pe.wait_ge(s_qroot_free, 8)
                    A.claim(pe, *job)
                    h = slice(0, DH) if kind == "s0" else slice(DH, P)
                    mm(ps[:, b, 0:T], qT[h, i, P:T], kT[h, i, :], True, True)
                    mm(ps[:, b, T:3 * P], qT[h, i, 0:P], kT[h, i, 0:P], True, True).then_inc(full[b], 1)
                elif kind == "dT":
                    pe.wait_ge(s_diff, i + 1)
                    A.claim(pe, *job)
                    pe.transpose(ps[:, b, 0:P], probs[i % 2][:, 0, T:3 * P], ident)
                    pe.transpose(ps[:, b, P:2 * P], probs[i % 2][:, 0, 0:P], ident)
                    pe.transpose(ps[:, b, 2 * P:3 * P], probs[i % 2][:, 0, P:T], ident).then_inc(full[b], 1)
                elif kind == "o":
                    pe.wait_ge(s_dT, i + 1)
                    if i == 0:
                        pe.wait_ge(s_vr, 4)
                    A.claim(pe, *job)
                    mm(ps[:, b, 0:T], v_rows[:, 0, i * P:(i + 1) * P], dT[i % 2][:, 0:T], True, False)
                    mm(ps[:, b, P:T], v_rows[:, 1, i * P:(i + 1) * P], dT[i % 2][:, T:3 * P], False, True)\
                        .then_inc(full[b], 1)
                elif kind == "osum":
                    pe.wait_ge(s_osq, i + 1)
                    A.claim(pe, *job)
                    mm(ps[:, b, 0:T], ones, osq, True, True).then_inc(full[b], 1)
                elif kind == "brr":
                    if i == 0:
                        pe.wait_ge(s_gel_free, CR // 2)
                    unit_loaded(pe, "w_br_rnn", i)
                    w = unit("w_br_rnn", i).rearrange("p (c n) -> p c n", c=CR)
                    A.claim(pe, *job)
                    project(A, job, b, w, 0, rnnT, CR, 0)
                    project(A, job, b, w, 1, rnnT, CR, 1).then_inc(full[b], 1)
                    pe.wait_ge(full[b], A.number[job] // N_BANKS + 1).then_inc(unit_used("w_br_rnn", i), 1)
                elif kind in ("bra", "wo"):
                    name, src = ("w_br_attn", qT) if kind == "bra" else ("w_out", kT)
                    if i == 0:
                        if kind == "bra":
                            pe.wait_ge(s_o, HA)
                        else:
                            pe.wait_ge(s_mrg, 4)
                    unit_loaded(pe, name, i // 2)
                    w = unit(name, i // 2).rearrange("p (c n) -> p c n", c=KD)
                    A.claim(pe, *job)
                    project(A, job, b, w, 2 * (i % 2), src, KD, 0)
                    project(A, job, b, w, 2 * (i % 2) + 1, src, KD, 1).then_inc(full[b], 1)
                    if i % 2 == 1:
                        pe.wait_ge(full[b], A.number[job] // N_BANKS + 1).then_inc(unit_used(name, i // 2), 1)
                elif kind == "h2r":
                    if i == 0:
                        pe.wait_ge(s_h, 2 * KD)
                    A.claim(pe, *job)
                    for j in range(4):
                        last = pe.transpose(ps[:, b, j * P:(j + 1) * P],
                                            hT[:, 4 * (i % 2) + j, (i // 2) * P:(i // 2 + 1) * P], ident)
                    last.then_inc(full[b], 1)
                elif kind == "pq":
                    unit_loaded(pe, "w_peer_q", i // 2)
                    w = unit("w_peer_q", i // 2).rearrange("p (c n) -> p c n", c=KD)
                    A.claim(pe, *job)
                    project(A, job, b, w, 2 * (i % 2), hT, KD, 0)
                    project(A, job, b, w, 2 * (i % 2) + 1, hT, KD, 1).then_inc(full[b], 1)
                    if i % 2 == 1:
                        pe.wait_ge(full[b], A.number[job] // N_BANKS + 1).then_inc(unit_used("w_peer_q", i // 2), 1)
                elif kind == "key":
                    if i == 0:
                        unit_loaded(pe, "sub_keys", 0)
                        pe.wait_ge(s_pq, 8)
                    A.claim(pe, *job)
                    keys = unit("sub_keys", 0).rearrange("p (c n) -> p c n", n=PK)
                    for j in range(4):
                        hc = 4 * (i % 4) + j
                        last = mm(ps[:, b, j * PK:(j + 1) * PK], qpT[:, hc, (i // 4) * P:(i // 4 + 1) * P],
                                  keys[:, hc, :], True, True)
                    last.then_inc(full[b], 1)
                    if i == 7:
                        pe.wait_ge(full[b], A.number[job] // N_BANKS + 1).then_inc(unit_used("sub_keys", 0), 1)
                else:
                    raise ValueError(job)

            def add(o, l, r, start=False):
                return pe.matmul(o, l, r, start=start, stop=False, skip_group_check=True)

            A.all_free(pe)
            pe.sem_inc(s_pv, 17)
            for tile in range(TT):
                for c in range(KD):
                    add(ps[:, 2 * tile + c // 4, (c % 4) * P:(c % 4 + 1) * P], xT[:, c, tile * P:(tile + 1) * P],
                        ident, start=(c % 4 == 0))
                with pe.Fori(0, PH // 2) as i:
                    for par in range(2):
                        g = tile * PH + par
                        pe.wait_ge(s_diag, i * 2 + g + 1)
                        for k in range(TOPK):
                            pe.wait_ge(v_full[k], i * 32 + 16 * (g + 1))
                            add(ps[:, 2 * tile, :], diag[:, par, k, :], v_gath[k][:, 0:512])
                            add(ps[:, 2 * tile + 1, :], diag[:, par, k, :], v_gath[k][:, 512:D]).then_inc(s_pv, 1)

            def gather(b, half):
                for j in range(4):
                    c = 4 * half + j
                    for t in range(TT):
                        last = mm(ps[:, b, j * P:(j + 1) * P], h3_rows[:, t, c * P:(c + 1) * P], sel[:, t, :],
                                  t == 0, t == TT - 1)
                return last

            for job in plan_second():
                kind, i = job[0], job[1] if len(job) > 1 else 0
                b = B.bank(*job)

                def release(name, u):
                    pe.wait_ge(full[b], B.base[b] + B.number[job] // N_BANKS + 1).then_inc(unit_used(name, u), 1)

                if kind == "x2T":
                    if i == 0:
                        pe.wait_ge(s_x2r, TT)
                    B.claim(pe, *job)
                    for j in range(2):
                        for t in range(TT):
                            last = pe.transpose(ps[:, b, j * T + t * P:j * T + (t + 1) * P],
                                                x2_rows[:, t, (2 * i + j) * P:(2 * i + j + 1) * P], ident)
                    last.then_inc(full[b], 1)
                elif kind in ("ss3", "ss4"):
                    pe.wait_ge(s_sq, 3 if kind == "ss3" else 4)
                    B.claim(pe, *job)
                    for c in range(KD):
                        last = mm(ps[:, b, 0:T], ones, xsqB[:, c, :], c == 0, c == KD - 1)
                    last.then_inc(full[b], 1)
                elif kind in ("ug", "uv", "q", "k", "gate"):
                    u = {"ug": 1, "uv": 0, "q": 2, "k": 3, "gate": 5}[kind] + i // 2
                    w = unit("w_in_2", u).rearrange("p (c n) -> p c n", c=KD)
                    unit_loaded(pe, "w_in_2", u)
                    if kind == "ug" and i == 0:
                        pe.wait_ge(s_h, 2 * KD + 1)
                    B.claim(pe, *job)
                    project(B, job, b, w, 2 * (i % 2), hT, KD, 0)
                    project(B, job, b, w, 2 * (i % 2) + 1, hT, KD, 1).then_inc(full[b], 1)
                    if i % 2 == 1:
                        release("w_in_2", u)
                elif kind == "v":
                    w = unit("w_in_2", 4).rearrange("p (c n) -> p c n", c=KD)
                    unit_loaded(pe, "w_in_2", 4)
                    B.claim(pe, *job)
                    for c in range(KD):
                        last = mm(ps[:, b, :], hT[:, c, i * P:(i + 1) * P], w[:, c, :], c == 0, c == KD - 1)
                    last.then_inc(full[b], 1)
                    if i == 1:
                        release("w_in_2", 4)
                elif kind == "f":
                    pe.wait_ge(s_smallw, 16 * 5)
                    B.claim(pe, *job)
                    for c in range(KD):
                        last = mm(ps[0:DH, b, 0:T], w_f[:, c, :], hT[:, c, :], c == 0, c == KD - 1)
                    last.then_inc(full[b], 1)
                elif kind == "s":
                    if i == 0:
                        pe.wait_ge(s_qkv, 6)
                        pe.wait_ge(s_fm, 1)
                    B.claim(pe, *job)
                    mm(ps[:, b, 0:T], qz[:, i, P:T], kB[:, i // 2, :], True, False)
                    mm(ps[:, b, 0:T], f_left[:, i, P:T], f_right, False, True)
                    mm(ps[:, b, T:3 * P], qz[:, i, 0:P], kB[:, i // 2, 0:P], True, False)
                    mm(ps[:, b, T:3 * P], f_left[:, i, 0:P], f_right[:, 0:P], False, True).then_inc(full[b], 1)
                elif kind == "dT":
                    pe.wait_ge(s_diff, HA + i + 1)
                    B.claim(pe, *job)
                    pe.transpose(ps[:, b, 0:P], pB[i % 2][:, T:3 * P], ident)
                    pe.transpose(ps[:, b, P:2 * P], pB[i % 2][:, 0:P], ident)
                    pe.transpose(ps[:, b, 2 * P:3 * P], pB[i % 2][:, P:T], ident).then_inc(full[b], 1)
                elif kind == "o":
                    pe.wait_ge(s_dT, HA + i + 1)
                    B.claim(pe, *job)
                    c = slice(i // 2 * P, (i // 2 + 1) * P)
                    mm(ps[:, b, 0:T], vB[:, 0, c], pTB[i % 2][:, 0:T], True, False)
                    mm(ps[:, b, P:T], vB[:, 1, c], pTB[i % 2][:, T:3 * P], False, True).then_inc(full[b], 1)
                elif kind in ("mean", "var"):
                    if kind == "mean":
                        pe.wait_ge(s_conv, 1)
                    else:
                        pe.wait_ge(s_csq, 1)
                    B.claim(pe, *job)
                    for c in range(KC):
                        last = mm(ps[:, b, 0:T], ones, (conv if kind == "mean" else sqB)[:, c, :], c == 0, c == KC - 1)
                    last.then_inc(full[b], 1)
                elif kind in ("bra", "brc"):
                    name, src = ("w_attn_out_2", attnB) if kind == "bra" else ("w_conv_out_2", conv)
                    unit_loaded(pe, name, 0)
                    if i == 0:
                        if kind == "bra":
                            pe.wait_ge(s_o, HA + HB)
                        else:
                            pe.wait_ge(s_silu2, 1)
                    w = unit(name, 0).rearrange("p (c n) -> p c n", c=KC)
                    B.claim(pe, *job)
                    project(B, job, b, w, 2 * i, src, KC, 0)
                    project(B, job, b, w, 2 * i + 1, src, KC, 1).then_inc(full[b], 1)
                    if i == 3:
                        release(name, 0)
                elif kind == "wo":
                    if i == 0:
                        pe.wait_ge(s_mrg, 4 + 4)
                    unit_loaded(pe, "w_out_2", i // 2)
                    w = unit("w_out_2", i // 2).rearrange("p (c n) -> p c n", c=KD)
                    B.claim(pe, *job)
                    project(B, job, b, w, 2 * (i % 2), mixed, KD, 0)
                    project(B, job, b, w, 2 * (i % 2) + 1, mixed, KD, 1).then_inc(full[b], 1)
                    if i % 2 == 1:
                        release("w_out_2", i // 2)
                elif kind == "route":
                    if i == 0:
                        pe.wait_ge(s_h, 2 * KD + 2)
                    B.claim(pe, *job)
                    for c in range(KD):
                        last = mm(ps[:, b, 0:E], hT[:, c, i * P:(i + 1) * P], w_r[:, c, :], c == 0, c == KD - 1)
                    last.then_inc(full[b], 1)
                elif kind == "gT":
                    pe.wait_ge(s_gr, TT)
                    B.claim(pe, *job)
                    for t in range(TT):
                        last = pe.transpose(ps[0:E, b, t * P:(t + 1) * P], gate_rows[:, t, :], ident)
                    last.then_inc(full[b], 1)
                elif kind == "rank":
                    pe.wait_ge(s_pick, 1)
                    pe.wait_ge(s_poolM, 1)
                    B.claim(pe, *job)
                    mm(ps[:, b, 0:E], before, picked[:, 0, :], True, True)
                    mm(ps[:, b, E:2 * E], before, picked[:, 1, :], True, False)
                    mm(ps[:, b, E:2 * E], ones, picked[:, 0, :], False, True)
                    mm(ps[:, b, 2 * E:3 * E], ones, picked[:, 0, :], True, False)
                    mm(ps[:, b, 2 * E:3 * E], ones, picked[:, 1, :], False, True).then_inc(full[b], 1)
                elif kind == "xg":
                    if i == 0:
                        pe.wait_ge(s_sel, 1)
                        pe.wait_ge(s_h3r, 4)
                    B.claim(pe, *job)
                    gather(b, i).then_inc(full[b], 1)
                elif kind == "h3r":
                    B.claim(pe, *job)
                    for j in range(4):
                        last = pe.transpose(ps[:, b, j * P:(j + 1) * P],
                                            hT[:, 4 * (i % 2) + j, (i // 2) * P:(i // 2 + 1) * P], ident)
                    last.then_inc(full[b], 1)
                elif kind == "x3r":
                    B.claim(pe, *job)
                    for j in range(4):
                        last = pe.transpose(ps[:, b, j * P:(j + 1) * P],
                                            xT[:, 4 * (i % 2) + j, (i // 2) * P:(i // 2 + 1) * P], ident)
                    last.then_inc(full[b], 1)
                elif kind == "g2r":
                    if i == 0:
                        pe.wait_ge(s_g2d, 1)
                    B.claim(pe, *job)
                    mm(ps[:, b, :], ones, g2_diag[:, 4 * i:4 * i + 4, :].rearrange("p c j -> p (c j)"),
                       True, True).then_inc(full[b], 1)
                else:
                    raise ValueError(job)

            B.all_free(pe)
            pe.wait_ge(s_gT, 1)
            for t in range(TT):
                for half in range(2):
                    add(ps[:, 2 * t + half, :], gT[:, t * P:(t + 1) * P], b2[:, half * 512:(half + 1) * 512],
                        start=True)
            for b in range(4):
                pe.sem_inc(x_free[b], 1)
            pe.sem_inc(s_selgT, 1)
            pe.sem_inc(s_yg, 1)

            def filled_by(ins, job):
                ins.then_inc(x_full[EXPERT_BANK[job] - 4], 1)

            def hidden(q, n, job):
                pe.wait_ge(w_full[n], q * 16 + 16)
                X.claim(pe, q, job)
                for c in range(KD):
                    last = mm(ps[:, EXPERT_BANK[job], :], xg[:, c, :], w1_unit[n][:, c, :], c == 0, c == KD - 1)
                filled_by(last, job)

            def turn(q, n, job):
                pe.wait_ge(s_zc, q * 4 + n + 1)
                X.claim(pe, q, job)
                for j in range(4):
                    last = pe.transpose(ps[:, EXPERT_BANK[job], j * P:(j + 1) * P], z_sb[:, n, j * P:(j + 1) * P],
                                        ident)
                filled_by(last, job)

            def combine(q):
                pe.wait_ge(s_yg, q * 2 + 1)
                pe.wait_ge(s_selgT, q + 1)
                for t in range(TT):
                    for half in range(2):
                        last = add(ps[:, 2 * t + half, :], selgT[:, t * P:(t + 1) * P],
                                   yg[:, half * 512:(half + 1) * 512])
                return last

            pe.wait_ge(s_slots, 1)
            passes = pe.value_load(passes_i[0:1, 0:1].bitcast(mybir.dt.int32), min_val=1, max_val=2)
            with pe.Fori(0, passes) as p:
                with pe.Fori(0, E) as e:
                    q = p * E + e
                    pe.wait_ge(s_xg, q * 2 + 2)
                    hidden(q, 0, "Zg0")
                    combine(q)
                    hidden(q, 1, "Zu0")
                    hidden(q, 2, "Zg1")
                    turn(q, 0, "Tg0")
                    turn(q, 1, "Tu0")
                    hidden(q, 3, "Zu1")
                    turn(q, 2, "Tg1")
                    pe.wait_ge(s_selg, q + 1)
                    X.claim(pe, q, "S")
                    pe.transpose(ps[:, 7, 0:P], selg[:, 0, :], ident)
                    filled_by(pe.transpose(ps[:, 7, P:T], selg[:, 1, :], ident), "S")
                    pe.wait_ge(s_sel, q + 2)
                    for half, job in ((0, "G0"), (1, "G1")):
                        X.claim(pe, q, job)
                        filled_by(gather(EXPERT_BANK[job], half), job)
                    turn(q, 3, "Tu1")
                    X.claim(pe, q, "D0")
                    X.claim(pe, q, "D1")
                    for k in range(KD):
                        if k % 4 == 0:
                            pe.wait_ge(w_full[4 + k // 4], q * 16 + 16)
                            pe.wait_ge(s_hm, q * 2 + k // 4 + 1)
                        for half, job in ((0, "D0"), (1, "D1")):
                            last = mm(ps[:, EXPERT_BANK[job], :], hm[:, k, :],
                                      w2_unit[k // 4][:, k % 4, half * 512:(half + 1) * 512], k == 0, k == KD - 1)
                            if k == KD - 1:
                                filled_by(last, job)
            combine(passes * E).then_inc(s_fin, 1)

        @block.scalar
        def _(act):
            own = Own(act, s_a)
            fn = act.activation
            act.wait_ge(s_x, 16)
            fn(x_sq[:, 0:KD, :], xT, ACT.Square).then_inc(s_sq, 1)
            act.wait_ge(s_const, 1)
            act.wait_ge(s_par, 16 * 6)
            fn(c_row, c_row, ACT.Silu).then_inc(s_silu, 1)
            act.wait_ge(s_spw, 1)
            fn(sp[:, 1, :], sp[:, 0, :], ACT.Exp)
            fn(small[:, 2:4], small[:, 0:2], ACT.Exp).then_inc(s_sp, 1)
            qn = 0
            for job in plan_first():
                kind, i = job[0], job[1] if len(job) > 1 else 0
                b = A.bank(*job)
                bank = ps[:, b, :]
                pair = bank.rearrange("p (a b) -> p a b", b=T)
                if kind in ("ss1", "ss2"):
                    A.filled(act, *job)
                    own(fn(rstd, ps[:, b, 0:T], ACT.Sqrt, bias=eps[:, 0:1], scale=1.0 / D))
                    act.sem_inc(free[b], 1)
                    act.sem_inc(s_root, 1)
                elif kind == "xr":
                    A.filled(act, *job)
                    if i >= 2:
                        act.wait_ge(s_xc, i - 1)
                    own(act.copy(xr[i % 2][:, :, TAPS1 - 1:], pair))
                    act.sem_inc(free[b], 1)
                    act.sem_inc(s_xr, 1)
                elif kind == "rg":
                    A.filled(act, *job)
                    if i % 2 == 0 and i >= 2:
                        act.wait_ge(s_rnn_free, i // 2)
                    own.mark(fn(ri[:, 0, i % 2, :], ps[:, b, 0:T], ACT.Sigmoid, bias=col("b_rg_a", i)))
                    own(fn(ri[:, 1, i % 2, :], ps[:, b, T:2 * T], ACT.Sigmoid, bias=col("b_rg_x", i)))
                    act.sem_inc(free[b], 1)
                    if i % 2 == 1:
                        act.sem_inc(s_ri, 1)
                        act.wait_ge(s_dec, i // 2 + 1)
                        fn(e_w, decay, ACT.Exp, scale=-0.5).then_inc(s_expw, 1)
                        act.wait_ge(s_poly, i // 2 + 1)
                        fn(poly, poly, ACT.Sqrt).then_inc(s_mult, 1)
                elif kind == "yr":
                    A.filled(act, *job)
                    if i >= 1:
                        act.wait_ge(s_gel_free, i)
                    own(fn(gelu_y, pair, ACT.Gelu_apprx_tanh))
                    act.sem_inc(free[b], 1)
                    act.sem_inc(s_gel, 1)
                elif kind in ("q", "k"):
                    A.filled(act, *job)
                    n = i + (4 if kind == "k" else 0)
                    if n >= 1:
                        A.filled(act, "ssq" if n - 1 < 4 else "ssk", (n - 1) % 4)
                    fn(sq, pair, ACT.Square).then_inc(s_qsq, 1)
                elif kind in ("ssq", "ssk"):
                    A.filled(act, *job)
                    n = i + (4 if kind == "ssk" else 0)
                    if n >= 1:
                        act.wait_ge(s_qroot_free, n)
                    own(fn(inv, pair, ACT.Sqrt, bias=eps[:, 0:1], scale=1.0 / DH))
                    act.sem_inc(free[b], 1)
                    act.sem_inc(s_qroot, 1)
                elif kind == "v":
                    A.filled(act, *job)
                    own(act.copy(v_rows[:, i % 2, (i // 2) * 512:(i // 2 + 1) * 512], bank))
                    act.sem_inc(free[b], 1)
                    act.sem_inc(s_vr, 1)
                elif kind == "gate":
                    A.filled(act, *job)
                    own.mark(fn(gates[:, 2 * i, :], ps[:, b, 0:T], ACT.Sigmoid, bias=col("b_gate", 2 * i)))
                    own(fn(gates[:, 2 * i + 1, :], ps[:, b, T:2 * T], ACT.Sigmoid, bias=col("b_gate", 2 * i + 1)))
                    act.sem_inc(free[b], 1)
                    act.sem_inc(s_gate, 1)
                elif kind == "s1":
                    act.wait_ge(s_nm, i + 1)
                    if i >= 2:
                        A.filled(act, "dT", i - 2)
                    nm = small[:, 8 + 8 * (i % 2):12 + 8 * (i % 2)]
                    z = small[:, 12 + 8 * (i % 2):16 + 8 * (i % 2)]
                    b0 = A.bank("s0", i)
                    for c, bc in ((0, b0), (1, b)):
                        for t, keys in ((0, slice(0, T)), (1, slice(T, 3 * P))):
                            own.mark(fn(probs[i % 2][:, c, keys], ps[:, bc, keys], ACT.Exp,
                                        bias=nm[:, 2 * t + c:2 * t + c + 1], scale=DH ** -0.5,
                                        accum_out=z[:, 2 * t + c:2 * t + c + 1]))
                    own.settle()
                    act.sem_inc(free[b], 1)
                    act.sem_inc(free[b0], 1)
                    act.sem_inc(s_exp, 1)
                elif kind == "o":
                    A.filled(act, *job)
                    if i >= 1:
                        A.filled(act, "osum", i - 1)
                    fn(osq, ps[:, b, 0:T], ACT.Square).then_inc(s_osq, 1)
                elif kind == "osum":
                    A.filled(act, *job)
                    if i >= 1:
                        act.wait_ge(s_o, i)
                    own(fn(oinv, ps[:, b, 0:T], ACT.Sqrt, bias=eps[:, 0:1], scale=1.0 / P))
                    act.sem_inc(free[b], 1)
                    act.sem_inc(s_oroot, 1)
                elif kind == "wo":
                    if i == 3:
                        act.wait_ge(s_x1, 4)
                        fn(x_sq[:, 0:KD, :], xT, ACT.Square).then_inc(s_sq, 1)
                elif kind == "h2r":
                    A.filled(act, *job)
                    own(act.copy(h2_rows[:, i // 2, (i % 2) * 512:(i % 2 + 1) * 512], bank))
                    act.sem_inc(free[b], 1)
                    act.sem_inc(s_h2r, 1)
                elif kind == "pq":
                    A.filled(act, *job)
                    own(act.copy(qpT[:, 2 * i:2 * i + 2, :], pair))
                    act.sem_inc(free[b], 1)
                    act.sem_inc(s_pq, 1)
                elif kind == "key":
                    A.filled(act, *job)
                    own(act.copy(scores[:, i // 4, 4 * (i % 4):4 * (i % 4) + 4, :],
                                 bank.rearrange("p (a b) -> p a b", b=PK)))
                    act.sem_inc(free[b], 1)
                    act.sem_inc(s_ps, 1)
            for tile in range(TT):
                act.wait_ge(s_soft_in, tile + 1)
                fn(top_s, top_s, ACT.Exp).then_inc(s_soft, 1)
            for tile in range(TT):
                with act.Fori(0, PH // 2) as i:
                    for par in range(2):
                        g = tile * PH + par
                        act.wait_ge(s_dots, i * 2 + g + 1)
                        fn(dots[:, par, :], dots[:, par, :], ACT.Gelu_apprx_tanh).then_inc(s_act, 1)
                        act.wait_ge(s_wts, i * 2 + g + 1)
                        act.wait_ge(s_pv, i * (2 * TOPK) + TOPK * g + 1)
                        for k in range(TOPK):
                            last = fn(diag[:, par, k, :], ident, ACT.Copy, scale=wts[:, par, k:k + 1])
                        last.then_inc(s_diag, 1)
                act.wait_ge(s_pv, 17 + (tile + 1) * PH * TOPK)
                for half in range(2):
                    last = act.copy(x2_rows[:, tile, half * 512:(half + 1) * 512], ps[:, 2 * tile + half, :])
                last.then_inc(s_x2r, 1)

            for job in plan_second():
                kind, i = job[0], job[1] if len(job) > 1 else 0
                b = B.bank(*job)
                bank = ps[:, b, :]
                pair = bank.rearrange("p (a b) -> p a b", b=T)
                if kind == "x2T":
                    B.filled(act, *job)
                    own(act.copy(xT[:, 2 * i:2 * i + 2, :], pair))
                    act.sem_inc(free[b], 1)
                    act.sem_inc(s_x2, 1)
                    if i == 3:
                        fn(xsqB, xT, ACT.Square).then_inc(s_sq, 1)
                elif kind in ("ss3", "ss4"):
                    B.filled(act, *job)
                    own(fn(rstd, ps[:, b, 0:T], ACT.Sqrt, bias=eps[:, 1:2], scale=1.0 / D))
                    act.sem_inc(free[b], 1)
                    act.sem_inc(s_root, 1)
                elif kind == "ug":
                    B.filled(act, *job)
                    own(fn(sigB[:, 2 * i:2 * i + 2, :], pair, ACT.Sigmoid))
                    act.sem_inc(free[b], 1)
                    act.sem_inc(s_sig, 1)
                elif kind == "f":
                    act.wait_ge(s_fe, 1)
                    own(fn(fx[0:DH, 2, :], fx[0:DH, 1, :], ACT.Exp))
                    own(fn(fx[0:DH, 2, :], fx[0:DH, 2, :], ACT.Ln, bias=1.0))
                    act.sem_inc(s_fl, 1)
                elif kind == "q":
                    B.filled(act, *job)
                    if i == 0:
                        act.wait_ge(s_poolB, 1)
                    z4 = qz.rearrange("p (c s) t -> p c s t", s=2)
                    own.mark(act.copy(z4[0:DH, 2 * i:2 * i + 2, 0, :], pair[0:DH]))
                    own(act.copy(z4[DH:P, 2 * i:2 * i + 2, 1, :], pair[DH:P]))
                    act.sem_inc(free[b], 1)
                    act.sem_inc(s_qkv, 1)
                elif kind == "k":
                    B.filled(act, *job)
                    own(act.copy(kB[:, 2 * i:2 * i + 2, :], pair))
                    act.sem_inc(free[b], 1)
                    act.sem_inc(s_qkv, 1)
                elif kind == "v":
                    B.filled(act, *job)
                    own(act.copy(vB[:, i, :], bank))
                    act.sem_inc(free[b], 1)
                    act.sem_inc(s_qkv, 1)
                elif kind == "gate":
                    B.filled(act, *job)
                    own(fn(gates[:, 2 * i:2 * i + 2, :], pair, ACT.Sigmoid))
                    act.sem_inc(free[b], 1)
                    act.sem_inc(s_gate, 1)
                elif kind == "s":
                    act.wait_ge(s_nm, HA + i + 1)
                    if i >= 2:
                        B.filled(act, "dT", i - 2)
                    nm = smallB[:, 2 * (i % 2):2 * (i % 2) + 2]
                    z = smallB[:, 4 + 2 * (i % 2):6 + 2 * (i % 2)]
                    for t, keys in ((0, slice(0, T)), (1, slice(T, 3 * P))):
                        own.mark(fn(pB[i % 2][:, keys], ps[:, b, keys], ACT.Exp, bias=nm[:, t:t + 1],
                                    scale=DH ** -0.5, accum_out=z[:, t:t + 1]))
                    own.settle()
                    act.sem_inc(free[b], 1)
                    act.sem_inc(s_exp, 1)
                elif kind == "o":
                    B.filled(act, *job)
                    h = slice(0, DH) if i % 2 == 0 else slice(DH, P)
                    own(act.copy(attnB[h, i // 2, :], ps[h, b, 0:T]))
                    act.sem_inc(free[b], 1)
                    act.sem_inc(s_o, 1)
                elif kind == "mean":
                    act.wait_ge(s_cen, 1)
                    fn(sqB, conv, ACT.Square).then_inc(s_csq, 1)
                elif kind == "var":
                    B.filled(act, *job)
                    own(fn(invB, ps[:, b, 0:T], ACT.Sqrt, bias=eps[:, 1:2], scale=1.0 / CW))
                    act.sem_inc(free[b], 1)
                    act.sem_inc(s_croot, 1)
                    act.wait_ge(s_cn, 1)
                    for c in range(KC):
                        last = fn(conv[:, c, :], conv[:, c, :], ACT.Silu, bias=col("conv_ln_b", c),
                                  scale=col("conv_ln_g", c))
                    last.then_inc(s_silu2, 1)
                elif kind == "wo" and i == 3:
                    act.wait_ge(s_x1, 4 + 4)
                    fn(xsqB, xT, ACT.Square).then_inc(s_sq, 1)
                elif kind == "route":
                    act.wait_ge(s_rmax, i + 1)
                    fn(chosen, logits[:, 0:E], ACT.Exp, bias=smallM[:, 0:1]).then_inc(s_rexp, 1)
                elif kind == "xg":
                    B.filled(act, *job)
                    own(act.copy(xg[:, 4 * i:4 * i + 4, :], bank.rearrange("p (a b) -> p a b", b=P)))
                    act.sem_inc(free[b], 1)
                    act.sem_inc(s_xg, 1)
                elif kind == "h3r":
                    B.filled(act, *job)
                    own(act.copy(h3_rows[:, i // 2, (i % 2) * 512:(i % 2 + 1) * 512], bank))
                    act.sem_inc(free[b], 1)
                    act.sem_inc(s_h3r, 1)
                elif kind == "x3r":
                    B.filled(act, *job)
                    own(act.copy(x3_rows[:, i // 2, (i % 2) * 512:(i % 2 + 1) * 512], bank))
                    act.sem_inc(free[b], 1)
                    act.sem_inc(s_x3r, 1)
                elif kind == "g2r":
                    B.filled(act, *job)
                    own(act.copy(g2_row[:, i * 512:(i + 1) * 512], bank))
                    act.sem_inc(free[b], 1)
                    act.sem_inc(s_x3r, 1)

            act.wait_ge(s_slots, 1)
            passes = act.value_load(passes_i[0:1, 0:1].bitcast(mybir.dt.int32), min_val=1, max_val=2)
            with act.Fori(0, passes) as p:
                with act.Fori(0, E) as e:
                    q = p * E + e
                    own.enter(q, 11 - 2)

                    def copy_out(job, dst, src, done):
                        X.filled(act, q, job)
                        own(act.copy(dst, src))
                        act.sem_inc(x_free[EXPERT_BANK[job] - 4], 1)
                        act.sem_inc(done, 1)

                    def sigmoid(n):
                        act.wait_ge(s_g, q * 2 + n + 1)
                        fn(sg_act[n], g_act[n], ACT.Sigmoid, scale=ALPHA).then_inc(s_sg, 1)

                    for n, job in enumerate(("Zg0", "Zu0", "Zg1")):
                        copy_out(job, z_sb[:, n, :], ps[:, EXPERT_BANK[job], :], s_zc)
                    sigmoid(0)
                    copy_out("Zu1", z_sb[:, 3, :], ps[:, EXPERT_BANK["Zu1"], :], s_zc)
                    copy_out("S", selgT, ps[:, 7, 0:T], s_selgT)
                    for half, job in ((0, "G0"), (1, "G1")):
                        copy_out(job, xg[:, 4 * half:4 * half + 4, :],
                                 ps[:, EXPERT_BANK[job], :].rearrange("p (a b) -> p a b", b=P), s_xg)
                    sigmoid(1)
                    for half, job in ((0, "D0"), (1, "D1")):
                        copy_out(job, yg[:, half * 512:(half + 1) * 512], ps[:, EXPERT_BANK[job], :], s_yg)
                    own.leave_open()
            act.wait_ge(s_y, 1)
            fn(smallM[:, 2:4], smallM[:, 2:4], ACT.Sqrt, bias=eps[:, 1:2], scale=1.0 / D).then_inc(s_yroot, 1)

        @block.vector
        def _(dve):
            own = Own(dve, s_v)
            ts, tt, stt = dve.tensor_scalar, dve.tensor_tensor, dve.scalar_tensor_tensor

            dve.wait_ge(s_par, 16 * 6)
            dve.wait_ge(s_const, 1)
            for i in range(2):
                own.mark(dve.tensor_tensor_reduce(lams[:, 2 * i, :], lams[:, 2 * i, :], lams[:, 2 * i + 1, :], 1.0,
                                                  0.0, ALU.mult, ALU.add, small[:, i:i + 1]))
            lam_r = col("rg_lambda", 0, CR)
            own(ts(sp[:, 2, :], lam_r, -1.0, None, ALU.mult))
            own(tt(sp[:, 0, :], sp[:, 2, :], lam_r, ALU.min))
            dve.sem_inc(s_spw, 1)
            dve.wait_ge(s_sp, 1)
            own(tt(small[:, 4:5], small[:, 2:3], small[:, 3:4], ALU.subtract))
            own(ts(small[:, 4:5], small[:, 4:5], LAM_INIT, None, ALU.add))
            lam = small[:, 4:5]
            own(ts(small[:, 5:6], col("subln_g"), 1.0 - LAM_INIT, None, ALU.mult))
            sub_g = small[:, 5:6]
            y, s_, s2, acc = sp[:, 1, :], sp[:, 3, :], sp[:, 4, :], sp[:, 5, :]
            own(ts(s_, y, 2.0, None, ALU.add))
            own(dve.reciprocal(s_, s_))
            own(tt(s_, s_, y, ALU.mult))
            own(tt(s2, s_, s_, ALU.mult))
            own(ts(acc, s2, 1.0 / 17, 1.0 / 15, ALU.mult, ALU.add))
            for k in (13, 11, 9, 7, 5, 3, 1):
                own(tt(acc, acc, s2, ALU.mult))
                own(ts(acc, acc, 1.0 / k, None, ALU.add))
            own(tt(acc, acc, s_, ALU.mult))
            own(ts(sp[:, 2, :], sp[:, 2, :], 0.0, None, ALU.max))
            own(stt(acc, acc, 2.0, sp[:, 2, :], ALU.mult, ALU.add))
            own(ts(acc, acc, 16.0, None, ALU.mult))
            decay_rate = acc

            def ada(n):
                unit_loaded(dve, "w_ada", n)
                w = unit("w_ada", n).rearrange("p (c n) -> p c n", n=D)
                if n == 0:
                    dve.wait_ge(s_silu, 1)
                for j in range(4):
                    m = 4 * n + j
                    own.mark(dve.tensor_tensor_reduce(w[:, j, :], w[:, j, :], c_row, 1.0, 0.0, ALU.mult, ALU.add,
                                                      mod[:, m:m + 1]))
                own.settle()
                dve.sem_inc(unit_used("w_ada", n), 1)

            def norm_h(coef):
                own(dve.reciprocal(rstd, rstd))
                for c in range(KD):
                    stt(hT[:, c, :], xT[:, c, :], coef(c), rstd, ALU.mult, ALU.mult).then_inc(s_h, 1)

            ada_at = {("q", 0): 0, ("q", 2): 1, ("k", 0): 2, ("k", 2): 3, ("v", 0): 4, ("v", 2): 5,
                      ("yr", 1): 6, ("yr", 3): 7, ("gate", 0): 8, ("gate", 2): 9, ("gate", 4): 10, ("gate", 6): 11}
            for job in plan_first():
                kind, i = job[0], job[1] if len(job) > 1 else 0
                b = A.bank(*job)
                bank = ps[:, b, :]
                pair = bank.rearrange("p (a b) -> p a b", b=T)
                if job in ada_at:
                    ada(ada_at[job])
                if kind == "ss1":
                    dve.wait_ge(s_x, 16)
                    dve.wait_ge(s_root, 1)
                    norm_h(lambda c: col("norm1_g", c))
                elif kind == "ss2":
                    dve.wait_ge(s_root, 2)
                    dve.wait_ge(full[A.bank("gate", 7)], A.number[("gate", 7)] // N_BANKS + 1)
                    norm_h(lambda c: col("norm2_g", c))
                elif kind == "xr":
                    dve.wait_ge(s_xr, i + 1)
                    if i >= 3:
                        A.filled(dve, "rg", 2 * (i - 3) + 1)
                    for tap in range(TAPS1):
                        for j in range(2):
                            c = 2 * i + j
                            src = xr[i % 2][:, j, tap:tap + T]
                            w = col("conv_w", c * TAPS1 + tap)
                            if tap == 0:
                                own.mark(ts(xc[i % 3][:, j, :], src, w, col("conv_b", c), ALU.mult, ALU.add))
                            else:
                                own.mark(stt(xc[i % 3][:, j, :], src, w, xc[i % 3][:, j, :], ALU.mult, ALU.add))
                        own.settle()
                    dve.sem_inc(s_xc, 1)
                elif kind == "rg" and i % 2 == 1:
                    n = i // 2
                    dve.wait_ge(s_ri, n + 1)
                    for j in range(2):
                        own.mark(ts(decay[:, j, :], ri[:, 0, j, :], decay_rate[:, 2 * n + j:2 * n + j + 1], None,
                                    ALU.mult))
                    own.settle()
                    dve.sem_inc(s_dec, 1)
                    coef = [1.0, -1.0 / 2, 1.0 / 6, -1.0 / 24, 1.0 / 120, -1.0 / 720]
                    own(ts(poly, decay, coef[5], None, ALU.mult))
                    for k in (4, 3, 2, 1, 0):
                        own(stt(poly, poly, coef[k], decay, ALU.add, ALU.mult))
                    own(tt(ri[:, 1], ri[:, 1], xc[n % 3], ALU.mult))
                    mask = ri[:, 0].bitcast(U32)
                    own(ts(mask, decay, 0.25, None, ALU.is_gt))
                    dve.wait_ge(s_expw, n + 1)
                    own(tt(decay, e_w, e_w, ALU.mult))
                    own(ts(decay, decay, -1.0, 1.0, ALU.mult, ALU.add))
                    own(dve.copy_predicated(poly, mask, decay))
                    own(ts(poly, poly, 1e-34, None, ALU.max))
                    dve.sem_inc(s_poly, 1)
                    dve.wait_ge(s_mult, n + 1)
                    own(tt(decay, poly, ri[:, 1], ALU.mult))
                    dve.sem_inc(s_rnn_free, 1)
                    for j in range(2):
                        own.mark(dve.tensor_tensor_scan(rnnT[:, 2 * n + j, :], e_w[:, j, :], decay[:, j, :], 0.0,
                                                        ALU.mult, ALU.add))
                    own.settle()
                elif kind == "yr":
                    dve.wait_ge(s_gel, i + 1)
                    own(tt(rnnT[:, 2 * i:2 * i + 2, :], rnnT[:, 2 * i:2 * i + 2, :], gelu_y, ALU.mult))
                    dve.sem_inc(s_gel_free, 1)
                elif kind in ("ssq", "ssk"):
                    n = i + (4 if kind == "ssk" else 0)
                    dst = (qT if kind == "ssq" else kT)[:, 2 * i:2 * i + 2, :]
                    bz = A.bank(kind[2], i)
                    dve.wait_ge(s_qroot, n + 1)
                    own(dve.reciprocal(inv, inv))
                    own(stt(dst, ps[:, bz, :].rearrange("p (a b) -> p a b", b=T), col(kind[2] + "_norm_g"), inv,
                            ALU.mult, ALU.mult))
                    dve.sem_inc(free[bz], 1)
                    dve.sem_inc(s_qroot_free, 1)
                elif kind == "s1":
                    b0 = A.bank("s0", i)
                    nm = small[:, 8 + 8 * (i % 2):12 + 8 * (i % 2)]
                    z = small[:, 12 + 8 * (i % 2):16 + 8 * (i % 2)]
                    A.filled(dve, "s0", i)
                    A.filled(dve, *job)
                    for bc in (b0, b):
                        diagonal = ps[:, bc, P:3 * P].rearrange("p (a b) -> p a b", b=P)
                        own.mark(dve.memset(diagonal[0:DH, :, DH:P], NEG))
                    own.settle()
                    for c, bc in ((0, b0), (1, b)):
                        own.mark(dve.tensor_reduce(nm[:, c:c + 1], ps[:, bc, 0:T], AX, ALU.max))
                        own.mark(dve.tensor_reduce(nm[:, 2 + c:3 + c], ps[:, bc, T:3 * P], AX, ALU.max))
                    own.settle()
                    own(ts(nm, nm, -DH ** -0.5, None, ALU.mult))
                    dve.sem_inc(s_nm, 1)
                    dve.wait_ge(s_exp, i + 1)
                    own(dve.reciprocal(z, z))
                    zl = small[:, 24 + 2 * (i % 2):26 + 2 * (i % 2)]
                    own.mark(ts(zl[:, 0:1], z[:, 1:2], lam, None, ALU.mult))
                    own(ts(zl[:, 1:2], z[:, 3:4], lam, None, ALU.mult))
                    buf = probs[i % 2]
                    halves = ((slice(0, T), z[:, 0:1], zl[:, 0:1]), (slice(T, 3 * P), z[:, 2:3], zl[:, 1:2]))
                    for keys, _, l in halves:
                        own.mark(ts(buf[:, 1, keys], buf[:, 1, keys], l, None, ALU.mult))
                    own.settle()
                    for keys, r, _ in halves:
                        own.mark(stt(buf[:, 0, keys], buf[:, 0, keys], r, buf[:, 1, keys], ALU.mult, ALU.subtract))
                    own.settle()
                    dve.sem_inc(s_diff, 1)
                elif kind == "dT":
                    A.filled(dve, *job)
                    if i >= 2:
                        A.filled(dve, "o", i - 2)
                    own(dve.tensor_copy(dT[i % 2], ps[:, b, 0:3 * P]))
                    dve.sem_inc(free[b], 1)
                    dve.sem_inc(s_dT, 1)
                elif kind == "osum":
                    bo = A.bank("o", i)
                    dve.wait_ge(s_oroot, i + 1)
                    own(dve.reciprocal(oinv, oinv))
                    own(stt(qT[:, i, :], ps[:, bo, 0:T], sub_g, oinv, ALU.mult, ALU.mult))
                    dve.sem_inc(free[bo], 1)
                    dve.sem_inc(s_o, 1)
                elif kind in ("brr", "bra"):
                    if i == 0:
                        dve.wait_ge(s_gate, KD)
                    g = 2 * i + (KD if kind == "brr" else 0)
                    dst = kT[:, 2 * i:2 * i + 2, :]
                    A.filled(dve, *job)
                    if kind == "brr":
                        own(tt(dst, pair, gates[:, g:g + 2, :], ALU.mult))
                        dve.sem_inc(free[b], 1)
                    else:
                        own(tt(sq, pair, gates[:, g:g + 2, :], ALU.mult))
                        dve.sem_inc(free[b], 1)
                        own(tt(dst, dst, sq, ALU.add))
                        dve.sem_inc(s_mrg, 1)
                elif kind == "wo":
                    A.filled(dve, *job)
                    own(tt(xT[:, 2 * i:2 * i + 2, :], pair, xT[:, 2 * i:2 * i + 2, :], ALU.add))
                    dve.sem_inc(free[b], 1)
                    dve.sem_inc(s_x1, 1)

            own(tt(mod, mod, col("b_ada", 0, 6 * KD), ALU.add))
            own.mark(stt(scale1, mod[:, KD:2 * KD], 1.0, col("norm1_g_2", 0, KD), ALU.add, ALU.mult))
            own(stt(scale2, mod[:, 4 * KD:5 * KD], 1.0, col("norm2_g_2", 0, KD), ALU.add, ALU.mult))

            def top16(values, best, where, n):
                for half in range(2):
                    s = slice(8 * half, 8 * half + 8)
                    for r in range(n):
                        own.mark(dve.max(best[:, r, s], values[:, r, :]))
                    own.settle()
                    for r in range(n):
                        own.mark(dve.max_index(where[:, r, s], best[:, r, s], values[:, r, :]))
                    own.settle()
                    if half == 0:
                        for r in range(n):
                            own.mark(dve.match_replace(values[:, r, :], best[:, r, s], values[:, r, :], -3e38))
                        own.settle()

            dve.wait_ge(s_iota, 1)
            for tile in range(TT):
                dve.wait_ge(s_ps, 4 * (tile + 1))
                top16(scores[:, tile], top, top_i.bitcast(U32), 2 * PH)
                own.mark(dve.tensor_copy(top_f, top_i.bitcast(U32)))
                of = top.rearrange("p (h c) k -> p h c k", c=2)
                fi = top_f.rearrange("p (h c) k -> p h c k", c=2)
                four = [P, PH, TOPK, TOPK]
                own(tt(cand.rearrange("p h (x y) -> p h x y", y=TOPK), of[:, :, 0, :].unsqueeze(3).to_broadcast(four),
                       of[:, :, 1, :].unsqueeze(2).to_broadcast(four), ALU.add))
                top16(cand, top_s, pos.bitcast(U32), PH)
                own(dve.tensor_copy(soft[:, 0:PH], top_s[:, :, 0]))
                own(tt(top_s, top_s, soft[:, 0:PH].unsqueeze(2).to_broadcast([P, PH, TOPK]), ALU.subtract))
                dve.sem_inc(s_soft_in, 1)
                hot4 = hot.rearrange("p (h k) x -> p h k x", k=TOPK)
                for op, arg, c, dst in ((ALU.logical_shift_right, 4, 0, i1_of), (ALU.bitwise_and, 15, 1, i2_of)):
                    own(ts(half_pos.bitcast(U32), pos.bitcast(U32), arg, None, op))
                    own(dve.tensor_copy(half_f, half_pos.bitcast(U32)))
                    own(tt(hot4, half_f.unsqueeze(3).to_broadcast(four),
                           iota16.unsqueeze(1).unsqueeze(1).to_broadcast(four), ALU.is_equal))
                    own(tt(hot4, hot4, fi[:, :, c, :].unsqueeze(2).to_broadcast(four), ALU.mult))
                    own(dve.tensor_reduce(dst, hot4, AX, ALU.add))
                own(stt(i1_of, i1_of, float(PK), i2_of, ALU.mult, ALU.add))
                own(dve.tensor_copy(peer_idx[:, tile, :].bitcast(U32), i1_of.rearrange("p h k -> p (h k)")))
                dve.wait_ge(s_soft, tile + 1)
                own(dve.tensor_reduce(soft[:, 0:PH], top_s, AX, ALU.add))
                own(dve.reciprocal(soft[:, 0:PH], soft[:, 0:PH]))
                own(tt(peer_g[:, tile, :].rearrange("p (h k) -> p h k", k=TOPK), top_s,
                       soft[:, 0:PH].unsqueeze(2).to_broadcast([P, PH, TOPK]), ALU.mult))
                dve.sem_inc(s_route, 1)

            dve.sem_inc(s_dot, 8)
            for tile in range(TT):
                dve.wait_ge(s_h2r, 2 * (tile + 1))
                with dve.Fori(0, PH // 2) as i:
                    for par in range(2):
                        g = tile * PH + par
                        for k in range(TOPK):
                            dve.wait_ge(u_full[k % 8], i * 64 + 16 * (2 * g + k // 8 + 1))
                            dve.tensor_tensor_reduce(u_rows[k % 8], u_rows[k % 8], h2_rows[:, tile, :], 1.0, 0.0,
                                                     ALU.mult, ALU.add, dots[:, par, k:k + 1]).then_inc(s_dot, 1)
                        dve.wait_ge(s_dot, i * 32 + TOPK * (g + 1) + 8)
                        dve.sem_inc(s_dots, 1)
                        dve.wait_ge(s_act, i * 2 + g + 1)
                        tt(wts[:, par, :], dots[:, par, :],
                           peer_g[:, tile, bass.ds(i * (2 * TOPK) + par * TOPK, TOPK)], ALU.mult).then_inc(s_wts, 1)

            def norm_hB(scale, shift):
                own(dve.reciprocal(rstd, rstd))
                for c in range(KD):
                    own.mark(stt(hT[:, c, :], xT[:, c, :], scale[:, c:c + 1], rstd, ALU.mult, ALU.mult))
                own.settle()
                for c in range(KD):
                    own.mark(ts(hT[:, c, :], hT[:, c, :], mod[:, shift + c:shift + c + 1], None, ALU.add))
                own.settle()
                dve.sem_inc(s_h, 1)

            def select(dst, n, gated):
                for t in range(TT):
                    at_n = bass.ds(n, 1)
                    if gated:
                        own.mark(ts(dst[:, t, :], iota_row, slot_of[:, t, at_n], gate_of[:, t, at_n], ALU.is_equal,
                                    ALU.mult))
                    else:
                        own.mark(ts(dst[:, t, :], iota_row, slot_of[:, t, at_n], None, ALU.is_equal))
                own.settle()

            taps = [(tap, c) for tap in range(TAPS2) for c in range(KC)]
            for job in plan_second():
                kind, i = job[0], job[1] if len(job) > 1 else 0
                b = B.bank(*job)
                bank = ps[:, b, :]
                pair = bank.rearrange("p (a b) -> p a b", b=T)
                if kind == "ss3":
                    dve.wait_ge(s_x2, 4)
                    dve.wait_ge(s_root, 2 + 1)
                    norm_hB(scale1, 0)
                elif kind == "ss4":
                    dve.wait_ge(s_root, 2 + 2)
                    norm_hB(scale2, 3 * KD)
                elif kind == "uv":
                    B.filled(dve, *job)
                    dve.wait_ge(s_sig, i + 1)
                    own(tt(pad[:, 2 * i:2 * i + 2, TAPS2 - 1:], pair, sigB[:, 2 * i:2 * i + 2, :], ALU.mult))
                    dve.sem_inc(free[b], 1)
                elif kind == "f":
                    B.filled(dve, *job)
                    x, y, l, w = (fx[0:DH, j, :] for j in range(4))
                    own(ts(x, ps[0:DH, b, 0:T], col("b_forget")[0:DH], None, ALU.add))
                    dve.sem_inc(free[b], 1)
                    own(ts(y, x, -1.0, None, ALU.mult))
                    own(tt(y, x, y, ALU.min))
                    dve.sem_inc(s_fe, 1)
                    own(ts(x, x, 0.0, None, ALU.min))
                    dve.wait_ge(s_fl, 1)
                    own(tt(x, x, l, ALU.subtract))
                    own(dve.memset(w, 1.0))
                    own(dve.tensor_tensor_scan(y, w, x, 0.0, ALU.mult, ALU.add))
                    own(ts(y, y, DH ** 0.5, None, ALU.mult))
                    dve.wait_ge(s_poolB, 1)
                    own.mark(ts(f_right[0:32, :], y[0:32, :], -1.0, None, ALU.mult))
                    own.mark(dve.tensor_copy(f_left[0:32], ident[0:32, 0:HB].unsqueeze(2).to_broadcast([32, HB, T])))
                    own.mark(tt(f_left[32:64], fx[32:64, 1, :].unsqueeze(1).to_broadcast([32, HB, T]),
                                ident[32:64, 32:32 + HB].unsqueeze(2).to_broadcast([32, HB, T]), ALU.mult))
                    own.settle()
                    dve.sem_inc(s_fm, 1)
                elif kind == "s":
                    nm = smallB[:, 2 * (i % 2):2 * (i % 2) + 2]
                    z = smallB[:, 4 + 2 * (i % 2):6 + 2 * (i % 2)]
                    B.filled(dve, *job)
                    diagonal = ps[:, b, P:3 * P].rearrange("p (a b) -> p a b", b=P)
                    own(tt(diagonal, diagonal, cmask.unsqueeze(1).to_broadcast([P, 2, P]), ALU.add))
                    own.mark(dve.tensor_reduce(nm[:, 0:1], ps[:, b, 0:T], AX, ALU.max))
                    own(dve.tensor_reduce(nm[:, 1:2], ps[:, b, T:3 * P], AX, ALU.max))
                    own(ts(nm, nm, -DH ** -0.5, None, ALU.mult))
                    dve.sem_inc(s_nm, 1)
                    for tap, c in taps[16 * i:16 * i + 16]:
                        src = pad[:, c, tap:tap + T]
                        w = col("conv_w_2", c * TAPS2 + tap)
                        if tap == 0:
                            own.mark(ts(conv[:, c, :], src, w, col("conv_b_2", c), ALU.mult, ALU.add))
                        else:
                            own.mark(stt(conv[:, c, :], src, w, conv[:, c, :], ALU.mult, ALU.add))
                        if c == KC - 1:
                            own.settle()
                    if i == HB - 1:
                        dve.sem_inc(s_conv, 1)
                    dve.wait_ge(s_exp, HA + i + 1)
                    own(dve.reciprocal(z, z))
                    for t, keys in ((0, slice(0, T)), (1, slice(T, 3 * P))):
                        own.mark(ts(pB[i % 2][:, keys], pB[i % 2][:, keys], z[:, t:t + 1], None, ALU.mult))
                    own.settle()
                    dve.sem_inc(s_diff, 1)
                elif kind == "dT":
                    B.filled(dve, *job)
                    if i >= 2:
                        B.filled(dve, "o", i - 2)
                    own(dve.tensor_copy(pTB[i % 2], ps[:, b, 0:3 * P]))
                    dve.sem_inc(free[b], 1)
                    dve.sem_inc(s_dT, 1)
                elif kind == "mean":
                    B.filled(dve, *job)
                    own(ts(meanB, ps[:, b, 0:T], 1.0 / CW, None, ALU.mult))
                    dve.sem_inc(free[b], 1)
                    own(tt(conv, conv, meanB.unsqueeze(1).to_broadcast([P, KC, T]), ALU.subtract))
                    dve.sem_inc(s_cen, 1)
                elif kind == "var":
                    dve.wait_ge(s_croot, 1)
                    dve.wait_ge(s_csq, 1)
                    own(dve.reciprocal(invB, invB))
                    own(tt(conv, conv, invB.unsqueeze(1).to_broadcast([P, KC, T]), ALU.mult))
                    dve.sem_inc(s_cn, 1)
                elif kind in ("bra", "brc"):
                    if i == 0:
                        dve.wait_ge(s_gate, KD + KD)
                    g = 2 * i + (KD if kind == "bra" else 0)
                    dst = mixed[:, 2 * i:2 * i + 2, :]
                    B.filled(dve, *job)
                    if kind == "bra":
                        own(tt(dst, pair, gates[:, g:g + 2, :], ALU.mult))
                        dve.sem_inc(free[b], 1)
                    else:
                        own(tt(sigB[:, 0:2, :], pair, gates[:, g:g + 2, :], ALU.mult))
                        dve.sem_inc(free[b], 1)
                        own(tt(dst, dst, sigB[:, 0:2, :], ALU.add))
                        dve.sem_inc(s_mrg, 1)
                elif kind == "wo":
                    B.filled(dve, *job)
                    for j in range(2):
                        c = 2 * i + j
                        own.mark(stt(xT[:, c, :], ps[:, b, j * T:(j + 1) * T], mod[:, 2 * KD + c:2 * KD + c + 1],
                                     xT[:, c, :], ALU.mult, ALU.add))
                    own.settle()
                    dve.sem_inc(free[b], 1)
                    dve.sem_inc(s_x1, 1)
                    if i == 3:
                        for s in range(RING):
                            dve.wait_ge(r_free[s], len([n for n in range(len(units)) if n % RING == s]))
                        own(tt(g2_diag, ident.unsqueeze(1).to_broadcast([P, KD, P]),
                               mod[:, 5 * KD:6 * KD].unsqueeze(2).to_broadcast([P, KD, P]), ALU.mult))
                        dve.sem_inc(s_g2d, 1)
                elif kind == "route":
                    B.filled(dve, *job)
                    own.mark(dve.memset(logits[:, E:E + 4], 3e38))
                    own(tt(logits[:, 0:E], ps[:, b, 0:E], b_route, ALU.add))
                    dve.sem_inc(free[b], 1)
                    own(dve.max(m8, logits))
                    own(dve.match_replace(logits_r, m8, logits, -3e38))
                    own(ts(smallM[:, 0:1], m8[:, 4:5], -1.0, None, ALU.mult))
                    dve.sem_inc(s_rmax, 1)
                    dve.wait_ge(s_rexp, i + 1)
                    own(tt(logits_r[:, 0:E], logits_r[:, 0:E], logits[:, 0:E], ALU.not_equal))
                    own(tt(chosen, chosen, logits_r[:, 0:E], ALU.mult))
                    own(dve.tensor_reduce(smallM[:, 1:2], chosen, AX, ALU.add))
                    own(dve.reciprocal(smallM[:, 1:2], smallM[:, 1:2]))
                    own(ts(gate_rows[:, i, :], chosen, smallM[:, 1:2], None, ALU.mult))
                    dve.sem_inc(s_gr, 1)
                    if i == TT - 1:
                        own(ts(picked, gate_rows, 0.0, None, ALU.is_gt))
                        dve.sem_inc(s_pick, 1)
                elif kind == "rank":
                    B.filled(dve, *job)
                    dve.wait_ge(s_poolM, 1)
                    first = slot_of[:, :, 0:E]
                    rank = ps[:, b, 0:2 * E].rearrange("p (a b) -> p a b", b=E)
                    own(stt(first, rank, 1.0, picked, ALU.add, ALU.mult))
                    own(ts(first, first, -1.0, None, ALU.add))
                    own.mark(ts(slot_of[:, :, E:2 * E], first, -float(P), None, ALU.add))
                    own.mark(dve.tensor_copy(gate_of[:, :, 0:E], gate_rows))
                    own.mark(dve.tensor_copy(gate_of[:, :, E:2 * E], gate_rows))
                    own(dve.tensor_reduce(smallM[:, 4:5], ps[:, b, 2 * E:3 * E], AX, ALU.max))
                    dve.sem_inc(free[b], 1)
                    own(ts(smallM[:, 5:6], smallM[:, 4:5], P + 0.5, 1.0, ALU.is_gt, ALU.add))
                    own(dve.tensor_copy(passes_i[:, 0:1].bitcast(mybir.dt.int32), smallM[:, 5:6]))
                    dve.sem_inc(s_slots, 1)
                    select(sel, 0, False)
                    dve.sem_inc(s_sel, 1)
                elif kind == "gT":
                    B.filled(dve, *job)
                    own(dve.tensor_copy(gT[0:E, :], ps[0:E, b, 0:T]))
                    dve.sem_inc(free[b], 1)
                    dve.sem_inc(s_gT, 1)

            passes = dve.value_load(passes_i[0:1, 0:1].bitcast(mybir.dt.int32), min_val=1, max_val=2)
            with dve.Fori(0, passes) as p:
                with dve.Fori(0, E) as e:
                    q = p * E + e
                    own.enter(q, 4 + 12)
                    dve.wait_ge(s_xg, q * 2 + 2)
                    select(sel, q + 1, False)
                    dve.sem_inc(s_sel, 1)
                    dve.wait_ge(s_selgT, q + 1)
                    select(selg, q, True)
                    dve.sem_inc(s_selg, 1)
                    dve.wait_ge(s_yg, q * 2 + 1)
                    for n in range(2):
                        g, u, sg = g_act[n], u_act[n], sg_act[n]
                        for part, dst, job in ((0, g, f"Tg{n}"), (1, u, f"Tu{n}")):
                            bank = EXPERT_BANK[job]
                            bias = b1[:, bass.ds(e, 1), part * KD + 4 * n:part * KD + 4 * n + 4]
                            X.filled(dve, q, job)
                            own(tt(dst, ps[:, bank, :].rearrange("p (a b) -> p a b", b=P),
                                   bias.rearrange("p e c -> p (e c)").unsqueeze(2).to_broadcast([P, 4, P]), ALU.add))
                            dve.sem_inc(x_free[bank - 4], 1)
                            if part == 0:
                                own(ts(g, g, LIMIT, None, ALU.min))
                                dve.sem_inc(s_g, 1)
                        own(ts(u, u, LIMIT, -LIMIT, ALU.min, ALU.max))
                        own(stt(u, u, 1.0, g, ALU.add, ALU.mult))
                        dve.wait_ge(s_sg, q * 2 + n + 1)
                        own(tt(hm[:, 4 * n:4 * n + 4, :], u, sg, ALU.mult))
                        dve.sem_inc(s_hm, 1)
                    own.leave_open()
            end = Own(dve, s_vend)

            dve.wait_ge(s_fin, 1)
            dve.wait_ge(s_row, 16)
            for t in range(TT):
                for half in range(2):
                    h = slice(half * 512, (half + 1) * 512)
                    end(tt(y_rows[:, t, h], ps[:, 2 * t + half, :], g2_row[:, h], ALU.mult))
                end(tt(y_rows[:, t, :], y_rows[:, t, :], x3_rows[:, t, :], ALU.add))
                end(dve.tensor_tensor_reduce(x3_rows[:, t, :], y_rows[:, t, :], y_rows[:, t, :], 1.0, 0.0, ALU.mult,
                                             ALU.add, smallM[:, 2 + t:3 + t]))
            dve.sem_inc(s_y, 1)
            dve.wait_ge(s_yroot, 1)
            end(dve.reciprocal(smallM[:, 2:4], smallM[:, 2:4]))
            for t in range(TT):
                stt(y_rows[:, t, :], y_rows[:, t, :], smallM[:, 2 + t:3 + t], final_row, ALU.mult, ALU.mult)\
                    .then_inc(s_yn, 1)


def _units(w, columns):
    k, n = w.shape
    return np.ascontiguousarray(w.reshape(k // P, P, n // columns, columns).transpose(2, 1, 0, 3)).reshape(
        n // columns, P, k // P * columns)


def _chunks(v):
    return v.reshape(-1, P).T


def _layout(i):
    a = {}
    a["xT"] = np.ascontiguousarray(i["x"][0].T.reshape(KD, P, T).transpose(1, 0, 2))
    w_in = i["w_in"][0]
    a["w_in"] = _units(w_in, 512)
    a["w_br_rnn"] = _units(i["w_br_rnn"][0], 256)
    for name in ("w_br_attn", "w_out", "w_peer_q"):
        a[name] = _units(i[name][0], 512)
    a["sub_keys"] = np.ascontiguousarray(i["peer_sub_keys"][0].reshape(2 * PH, PK, P).transpose(2, 0, 1)).reshape(
        1, P, 2 * PH * PK)
    a["w_ada"] = np.ascontiguousarray(i["w_ada_2"][0].T.reshape(12, 4, P, D).transpose(0, 2, 1, 3)).reshape(
        12, P, 4 * D)
    a["peer_u"], a["peer_v"] = i["peer_u"][0], i["peer_v"][0]
    w = i["w_in_2"][0]
    a["w_in_2"] = np.concatenate([_units(w[:, 0:2560], 512), _units(w[:, 2568:], 512)])
    w_f = np.zeros((P, KD, DH), np.float32)
    for s in (0, 32):
        w_f[:, :, s:s + HB] = w[:, 2560:2568].reshape(KD, P, HB).transpose(1, 0, 2)
    a["w_f"] = w_f
    a["w_router"] = np.ascontiguousarray(i["w_router_2"][0].reshape(KD, P, E).transpose(1, 0, 2))
    a["w_attn_out_2"] = _units(i["w_attn_out_2"][0], D)
    a["w_conv_out_2"] = _units(i["w_conv_out_2"][0], D)
    a["w_out_2"] = _units(i["w_out_2"][0], 512)
    a["b_router"] = i["b_router_2"][0]
    a["b_exp_in"] = np.ascontiguousarray(i["b_exp_in_2"][0].reshape(E, 2 * KD, P).transpose(2, 0, 1))
    a["b_exp_out"] = i["b_exp_out_2"][0]
    a["final_g"] = i["final_g_2"]
    a["w_exp"] = w_exp = np.empty((E, 6, P, SLOT), np.float32)
    up = i["w_exp_in_2"][0].reshape(E, KD, P, 2, 2, 512)
    w_exp[:, 0:4] = up.transpose(0, 4, 3, 2, 1, 5).reshape(E, 4, P, SLOT)
    w_exp[:, 4:6] = i["w_exp_out_2"][0].reshape(E, 2, 4, P, D).transpose(0, 1, 3, 2, 4).reshape(E, 2, P, SLOT)
    gates = np.zeros((P, 2, CR, P), np.float32)
    for g, name in enumerate(("w_rg_a", "w_rg_x")):
        w = i[name][0].reshape(CR, 2, DH, DH)
        for s in range(2):
            gates[s * DH:(s + 1) * DH, g, :, s * DH:(s + 1) * DH] = w[:, s].transpose(1, 0, 2)
    a["w_rg"] = gates
    for name in ("lambda_q1", "lambda_k1", "lambda_q2", "lambda_k2"):
        a[name] = i[name][0]
    a["c_2"] = i["c_2"][0]
    cols = np.zeros((P, N_COLS), np.float32)

    def put(name, v):
        s, n = COLS[name]
        cols[0:v.shape[0], s:s + n] = v

    for name, key in (("norm1_g", "norm1_g"), ("b_gate", "b_gate"), ("conv_b", "conv_b"), ("b_rg_a", "b_rg_a"),
                      ("b_rg_x", "b_rg_x"), ("rg_lambda", "rg_lambda"), ("norm2_g", "norm2_g"), ("b_ada", "b_ada_2"),
                      ("norm1_g_2", "norm1_g_2"), ("conv_b_2", "conv_b_2"), ("conv_ln_g", "conv_ln_g_2"),
                      ("conv_ln_b", "conv_ln_b_2"), ("norm2_g_2", "norm2_g_2"), ("subln_g", "subln_g")):
        put(name, _chunks(i[key][0]))
    for name in ("q_norm_g", "k_norm_g"):
        put(name, np.concatenate([i[name][0], i[name][0]])[:, None])
    put("conv_w", i["conv_w"][0].reshape(TAPS1, CR, P).transpose(2, 1, 0).reshape(P, CR * TAPS1))
    put("conv_w_2", i["conv_w_2"][0].reshape(TAPS2, KC, P).transpose(2, 1, 0).reshape(P, KC * TAPS2))
    put("b_forget", i["b_forget_2"][0][:, None])
    cols[32:32 + HB, COLS["b_forget"][0]] = i["b_forget_2"][0]
    a["cols"] = cols
    return a


def kernel(**inputs):
    import concourse.bacc as bacc
    from concourse.bass_utils import run_bass_kernel_spmd

    nc = bacc.Bacc("TRN2", target_bir_lowering=False, num_devices=1)
    arrays, aps = {}, {}
    for name, v in _layout(inputs).items():
        arrays[f"in_{name}"] = v
        aps[name] = nc.dram_tensor(f"in_{name}", v.shape, F32, kind="ExternalInput").ap()
    out = nc.dram_tensor("out", (T, D), F32, kind="ExternalOutput").ap()
    build_program(nc, aps, out)
    r = run_bass_kernel_spmd(nc, [arrays], core_ids=[0])
    return r.results[0]["out"].reshape(1, T, D)
```

```python
from contextlib import ExitStack

import numpy as np

import concourse.bass as bass
from concourse import mybir

F32 = mybir.dt.float32
U32 = mybir.dt.uint32
ALU = mybir.AluOpType
ACT = mybir.ActivationFunctionType
AX = mybir.AxisListType.X

P = 128
T = 256
TT = T // P
D = 1024
KD = D // P
EPS1 = 1e-6
EPS2 = 1e-5
NEG = -1e30
LAM_INIT = 0.2

HA, DH = 8, 64
DR = 1280
CR = DR // P
TAPS1 = 4
PH, PK, TOPK = 8, 128, 16
N_EXPERTS_PEER = PK * PK
HB = 8
CW = 512
KC = CW // P
TAPS2 = 31
E, FE = 32, 1024
LIMIT, ALPHA = 7.0, 1.702

SLOT = 4096
RING = 5
N_BANKS = 8

COLS = {}


def _column(name, n):
    start = sum(c for _, c in COLS.values())
    COLS[name] = (start, n)


for _name, _n in (("norm1_g", KD), ("b_gate", 2 * KD), ("q_norm_g", 1), ("k_norm_g", 1), ("subln_g", 1),
                  ("conv_w", CR * TAPS1), ("conv_b", CR), ("b_rg_a", CR), ("b_rg_x", CR), ("rg_lambda", CR),
                  ("norm2_g", KD), ("b_ada", 6 * KD), ("norm1_g_2", KD), ("conv_w_2", KC * TAPS2),
                  ("conv_b_2", KC), ("conv_ln_g", KC), ("conv_ln_b", KC), ("norm2_g_2", KD), ("b_forget", 1)):
    _column(_name, _n)
N_COLS = sum(c for _, c in COLS.values())



def plan_first():
    s = [("ss1",)]
    late = []
    projections = ([("xr", i) for i in range(CR // 2)] + [("yr", 0)] + [("q", i) for i in range(4)]
                   + [("k", i) for i in range(4)] + [("v", i) for i in range(4)])
    for n, p in enumerate(projections):
        s.append(p)
        for when, steps in [x for x in late if x[0] <= n]:
            s.extend(steps)
        late = [x for x in late if x[0] > n]
        if p[0] == "xr":
            late.append((n + 2, [("rg", 2 * p[1]), ("rg", 2 * p[1] + 1)]))
        if p[0] in "qk":
            late.append((n + 1, [("ss" + p[0], p[1])]))
    assert not late
    slots = [("yr", i) for i in range(1, 5)] + [("gate", i) for i in range(KD)]
    for n, p in enumerate(slots):
        s.append(p)
        if 3 <= n < HA + 3:
            s.append(("osum", n - 3))
        if 2 <= n < HA + 2:
            s.append(("o", n - 2))
        if 1 <= n < HA + 1:
            s.append(("dT", n - 1))
        if n < HA:
            s += [("s0", n), ("s1", n)]
    s += [("brr", i) for i in range(4)] + [("bra", i) for i in range(4)] + [("wo", i) for i in range(4)]
    s.append(("ss2",))
    s += [("h2r", i) for i in range(4)]
    for i in range(PH // 2):
        s.append(("pq", 2 * i))
        if i >= 1:
            s += [("key", i - 1), ("key", i + 3)]
        s.append(("pq", 2 * i + 1))
    s += [("key", 3), ("key", 7)]
    return s


def plan_second():
    s = [("x2T", i) for i in range(4)] + [("ss3",)]
    s += [("ug", i) for i in range(2)] + [("uv", i) for i in range(2)] + [("f",)]
    s += [("q", i) for i in range(2)] + [("k", i) for i in range(2)] + [("v", i) for i in range(2)]
    for n in range(KD):
        s.append(("gate", n))
        if n >= 2:
            s.append(("o", n - 2))
        if n >= 1:
            s.append(("dT", n - 1))
        s.append(("s", n))
    s += [("o", HB - 2), ("dT", HB - 1), ("mean",), ("o", HB - 1), ("var",)]
    s += [("bra", i) for i in range(4)] + [("brc", i) for i in range(4)] + [("wo", i) for i in range(4)]
    s.append(("ss4",))
    s += [("route", i) for i in range(TT)]
    s += [("x3r", i) for i in range(4)] + [("g2r", i) for i in range(2)]
    s += [("h3r", i) for i in range(4)] + [("rank",), ("gT",), ("xg", 0), ("xg", 1)]
    return s


EXPERT_JOBS = (("Zg", 4), ("Zu", 5), ("Tg", 6), ("G0", 7), ("Tu", 4), ("G1", 5), ("S", 6), ("D", 7))
EXPERT_BANK = dict(EXPERT_JOBS)
NS = 64
MAX_PASSES = E + T * 4 // NS


class ExpertJobs:

    def __init__(self, full, free):
        self.full, self.free = full, free
        self.uses = {b: [j for j, x in EXPERT_JOBS if x == b] for b in (4, 5, 6, 7)}

    def claim(self, pe, q, job):
        b = EXPERT_BANK[job]
        pe.wait_ge(self.free[b - 4], q * len(self.uses[b]) + self.uses[b].index(job) + 1)

    def filled(self, eng, q, job):
        b = EXPERT_BANK[job]
        eng.wait_ge(self.full[b - 4], q * len(self.uses[b]) + self.uses[b].index(job) + 1)


def plan_units():
    w = lambda i: ("w_in", i, SLOT)
    ada = lambda i: ("w_ada", i, SLOT)
    first = [w(6), w(7), w(8), ada(0), w(0), ada(1), w(1), ada(2), w(2), ada(3), w(3), ada(4), w(4), ada(5),
             w(5), ada(6), w(9), ada(7), w(10), ada(8), w(11), ada(9), w(12), ada(10), w(13), ada(11), w(14)]
    first += [("w_br_rnn", i, CR * 256) for i in range(4)] + [("w_br_attn", i, SLOT) for i in range(2)]
    first += [("w_out", i, SLOT) for i in range(2)] + [("w_peer_q", 0, SLOT), ("sub_keys", 0, 2 * PH * PK)]
    first += [("w_peer_q", i, SLOT) for i in range(1, 4)]
    second = [("w_in_2", i, SLOT) for i in (1, 0, 2, 3, 4, 5, 6, 7, 8)]
    second += [("w_attn_out_2", 0, SLOT), ("w_conv_out_2", 0, SLOT)] + [("w_out_2", i, SLOT) for i in range(2)]
    return first, second


class Jobs:

    def __init__(self, plan, full, free, before=None):
        self.number = {step: n for n, step in enumerate(plan)}
        self.full, self.free = full, free
        self.base = [before.base[b] + before.jobs(b) if before else 0 for b in range(N_BANKS)]

    def jobs(self, b):
        return sum(n % N_BANKS == b for n in self.number.values())

    def bank(self, *job):
        return self.number[job] % N_BANKS

    def claim(self, pe, *job):
        n = self.number[job]
        if n >= N_BANKS:
            pe.wait_ge(self.free[n % N_BANKS], self.base[n % N_BANKS] + n // N_BANKS)

    def filled(self, eng, *job):
        n = self.number[job]
        eng.wait_ge(self.full[n % N_BANKS], self.base[n % N_BANKS] + n // N_BANKS + 1)

    def all_free(self, eng):
        for b in range(N_BANKS):
            eng.wait_ge(self.free[b], self.base[b] + self.jobs(b))


class Own:

    def __init__(self, eng, sem):
        self.eng, self.sem, self.n, self.loop = eng, sem, 0, None

    def mark(self, ins):
        ins.then_inc(self.sem, 1)
        self.n += 1

    def settle(self):
        self.eng.wait_ge(self.sem, self.n if self.loop is None else self.loop + self.n)

    def __call__(self, ins):
        self.mark(ins)
        self.settle()

    def settle_apart(self):
        if self.loop is None:
            self.settle()
        else:
            self.mark(self.eng.wait_ge(self.sem, self.loop + self.n))

    def enter(self, i, per):
        self.start, self.per = self.n, per
        self.loop = i * per

    def leave_open(self):
        assert self.n - self.start == self.per, (self.n - self.start, self.per)
        self.loop = None

    def leave(self, count):
        assert self.n - self.start == self.per, (self.n - self.start, self.per)
        self.n, self.loop = self.start + self.per * count, None


def build_program(nc, a, out):
    first_units, second_units = plan_units()
    units = first_units + second_units
    unit_at = {(name, i): n for n, (name, i, _) in enumerate(units)}
    n_first = len(first_units)
    assert n_first % RING == 0

    with ExitStack() as ctx:
        def sem(name):
            return ctx.enter_context(nc.semaphore(name))

        ring = ctx.enter_context(nc.sbuf_tensor("ring", [P, 6 * SLOT], F32))
        arena_words = 27400
        arena = ctx.enter_context(nc.sbuf_tensor("arena", [P, arena_words], F32))
        ps = ctx.enter_context(nc.psum_tensor("ps", [P, N_BANKS, 512], F32))
        at = {"fixed": 0}

        def carve(region, *shape):
            n = int(np.prod(shape))
            start = at[region]
            at[region] = start + n
            assert at[region] <= arena_words, (region, at[region])
            v = arena[:, start:start + n]
            if len(shape) == 2:
                v = v.rearrange("p (a b) -> p a b", b=shape[1])
            if len(shape) == 3:
                v = v.rearrange("p (a b c) -> p a b c", b=shape[1], c=shape[2])
            return v

        ident = carve("fixed", P)
        ones = carve("fixed", P)
        cols = carve("fixed", N_COLS)
        eps = carve("fixed", 2)
        xT = carve("fixed", KD, T)
        hT = carve("fixed", KD, T)
        rstd = carve("fixed", T)
        mod = carve("fixed", 6 * KD)
        scale1, scale2 = carve("fixed", KD), carve("fixed", KD)
        iota_i, iota16 = carve("fixed", TOPK), carve("fixed", TOPK)

        def col(name, i=0, n=1):
            s = COLS[name][0] + i
            return cols[:, s:s + n]

        at["A"] = at["fixed"]
        qT = carve("A", KD, T)
        kT = carve("A", KD, T)
        v_rows = carve("A", TT, D)
        rnnT = carve("A", CR, T)
        w_gates = carve("A", 2, CR, P)
        c_row = carve("A", D)
        xr = [carve("A", 2, T + TAPS1 - 1) for _ in range(2)]
        xc = [carve("A", 2, T) for _ in range(3)]
        ri = carve("A", 2, 2, T)
        decay, e_w, poly, gelu_y = (carve("A", 2, T) for _ in range(4))
        blocks = carve("A", P)
        probs = [carve("A", 2, 3 * P) for _ in range(2)]
        dT = [carve("A", 3 * P) for _ in range(2)]
        sq = carve("A", 2, T)
        inv = carve("A", 2, T)
        osq = carve("A", T)
        oinv = carve("A", T)
        lams = carve("A", 4, DH)
        small = carve("A", 40)
        sp = carve("A", 6, CR)
        x_sq = rnnT
        gates = ring[:, 5 * SLOT:6 * SLOT].rearrange("p (a b) -> p a b", b=T)

        at["P"] = at["fixed"]
        h2_rows = carve("P", TT, D)
        qpT = carve("P", 2 * PH, T)
        n_pairs = TT * PH // 2
        all_scores = carve("P", (n_pairs + 1) * 4, PK)
        pair_scores = carve("P", 4, PK)
        scores = all_scores[:, 0:4 * n_pairs, :].rearrange("p (t r) k -> p t r k", t=TT)
        top, top_i, top_f = (carve("P", 4, TOPK) for _ in range(3))
        cand = carve("P", 2, TOPK * TOPK)
        hot = carve("P", 2 * TOPK, TOPK)
        top_s, pos = carve("P", 2, TOPK), carve("P", 2, TOPK)
        half_pos, half_f = carve("P", 2, TOPK), carve("P", 2, TOPK)
        i1_of, i2_of = carve("P", 2, TOPK), carve("P", 2, TOPK)
        soft = carve("P", 4)
        route_idx = carve("P", 2, TOPK)
        route_g = carve("P", 2, TOPK)
        idx_now = carve("P", 2, TOPK)
        dots = carve("P", 2, TOPK)
        wts = carve("P", 2, TOPK)
        x2_rows = h2_rows
        diag = qpT.rearrange("p (g k) t -> p g k t", g=2).rearrange("p g k t -> p g (k t)").rearrange(
            "p g (k t) -> p g k t", t=P)
        u_rows = [ring[:, i * D:(i + 1) * D] for i in (0, 1, 2, 3, 20, 21, 22, 23)]
        v_gath = [ring[:, (4 + i) * D:(5 + i) * D] for i in range(16)]

        at["B"] = at["fixed"] + TT * D
        qz = carve("B", HB, T)
        kv = carve("B", KD, T)
        kB = kv[:, 0:KC, :]
        vB = kv[:, KC:KD, :].rearrange("p (a b) t -> p a (b t)", a=TT)
        attnB = carve("B", KC, T)
        pad = carve("B", KC, T + TAPS2 - 1)
        conv = carve("B", KC, T)
        sigB = carve("B", KC, T)
        sqB = carve("B", KC, T)
        mixed = carve("B", KD, T)
        pB = [carve("B", 3 * P) for _ in range(2)]
        pTB = [carve("B", 3 * P) for _ in range(2)]
        cmask = carve("B", P)
        w_f = carve("B", KD, DH)
        fx = carve("B", 4, T)
        f_right = carve("B", T)
        f_left = carve("B", HB, T)
        smallB = carve("B", 24)
        meanB, invB = carve("B", T), carve("B", T)
        xsqB = kv
        kept = arena_words - (KD * E + E + E * 2 * KD + D)
        assert at["B"] <= kept, (at["B"], kept)
        at["K"] = kept
        w_r = carve("K", KD, E)
        b_route = carve("K", E)
        b1 = carve("K", E, 2 * KD)
        b2 = carve("K", D)

        at["M"] = at["fixed"]
        h3_rows = carve("M", TT, D)
        x3_rows = carve("M", TT, D)
        xg = carve("M", KD, P)
        z_sb = carve("M", 2, 512)
        hm = carve("M", 4, P)
        yg = carve("M", 512)
        g_act, u_act, sg_act = carve("M", 4, P), carve("M", 4, P), carve("M", 4, P)
        bias_now = carve("M", 2 * KD)
        sel = carve("M", TT, P)
        selg = carve("M", TT, P)
        selgT = carve("M", T)
        g2_row = carve("M", D)
        final_row = carve("M", D)
        slot_of = carve("M", TT, E)
        before = carve("M", P)
        slots4 = carve("M", 4 * P)
        slots4_i = carve("M", 4 * P)
        n_pass = carve("M", 4, E)
        table = carve("M", 3, MAX_PASSES + 1)
        of_pass = carve("M", MAX_PASSES + 1, E)
        logits = carve("M", E + 4)
        logits_r = carve("M", E + 4)
        m8 = carve("M", 8)
        chosen = carve("M", E)
        gate_rows = carve("M", TT, E)
        picked = carve("M", TT, E)
        gT = carve("M", T)
        smallM = carve("M", 8)
        total_i = carve("M", 2)
        expert_of = carve("M", MAX_PASSES + 1)
        part_of = carve("M", MAX_PASSES + 1)
        last_of = carve("M", E)
        hit = carve("M", MAX_PASSES + 1, E)
        assert at["M"] <= at["B"]
        g2_diag = carve("B", KD, P)
        assert at["B"] <= kept, (at["B"], kept)
        y_rows = ring[:, 0:TT * D].rearrange("p (a b) -> p a b", b=D)
        I32 = mybir.dt.int32
        w1_unit = [ring[:, n * SLOT:(n + 1) * SLOT].rearrange("p (c j) -> p c j", c=KD) for n in range(4)]
        w2_unit = [ring[:, n * SLOT:(n + 1) * SLOT].rearrange("p (c j) -> p c j", j=D) for n in (4, 5)]

        s_par = sem("params_loaded")
        s_x, s_cols = sem("x_loaded"), sem("columns_loaded")
        s_const, s_iota = sem("constants_ready"), sem("iota_ready")
        full = [sem(f"bank_full_{b}") for b in range(N_BANKS)]
        free = [sem(f"bank_free_{b}") for b in range(N_BANKS)]
        r_full = [sem(f"unit_loaded_{b}") for b in range(RING)]
        r_free = [sem(f"unit_used_{b}") for b in range(RING)]
        s_vend = sem("vector_own_end")
        s_v, s_a, s_p = sem("vector_own"), sem("scalar_own"), sem("pool_own")
        A = Jobs(plan_first(), full, free)
        B = Jobs(plan_second(), full, free, before=A)

        def unit(name, i):
            n = unit_at[(name, i)]
            s = n % RING
            return ring[:, s * SLOT:s * SLOT + units[n][2]]

        def unit_loaded(eng, name, i):
            n = unit_at[(name, i)]
            eng.wait_ge(r_full[n % RING], 16 * (n // RING + 1))

        def unit_used(name, i):
            return r_free[unit_at[(name, i)] % RING]

        s_sq = sem("squares_ready")
        s_root = sem("root_ready")
        s_h = sem("h_ready")
        s_xr = sem("xr_ready")
        s_xc = sem("xc_ready")
        s_ri = sem("rnn_gates_ready")
        s_rnn_free = sem("rnn_gates_used")
        s_dec = sem("decay_exponent_ready")
        s_expw = sem("decay_ready")
        s_poly = sem("mult_squared_ready")
        s_mult = sem("mult_ready")
        s_gel = sem("gelu_y_ready")
        s_gel_free = sem("rnn_pair_done")
        s_qsq = sem("qk_squares_ready")
        s_qroot = sem("qk_root_ready")
        s_qroot_free = sem("qk_ready")
        s_vr = sem("v_rows_ready")
        s_gate = sem("branch_gates_ready")
        s_nm = sem("negative_max_ready")
        s_exp = sem("exponentials_ready")
        s_diff = sem("probabilities_ready")
        s_dT = sem("transposed_probs_ready")
        s_osq = sem("head_squares_ready")
        s_oroot = sem("head_root_ready")
        s_o = sem("head_output_ready")
        s_mrg = sem("merged_ready")
        s_x1 = sem("residual_ready")
        s_silu = sem("silu_c_ready")
        s_sp = sem("lambda_exp_ready")
        s_spw = sem("lambda_in_ready")
        s_h2r = sem("h2_rows_ready")
        s_pq = sem("peer_queries_ready")
        s_ps = sem("peer_scores_ready")
        s_out = sem("output_stored")
        s_soft_in = sem("peer_top_ready")
        s_soft = sem("peer_exp_ready")
        s_route = sem("peer_routes_ready")
        s_taken = sem("peer_routes_taken")
        s_dot = sem("u_rows_used")
        s_dots = sem("dots_ready")
        s_act = sem("gelu_dots_ready")
        s_wts = sem("expert_weights_ready")
        s_diag = sem("diagonals_ready")
        s_pv = sem("v_rows_used")
        u_full = [sem(f"u_row_loaded_{k}") for k in range(8)]
        v_full = [sem(f"v_row_loaded_{k}") for k in range(16)]
        s_x2r = sem("x2_rows_ready")
        s_x2 = sem("x2_ready")
        s_smallw = sem("small_weights_loaded")
        s_poolB = sem("second_constants_ready")
        s_sig = sem("glu_gate_ready")
        s_fe, s_fl, s_fm = sem("forget_exp_in"), sem("forget_log_ready"), sem("forget_matrices_ready")
        s_qkv = sem("qkv_ready")
        s_conv, s_cen, s_csq = sem("conv_ready"), sem("centred_ready"), sem("centred_squares_ready")
        s_croot, s_cn, s_silu2 = sem("conv_root_ready"), sem("conv_normed_ready"), sem("conv_silu_ready")
        s_rmax, s_rexp, s_gr = sem("router_max_ready"), sem("router_exp_ready"), sem("gate_rows_ready")
        s_x3r, s_h3r = sem("x3_rows_ready"), sem("h3_rows_ready")
        s_pick, s_slots, s_gT = sem("picked_ready"), sem("slots_ready"), sem("gates_transposed")
        s_poolM = sem("expert_constants_ready")
        s_g2d = sem("g2_diagonals_ready")
        w_full = [sem(f"expert_unit_loaded_{n}") for n in range(6)]
        x_full = [sem(f"expert_bank_full_{b}") for b in range(4, 8)]
        x_free = [sem(f"expert_bank_free_{b}") for b in range(4, 8)]
        X = ExpertJobs(x_full, x_free)
        s_sel = sem("selection_ready")
        s_selg = sem("gated_selection_ready")
        s_selgT = sem("gated_selection_transposed")
        s_xg = sem("expert_tokens_ready")
        s_zc = sem("z_copied")
        s_g, s_sg = sem("expert_gate_ready"), sem("expert_sigmoid_ready")
        s_hm = sem("expert_hidden_ready")
        s_yg = sem("expert_rows_ready")
        s_fin = sem("experts_done")
        s_y, s_yroot, s_yn = sem("y_ready"), sem("y_root_ready"), sem("y_normed")
        s_row = sem("rows_loaded")

        block = ctx.enter_context(nc.Block())

        @block.sync
        def _(sp):
            sp.dma_start(xT, a["xT"]).then_inc(s_x, 16)
            sp.dma_start(cols, a["cols"]).then_inc(s_cols, 16)
            sp.dma_start(w_gates, a["w_rg"]).then_inc(s_par, 16)
            for i, name in enumerate(("lambda_q1", "lambda_k1", "lambda_q2", "lambda_k2")):
                sp.dma_start(lams[:, i, :], a[name].partition_broadcast(P)).then_inc(s_par, 16)
            sp.dma_start(c_row, a["c_2"].partition_broadcast(P)).then_inc(s_par, 16)
            for n, (name, i, words) in enumerate(units[:n_first]):
                if n >= RING:
                    sp.wait_ge(r_free[n % RING], n // RING)
                sp.dma_start(unit(name, i), a[name][i]).then_inc(r_full[n % RING], 16)
            for n in range(n_first, len(units)):
                name, i, words = units[n]
                if n == n_first:
                    sp.wait_ge(s_dot, 8 + TT * PH * TOPK)
                elif n < n_first + RING:
                    sp.wait_ge(s_pv, 17 + TT * PH * TOPK - 4 * (RING - 1 - n % RING))
                else:
                    sp.wait_ge(r_free[n % RING], n // RING)
                if n == n_first + RING - 1:
                    for small_name, dst in (("w_f", w_f), ("w_router", w_r), ("b_exp_in", b1)):
                        sp.dma_start(dst, a[small_name]).then_inc(s_smallw, 16)
                    sp.dma_start(b_route, a["b_router"].partition_broadcast(P)).then_inc(s_smallw, 16)
                sp.dma_start(unit(name, i), a[name][i]).then_inc(r_full[n % RING], 16)
                if n == n_first + RING - 1:
                    sp.wait_ge(s_poolB, 1)
                    sp.dma_start(b2[0:E, :], a["b_exp_out"]).then_inc(s_smallw, 16)
            def load(e, n):
                sp.dma_start(ring[:, n * SLOT:(n + 1) * SLOT],
                             a["w_exp"][bass.ds(e, 1), n].rearrange("e p w -> (e p) w")).then_inc(w_full[n], 16)

            n_second = len(units)
            for n in sorted(range(RING), key=lambda slot: max(m for m in range(n_second) if m % RING == slot)):
                if n == (n_second - 2) % RING:
                    sp.wait_ge(s_mrg, 4 + 4)
                    load(0, 5)
                sp.wait_ge(r_free[n], len([m for m in range(n_second) if m % RING == n]))
                load(0, n)
            sp.wait_ge(s_slots, 1)
            sp.dma_start(final_row, a["final_g"].partition_broadcast(P)).then_inc(s_row, 16)
            with sp.Fori(1, E) as e:
                q = sp.value_load(last_of[0:1, bass.ds(e - 1, 1)].bitcast(I32), min_val=0, max_val=MAX_PASSES - 1)
                for job, ns in (("Zg", (0, 1)), ("Zu", (2, 3)), ("D", (4, 5))):
                    X.filled(sp, q, job)
                    for n in ns:
                        load(e, n)
            sp.wait_ge(s_yn, TT)
            sp.dma_start(out.rearrange("(a p) d -> p a d", p=P), y_rows).then_inc(s_out, 16)
            sp.wait_ge(s_out, 16)

        @block.gpsimd
        def _(pool):
            own = Own(pool, s_p)
            own.mark(pool.memset(ident, 0.0))
            own.mark(pool.memset(blocks, 0.0))
            own.mark(pool.memset(ones, 1.0))
            own.mark(pool.memset(eps[:, 0:1], EPS1))
            own.mark(pool.memset(eps[:, 1:2], EPS2))
            own.settle()
            own(pool.affine_select(out=ident, in_=ident, compare_op=ALU.not_equal, fill=1.0, base=0,
                                   pattern=[[-1, P]], channel_multiplier=1))
            own(pool.memset(blocks[0:DH, 0:DH], 1.0))
            own(pool.memset(blocks[DH:P, DH:P], 1.0))
            for i in range(2):
                own.mark(pool.memset(xr[i][:, :, 0:TAPS1 - 1], 0.0))
            own.settle()
            pool.sem_inc(s_const, 1)
            own(pool.iota(iota_i.bitcast(mybir.dt.int32), pattern=[[1, TOPK]], base=0, channel_multiplier=0))
            own(pool.tensor_copy(iota16, iota_i.bitcast(mybir.dt.int32)))
            pool.sem_inc(s_iota, 1)

            first_in = [len([n for n in range(n_first) if n % RING == s]) for s in range(RING)]
            pool.wait_ge(r_free[0], first_in[0])
            pool.wait_ge(s_mrg, 4)
            for tile in range(TT):
                per = 2 * (2 + 2 * TOPK)
                with pool.Fori(0, PH // 2) as i:
                    own.enter(i, per)
                    for par in range(2):
                        g = tile * PH + par
                        pool.wait_ge(s_pv, i * (2 * TOPK) + TOPK * g + 1)
                        own.mark(pool.wait_ge(s_route, i + tile * PH // 2 + 1))
                        own(pool.tensor_copy(idx_now[:, par, :].bitcast(U32), route_idx[:, par, :].bitcast(U32)))
                        pool.sem_inc(s_taken, 1)
                        for k in range(TOPK):
                            own.mark(pool.wait_ge(s_dot, i * (2 * TOPK) + TOPK * g + k + 1))
                            pool.indirect_dma_start(
                                out=u_rows[k % 8], out_offset=None, in_=a["peer_u"],
                                in_offset=bass.IndirectOffsetOnAxis(ap=idx_now[:, par, k:k + 1].bitcast(U32), axis=0)
                            ).then_inc(u_full[k % 8], 16)
                        for s in range(1, RING):
                            pool.wait_ge(r_free[s], first_in[s])
                        for k in range(TOPK):
                            own.mark(pool.wait_ge(s_pv, i * (2 * TOPK) + TOPK * g + k + 2))
                            pool.indirect_dma_start(
                                out=v_gath[k], out_offset=None, in_=a["peer_v"],
                                in_offset=bass.IndirectOffsetOnAxis(ap=idx_now[:, par, k:k + 1].bitcast(U32), axis=0)
                            ).then_inc(v_full[k], 16)
                own.leave(PH // 2)

            pool.wait_ge(s_dot, 8 + TT * PH * TOPK)
            pool.wait_ge(s_pv, 17 + TT * PH * TOPK)
            for dst in (qz, f_left, pad[:, :, 0:TAPS2 - 1], b2, cmask):
                own.mark(pool.memset(dst, 0.0))
            own.mark(pool.memset(f_right, 1.0))
            own.settle()
            own(pool.affine_select(out=cmask, in_=cmask, compare_op=ALU.is_ge, fill=NEG, base=0,
                                   pattern=[[-1, P]], channel_multiplier=1))
            pool.sem_inc(s_poolB, 1)
            pool.wait_ge(s_x1, 4 + 4)
            own.mark(pool.memset(before, 1.0))
            own.mark(pool.memset(selgT, 0.0))
            own.mark(pool.memset(yg, 0.0))
            own.mark(pool.memset(gT, 0.0))
            own.mark(pool.iota(slots4_i.bitcast(I32), pattern=[[NS, 4], [0, 2], [1, NS]], base=0,
                               channel_multiplier=0))
            own.mark(pool.iota(of_pass.bitcast(I32), pattern=[[1, MAX_PASSES + 1], [0, E]], base=0,
                               channel_multiplier=0))
            own.settle()
            own(pool.affine_select(out=before, in_=before, compare_op=ALU.is_gt, fill=0.0, base=0,
                                   pattern=[[1, P]], channel_multiplier=-1))
            own(pool.tensor_copy(slots4, slots4_i.bitcast(I32)))
            own(pool.tensor_copy(of_pass, of_pass.bitcast(I32)))
            pool.sem_inc(s_poolM, 1)

        @block.tensor
        def _(pe):
            def mm(o, l, r, start, stop):
                return pe.matmul(o, l, r, start=start, stop=stop)

            def project(J, job, b, w, m, src, nk, half):
                for c in range(nk):
                    last = mm(ps[:, b, half * T:(half + 1) * T], w[:, c, m * P:(m + 1) * P], src[:, c, :],
                              c == 0, c == nk - 1)
                return last

            pe.sem_inc(s_pv, 17)
            pe.wait_ge(s_const, 1)
            inc = None
            seen = {}
            for job in plan_first():
                kind, i = job[0], job[1] if len(job) > 1 else 0
                b = A.bank(*job)
                seen[kind] = seen.get(kind, 0) + 1
                if kind in ("xr", "yr", "q", "k", "gate"):
                    first = {"q": 0, "k": 8, "xr": 24, "yr": 34, "gate": 44}[kind] + 2 * i
                    u = first // 4
                    w = unit("w_in", u).rearrange("p (c n) -> p c n", c=KD)
                    unit_loaded(pe, "w_in", u)
                    if kind == "xr" and i == 0:
                        pe.wait_ge(s_h, KD)
                    A.claim(pe, *job)
                    project(A, job, b, w, first % 4, hT, KD, 0)
                    last = project(A, job, b, w, first % 4 + 1, hT, KD, 1)
                    last.then_inc(full[b], 1)
                    if first % 4 == 2:
                        pe.wait_ge(full[b], A.number[job] // N_BANKS + 1).then_inc(unit_used("w_in", u), 1)
                elif kind == "v":
                    u = 4 + i // 2
                    w = unit("w_in", u).rearrange("p (c n) -> p c n", c=KD)
                    unit_loaded(pe, "w_in", u)
                    A.claim(pe, *job)
                    for c in range(KD):
                        last = mm(ps[:, b, :], hT[:, c, (i % 2) * P:(i % 2 + 1) * P], w[:, c, :], c == 0, c == KD - 1)
                    last.then_inc(full[b], 1)
                    if i % 2 == 1:
                        pe.wait_ge(full[b], A.number[job] // N_BANKS + 1).then_inc(unit_used("w_in", u), 1)
                elif kind in ("ss1", "ss2"):
                    pe.wait_ge(s_sq, 1 if kind == "ss1" else 2)
                    A.claim(pe, *job)
                    for c in range(KD):
                        last = mm(ps[:, b, 0:T], ones, x_sq[:, c, :], c == 0, c == KD - 1)
                    last.then_inc(full[b], 1)
                elif kind == "rg":
                    if i % 2 == 0:
                        pe.wait_ge(s_xc, i // 2 + 1)
                    if i == 0:
                        pe.wait_ge(s_par, 16 * 6)
                    A.claim(pe, *job)
                    for g in range(2):
                        last = mm(ps[:, b, g * T:(g + 1) * T], w_gates[:, g, i, :], xc[i // 2 % 3][:, i % 2, :],
                                  True, True)
                    last.then_inc(full[b], 1)
                elif kind in ("ssq", "ssk"):
                    n = i + (4 if kind == "ssk" else 0)
                    pe.wait_ge(s_qsq, n + 1)
                    A.claim(pe, *job)
                    mm(ps[:, b, :], blocks, sq.rearrange("p a b -> p (a b)"), True, True).then_inc(full[b], 1)
                elif kind in ("s0", "s1"):
                    if i == 0:
                        pe.wait_ge(s_qroot_free, 8)
                    A.claim(pe, *job)
                    h = slice(0, DH) if kind == "s0" else slice(DH, P)
                    mm(ps[:, b, 0:T], qT[h, i, P:T], kT[h, i, :], True, True)
                    mm(ps[:, b, T:3 * P], qT[h, i, 0:P], kT[h, i, 0:P], True, True).then_inc(full[b], 1)
                elif kind == "dT":
                    pe.wait_ge(s_diff, i + 1)
                    A.claim(pe, *job)
                    pe.transpose(ps[:, b, 0:P], probs[i % 2][:, 0, T:3 * P], ident)
                    pe.transpose(ps[:, b, P:2 * P], probs[i % 2][:, 0, 0:P], ident)
                    pe.transpose(ps[:, b, 2 * P:3 * P], probs[i % 2][:, 0, P:T], ident).then_inc(full[b], 1)
                elif kind == "o":
                    pe.wait_ge(s_dT, i + 1)
                    if i == 0:
                        pe.wait_ge(s_vr, 4)
                    A.claim(pe, *job)
                    mm(ps[:, b, 0:T], v_rows[:, 0, i * P:(i + 1) * P], dT[i % 2][:, 0:T], True, False)
                    mm(ps[:, b, P:T], v_rows[:, 1, i * P:(i + 1) * P], dT[i % 2][:, T:3 * P], False, True)\
                        .then_inc(full[b], 1)
                elif kind == "osum":
                    pe.wait_ge(s_osq, i + 1)
                    A.claim(pe, *job)
                    mm(ps[:, b, 0:T], ones, osq, True, True).then_inc(full[b], 1)
                elif kind == "brr":
                    if i == 0:
                        pe.wait_ge(s_gel_free, CR // 2)
                    unit_loaded(pe, "w_br_rnn", i)
                    w = unit("w_br_rnn", i).rearrange("p (c n) -> p c n", c=CR)
                    A.claim(pe, *job)
                    project(A, job, b, w, 0, rnnT, CR, 0)
                    project(A, job, b, w, 1, rnnT, CR, 1).then_inc(full[b], 1)
                    pe.wait_ge(full[b], A.number[job] // N_BANKS + 1).then_inc(unit_used("w_br_rnn", i), 1)
                elif kind in ("bra", "wo"):
                    name, src = ("w_br_attn", qT) if kind == "bra" else ("w_out", kT)
                    if i == 0:
                        if kind == "bra":
                            pe.wait_ge(s_o, HA)
                        else:
                            pe.wait_ge(s_mrg, 4)
                    unit_loaded(pe, name, i // 2)
                    w = unit(name, i // 2).rearrange("p (c n) -> p c n", c=KD)
                    A.claim(pe, *job)
                    project(A, job, b, w, 2 * (i % 2), src, KD, 0)
                    project(A, job, b, w, 2 * (i % 2) + 1, src, KD, 1).then_inc(full[b], 1)
                    if i % 2 == 1:
                        pe.wait_ge(full[b], A.number[job] // N_BANKS + 1).then_inc(unit_used(name, i // 2), 1)
                elif kind == "h2r":
                    if i == 0:
                        pe.wait_ge(s_h, 2 * KD)
                    A.claim(pe, *job)
                    for j in range(4):
                        last = pe.transpose(ps[:, b, j * P:(j + 1) * P],
                                            hT[:, 4 * (i % 2) + j, (i // 2) * P:(i // 2 + 1) * P], ident)
                    last.then_inc(full[b], 1)
                elif kind == "pq":
                    unit_loaded(pe, "w_peer_q", i // 2)
                    w = unit("w_peer_q", i // 2).rearrange("p (c n) -> p c n", c=KD)
                    A.claim(pe, *job)
                    project(A, job, b, w, 2 * (i % 2), hT, KD, 0)
                    project(A, job, b, w, 2 * (i % 2) + 1, hT, KD, 1).then_inc(full[b], 1)
                    if i % 2 == 1:
                        pe.wait_ge(full[b], A.number[job] // N_BANKS + 1).then_inc(unit_used("w_peer_q", i // 2), 1)
                elif kind == "key":
                    if i == 0:
                        unit_loaded(pe, "sub_keys", 0)
                    pe.wait_ge(s_pq, 2 * (i % 4) + 2)
                    A.claim(pe, *job)
                    keys = unit("sub_keys", 0).rearrange("p (c n) -> p c n", n=PK)
                    for j in range(4):
                        hc = 4 * (i % 4) + j
                        last = mm(ps[:, b, j * PK:(j + 1) * PK], qpT[:, hc, (i // 4) * P:(i // 4 + 1) * P],
                                  keys[:, hc, :], True, True)
                    last.then_inc(full[b], 1)
                    if i == 7:
                        pe.wait_ge(full[b], A.number[job] // N_BANKS + 1).then_inc(unit_used("sub_keys", 0), 1)
                else:
                    raise ValueError(job)

            def add(o, l, r, start=False):
                return pe.matmul(o, l, r, start=start, stop=False, skip_group_check=True)

            A.all_free(pe)
            for tile in range(TT):
                for c in range(KD):
                    add(ps[:, 2 * tile + c // 4, (c % 4) * P:(c % 4 + 1) * P], xT[:, c, tile * P:(tile + 1) * P],
                        ident, start=(c % 4 == 0))
                with pe.Fori(0, PH // 2) as i:
                    for par in range(2):
                        g = tile * PH + par
                        pe.wait_ge(s_diag, i * 2 + g + 1)
                        for k in range(TOPK):
                            pe.wait_ge(v_full[k], i * 32 + 16 * (g + 1))
                            add(ps[:, 2 * tile, :], diag[:, par, k, :], v_gath[k][:, 0:512])
                            add(ps[:, 2 * tile + 1, :], diag[:, par, k, :], v_gath[k][:, 512:D]).then_inc(s_pv, 1)

            def gather(b, half):
                for j in range(4):
                    c = 4 * half + j
                    for t in range(TT):
                        last = mm(ps[:, b, j * P:(j + 1) * P], h3_rows[:, t, c * P:(c + 1) * P], sel[:, t, :],
                                  t == 0, t == TT - 1)
                return last

            for job in plan_second():
                kind, i = job[0], job[1] if len(job) > 1 else 0
                b = B.bank(*job)

                def release(name, u):
                    pe.wait_ge(full[b], B.base[b] + B.number[job] // N_BANKS + 1).then_inc(unit_used(name, u), 1)

                if kind == "x2T":
                    if i == 0:
                        pe.wait_ge(s_x2r, TT)
                    B.claim(pe, *job)
                    for j in range(2):
                        for t in range(TT):
                            last = pe.transpose(ps[:, b, j * T + t * P:j * T + (t + 1) * P],
                                                x2_rows[:, t, (2 * i + j) * P:(2 * i + j + 1) * P], ident)
                    last.then_inc(full[b], 1)
                elif kind in ("ss3", "ss4"):
                    pe.wait_ge(s_sq, 3 if kind == "ss3" else 4)
                    B.claim(pe, *job)
                    for c in range(KD):
                        last = mm(ps[:, b, 0:T], ones, xsqB[:, c, :], c == 0, c == KD - 1)
                    last.then_inc(full[b], 1)
                elif kind in ("ug", "uv", "q", "k", "gate"):
                    u = {"ug": 1, "uv": 0, "q": 2, "k": 3, "gate": 5}[kind] + i // 2
                    w = unit("w_in_2", u).rearrange("p (c n) -> p c n", c=KD)
                    unit_loaded(pe, "w_in_2", u)
                    if kind == "ug" and i == 0:
                        pe.wait_ge(s_h, 2 * KD + 1)
                    B.claim(pe, *job)
                    project(B, job, b, w, 2 * (i % 2), hT, KD, 0)
                    project(B, job, b, w, 2 * (i % 2) + 1, hT, KD, 1).then_inc(full[b], 1)
                    if i % 2 == 1:
                        release("w_in_2", u)
                elif kind == "v":
                    w = unit("w_in_2", 4).rearrange("p (c n) -> p c n", c=KD)
                    unit_loaded(pe, "w_in_2", 4)
                    B.claim(pe, *job)
                    for c in range(KD):
                        last = mm(ps[:, b, :], hT[:, c, i * P:(i + 1) * P], w[:, c, :], c == 0, c == KD - 1)
                    last.then_inc(full[b], 1)
                    if i == 1:
                        release("w_in_2", 4)
                elif kind == "f":
                    pe.wait_ge(s_smallw, 16 * 5)
                    B.claim(pe, *job)
                    for c in range(KD):
                        last = mm(ps[0:DH, b, 0:T], w_f[:, c, :], hT[:, c, :], c == 0, c == KD - 1)
                    last.then_inc(full[b], 1)
                elif kind == "s":
                    if i == 0:
                        pe.wait_ge(s_qkv, 6)
                        pe.wait_ge(s_fm, 1)
                    B.claim(pe, *job)
                    mm(ps[:, b, 0:T], qz[:, i, P:T], kB[:, i // 2, :], True, False)
                    mm(ps[:, b, 0:T], f_left[:, i, P:T], f_right, False, True)
                    mm(ps[:, b, T:3 * P], qz[:, i, 0:P], kB[:, i // 2, 0:P], True, False)
                    mm(ps[:, b, T:3 * P], f_left[:, i, 0:P], f_right[:, 0:P], False, True).then_inc(full[b], 1)
                elif kind == "dT":
                    pe.wait_ge(s_diff, HA + i + 1)
                    B.claim(pe, *job)
                    pe.transpose(ps[:, b, 0:P], pB[i % 2][:, T:3 * P], ident)
                    pe.transpose(ps[:, b, P:2 * P], pB[i % 2][:, 0:P], ident)
                    pe.transpose(ps[:, b, 2 * P:3 * P], pB[i % 2][:, P:T], ident).then_inc(full[b], 1)
                elif kind == "o":
                    pe.wait_ge(s_dT, HA + i + 1)
                    B.claim(pe, *job)
                    c = slice(i // 2 * P, (i // 2 + 1) * P)
                    mm(ps[:, b, 0:T], vB[:, 0, c], pTB[i % 2][:, 0:T], True, False)
                    mm(ps[:, b, P:T], vB[:, 1, c], pTB[i % 2][:, T:3 * P], False, True).then_inc(full[b], 1)
                elif kind in ("mean", "var"):
                    if kind == "mean":
                        pe.wait_ge(s_conv, 1)
                    else:
                        pe.wait_ge(s_csq, 1)
                    B.claim(pe, *job)
                    for c in range(KC):
                        last = mm(ps[:, b, 0:T], ones, (conv if kind == "mean" else sqB)[:, c, :], c == 0, c == KC - 1)
                    last.then_inc(full[b], 1)
                elif kind in ("bra", "brc"):
                    name, src = ("w_attn_out_2", attnB) if kind == "bra" else ("w_conv_out_2", conv)
                    unit_loaded(pe, name, 0)
                    if i == 0:
                        if kind == "bra":
                            pe.wait_ge(s_o, HA + HB)
                        else:
                            pe.wait_ge(s_silu2, 1)
                    w = unit(name, 0).rearrange("p (c n) -> p c n", c=KC)
                    B.claim(pe, *job)
                    project(B, job, b, w, 2 * i, src, KC, 0)
                    project(B, job, b, w, 2 * i + 1, src, KC, 1).then_inc(full[b], 1)
                    if i == 3:
                        release(name, 0)
                elif kind == "wo":
                    if i == 0:
                        pe.wait_ge(s_mrg, 4 + 4)
                    unit_loaded(pe, "w_out_2", i // 2)
                    w = unit("w_out_2", i // 2).rearrange("p (c n) -> p c n", c=KD)
                    B.claim(pe, *job)
                    project(B, job, b, w, 2 * (i % 2), mixed, KD, 0)
                    project(B, job, b, w, 2 * (i % 2) + 1, mixed, KD, 1).then_inc(full[b], 1)
                    if i % 2 == 1:
                        release("w_out_2", i // 2)
                elif kind == "route":
                    if i == 0:
                        pe.wait_ge(s_h, 2 * KD + 2)
                    B.claim(pe, *job)
                    for c in range(KD):
                        last = mm(ps[:, b, 0:E], hT[:, c, i * P:(i + 1) * P], w_r[:, c, :], c == 0, c == KD - 1)
                    last.then_inc(full[b], 1)
                elif kind == "gT":
                    pe.wait_ge(s_gr, TT)
                    B.claim(pe, *job)
                    for t in range(TT):
                        last = pe.transpose(ps[0:E, b, t * P:(t + 1) * P], gate_rows[:, t, :], ident)
                    last.then_inc(full[b], 1)
                elif kind == "rank":
                    pe.wait_ge(s_pick, 1)
                    pe.wait_ge(s_poolM, 1)
                    B.claim(pe, *job)
                    mm(ps[:, b, 0:E], before, picked[:, 0, :], True, True)
                    mm(ps[:, b, E:2 * E], before, picked[:, 1, :], True, False)
                    mm(ps[:, b, E:2 * E], ones, picked[:, 0, :], False, True)
                    mm(ps[:, b, 2 * E:3 * E], ones, picked[:, 0, :], True, False)
                    mm(ps[:, b, 2 * E:3 * E], ones, picked[:, 1, :], False, True).then_inc(full[b], 1)
                elif kind == "xg":
                    if i == 0:
                        pe.wait_ge(s_sel, 1)
                        pe.wait_ge(s_h3r, 4)
                    B.claim(pe, *job)
                    gather(b, i).then_inc(full[b], 1)
                elif kind == "h3r":
                    B.claim(pe, *job)
                    for j in range(4):
                        last = pe.transpose(ps[:, b, j * P:(j + 1) * P],
                                            hT[:, 4 * (i % 2) + j, (i // 2) * P:(i // 2 + 1) * P], ident)
                    last.then_inc(full[b], 1)
                elif kind == "x3r":
                    B.claim(pe, *job)
                    for j in range(4):
                        last = pe.transpose(ps[:, b, j * P:(j + 1) * P],
                                            xT[:, 4 * (i % 2) + j, (i // 2) * P:(i // 2 + 1) * P], ident)
                    last.then_inc(full[b], 1)
                elif kind == "g2r":
                    if i == 0:
                        pe.wait_ge(s_g2d, 1)
                    B.claim(pe, *job)
                    mm(ps[:, b, :], ones, g2_diag[:, 4 * i:4 * i + 4, :].rearrange("p c j -> p (c j)"),
                       True, True).then_inc(full[b], 1)
                else:
                    raise ValueError(job)

            B.all_free(pe)
            pe.wait_ge(s_gT, 1)
            for t in range(TT):
                for half in range(2):
                    add(ps[:, 2 * t + half, :], gT[:, t * P:(t + 1) * P], b2[:, half * 512:(half + 1) * 512],
                        start=True)
            for b in range(4):
                pe.sem_inc(x_free[b], 1)
            pe.sem_inc(s_selgT, 1)
            pe.sem_inc(s_yg, 1)

            def filled_by(ins, job):
                ins.then_inc(x_full[EXPERT_BANK[job] - 4], 1)

            def hidden(q, e, n, job):
                for half in range(2):
                    pe.wait_ge(w_full[2 * n + half], e * 16 + 16)
                X.claim(pe, q, job)
                for c in range(KD):
                    for half in range(2):
                        last = mm(ps[half * NS:(half + 1) * NS, EXPERT_BANK[job], :], xg[:, c, 0:NS],
                                  w1_unit[2 * n + half][:, c, :], c == 0, c == KD - 1)
                filled_by(last, job)

            def turn(q, n, job):
                pe.wait_ge(s_zc, q * 2 + n + 1)
                X.claim(pe, q, job)
                for j in range(4):
                    last = pe.transpose(ps[:, EXPERT_BANK[job], j * P:(j + 1) * P], z_sb[:, n, j * P:(j + 1) * P],
                                        ident)
                filled_by(last, job)

            def combine(q):
                pe.wait_ge(s_yg, q + 1)
                pe.wait_ge(s_selgT, q + 1)
                for t in range(TT):
                    for half in range(2):
                        h = slice(half * NS, (half + 1) * NS)
                        last = add(ps[:, 2 * t + half, :], selgT[h, t * P:(t + 1) * P], yg[h, :])
                return last

            pe.wait_ge(s_slots, 1)
            total = pe.value_load(total_i[0:1, 0:1].bitcast(I32), min_val=E, max_val=MAX_PASSES)
            with pe.Fori(0, total) as q:
                e = pe.value_load(expert_of[0:1, bass.ds(q, 1)].bitcast(I32), min_val=0, max_val=E - 1)
                pe.wait_ge(s_xg, q * 2 + 2)
                hidden(q, e, 0, "Zg")
                hidden(q, e, 1, "Zu")
                turn(q, 0, "Tg")
                pe.wait_ge(s_sel, q + 2)
                X.claim(pe, q, "G0")
                filled_by(gather(EXPERT_BANK["G0"], 0), "G0")
                turn(q, 1, "Tu")
                X.claim(pe, q, "G1")
                filled_by(gather(EXPERT_BANK["G1"], 1), "G1")
                combine(q)
                pe.wait_ge(s_selg, q + 1)
                X.claim(pe, q, "S")
                pe.transpose(ps[:, EXPERT_BANK["S"], 0:P], selg[:, 0, :], ident)
                filled_by(pe.transpose(ps[:, EXPERT_BANK["S"], P:T], selg[:, 1, :], ident), "S")
                X.claim(pe, q, "D")
                pe.wait_ge(s_hm, q + 1)
                for k in range(KD):
                    if k % 4 == 0:
                        pe.wait_ge(w_full[4 + k // 4], e * 16 + 16)
                    for half in range(2):
                        last = mm(ps[half * NS:(half + 1) * NS, EXPERT_BANK["D"], :],
                                  hm[:, k % 4, (k // 4) * NS:(k // 4 + 1) * NS],
                                  w2_unit[k // 4][:, k % 4, half * 512:(half + 1) * 512], k == 0, k == KD - 1)
                filled_by(last, "D")
            combine(total).then_inc(s_fin, 1)

        @block.scalar
        def _(act):
            own = Own(act, s_a)
            fn = act.activation
            act.wait_ge(s_x, 16)
            fn(x_sq[:, 0:KD, :], xT, ACT.Square).then_inc(s_sq, 1)
            act.wait_ge(s_const, 1)
            for job in plan_first():
                kind, i = job[0], job[1] if len(job) > 1 else 0
                b = A.bank(*job)
                bank = ps[:, b, :]
                pair = bank.rearrange("p (a b) -> p a b", b=T)
                if kind in ("ss1", "ss2"):
                    A.filled(act, *job)
                    own(fn(rstd, ps[:, b, 0:T], ACT.Sqrt, bias=eps[:, 0:1], scale=1.0 / D))
                    act.sem_inc(free[b], 1)
                    act.sem_inc(s_root, 1)
                    if kind == "ss1":
                        act.wait_ge(s_par, 16 * 6)
                        fn(c_row, c_row, ACT.Silu).then_inc(s_silu, 1)
                        act.wait_ge(s_spw, 1)
                        fn(sp[:, 1, :], sp[:, 0, :], ACT.Exp)
                        fn(small[:, 2:4], small[:, 0:2], ACT.Exp).then_inc(s_sp, 1)
                elif kind == "xr":
                    A.filled(act, *job)
                    if i >= 2:
                        act.wait_ge(s_xc, i - 1)
                    own(act.copy(xr[i % 2][:, :, TAPS1 - 1:], pair))
                    act.sem_inc(free[b], 1)
                    act.sem_inc(s_xr, 1)
                elif kind == "rg":
                    A.filled(act, *job)
                    if i % 2 == 0 and i >= 2:
                        act.wait_ge(s_rnn_free, i // 2)
                    own.mark(fn(ri[:, 0, i % 2, :], ps[:, b, 0:T], ACT.Sigmoid, bias=col("b_rg_a", i)))
                    own(fn(ri[:, 1, i % 2, :], ps[:, b, T:2 * T], ACT.Sigmoid, bias=col("b_rg_x", i)))
                    act.sem_inc(free[b], 1)
                    if i % 2 == 1:
                        act.sem_inc(s_ri, 1)
                        act.wait_ge(s_dec, i // 2 + 1)
                        fn(e_w, decay, ACT.Exp, scale=-0.5).then_inc(s_expw, 1)
                        act.wait_ge(s_poly, i // 2 + 1)
                        fn(poly, poly, ACT.Sqrt).then_inc(s_mult, 1)
                elif kind == "yr":
                    A.filled(act, *job)
                    if i >= 1:
                        act.wait_ge(s_gel_free, i)
                    own(fn(gelu_y, pair, ACT.Gelu_apprx_tanh))
                    act.sem_inc(free[b], 1)
                    act.sem_inc(s_gel, 1)
                elif kind in ("q", "k"):
                    A.filled(act, *job)
                    n = i + (4 if kind == "k" else 0)
                    if n >= 1:
                        A.filled(act, "ssq" if n - 1 < 4 else "ssk", (n - 1) % 4)
                    fn(sq, pair, ACT.Square).then_inc(s_qsq, 1)
                elif kind in ("ssq", "ssk"):
                    A.filled(act, *job)
                    n = i + (4 if kind == "ssk" else 0)
                    if n >= 1:
                        act.wait_ge(s_qroot_free, n)
                    own(fn(inv, pair, ACT.Sqrt, bias=eps[:, 0:1], scale=1.0 / DH))
                    act.sem_inc(free[b], 1)
                    act.sem_inc(s_qroot, 1)
                elif kind == "v":
                    A.filled(act, *job)
                    own(act.copy(v_rows[:, i % 2, (i // 2) * 512:(i // 2 + 1) * 512], bank))
                    act.sem_inc(free[b], 1)
                    act.sem_inc(s_vr, 1)
                elif kind == "gate":
                    A.filled(act, *job)
                    own.mark(fn(gates[:, 2 * i, :], ps[:, b, 0:T], ACT.Sigmoid, bias=col("b_gate", 2 * i)))
                    own(fn(gates[:, 2 * i + 1, :], ps[:, b, T:2 * T], ACT.Sigmoid, bias=col("b_gate", 2 * i + 1)))
                    act.sem_inc(free[b], 1)
                    act.sem_inc(s_gate, 1)
                elif kind == "s1":
                    act.wait_ge(s_nm, i + 1)
                    if i >= 2:
                        A.filled(act, "dT", i - 2)
                    nm = small[:, 8 + 8 * (i % 2):12 + 8 * (i % 2)]
                    z = small[:, 12 + 8 * (i % 2):16 + 8 * (i % 2)]
                    b0 = A.bank("s0", i)
                    for c, bc in ((0, b0), (1, b)):
                        for t, keys in ((0, slice(0, T)), (1, slice(T, 3 * P))):
                            own.mark(fn(probs[i % 2][:, c, keys], ps[:, bc, keys], ACT.Exp,
                                        bias=nm[:, 2 * t + c:2 * t + c + 1], scale=DH ** -0.5,
                                        accum_out=z[:, 2 * t + c:2 * t + c + 1]))
                    own.settle()
                    act.sem_inc(free[b], 1)
                    act.sem_inc(free[b0], 1)
                    act.sem_inc(s_exp, 1)
                elif kind == "o":
                    A.filled(act, *job)
                    if i >= 1:
                        A.filled(act, "osum", i - 1)
                    fn(osq, ps[:, b, 0:T], ACT.Square).then_inc(s_osq, 1)
                elif kind == "osum":
                    A.filled(act, *job)
                    if i >= 1:
                        act.wait_ge(s_o, i)
                    own(fn(oinv, ps[:, b, 0:T], ACT.Sqrt, bias=eps[:, 0:1], scale=1.0 / P))
                    act.sem_inc(free[b], 1)
                    act.sem_inc(s_oroot, 1)
                elif kind == "wo":
                    if i == 3:
                        act.wait_ge(s_x1, 4)
                        fn(x_sq[:, 0:KD, :], xT, ACT.Square).then_inc(s_sq, 1)
                elif kind == "h2r":
                    A.filled(act, *job)
                    own(act.copy(h2_rows[:, i // 2, (i % 2) * 512:(i % 2 + 1) * 512], bank))
                    act.sem_inc(free[b], 1)
                    act.sem_inc(s_h2r, 1)
                elif kind == "pq":
                    A.filled(act, *job)
                    own(act.copy(qpT[:, 2 * i:2 * i + 2, :], pair))
                    act.sem_inc(free[b], 1)
                    act.sem_inc(s_pq, 1)
                elif kind == "key":
                    A.filled(act, *job)
                    own(act.copy(scores[:, i // 4, 4 * (i % 4):4 * (i % 4) + 4, :],
                                 bank.rearrange("p (a b) -> p a b", b=PK)))
                    act.sem_inc(free[b], 1)
                    act.sem_inc(s_ps, 1)
                    if i == 5:
                        act.wait_ge(s_soft_in, 1)
                        fn(top_s, top_s, ACT.Exp).then_inc(s_soft, 1)
            for tile in range(TT):
                with act.Fori(0, PH // 2) as i:
                    for par in range(2):
                        g = tile * PH + par
                        act.wait_ge(s_dots, i * 2 + g + 1)
                        fn(dots[:, par, :], dots[:, par, :], ACT.Gelu_apprx_tanh).then_inc(s_act, 1)
                        act.wait_ge(s_wts, i * 2 + g + 1)
                        act.wait_ge(s_pv, i * (2 * TOPK) + TOPK * g + 1)
                        for k in range(TOPK):
                            last = fn(diag[:, par, k, :], ident, ACT.Copy, scale=wts[:, par, k:k + 1])
                        last.then_inc(s_diag, 1)
                    act.wait_ge(s_soft_in, i + tile * PH // 2 + 2)
                    fn(top_s, top_s, ACT.Exp).then_inc(s_soft, 1)
                act.wait_ge(s_pv, 17 + (tile + 1) * PH * TOPK)
                for half in range(2):
                    last = act.copy(x2_rows[:, tile, half * 512:(half + 1) * 512], ps[:, 2 * tile + half, :])
                last.then_inc(s_x2r, 1)

            for job in plan_second():
                kind, i = job[0], job[1] if len(job) > 1 else 0
                b = B.bank(*job)
                bank = ps[:, b, :]
                pair = bank.rearrange("p (a b) -> p a b", b=T)
                if kind == "x2T":
                    B.filled(act, *job)
                    own(act.copy(xT[:, 2 * i:2 * i + 2, :], pair))
                    act.sem_inc(free[b], 1)
                    act.sem_inc(s_x2, 1)
                    if i == 3:
                        fn(xsqB, xT, ACT.Square).then_inc(s_sq, 1)
                elif kind in ("ss3", "ss4"):
                    B.filled(act, *job)
                    own(fn(rstd, ps[:, b, 0:T], ACT.Sqrt, bias=eps[:, 1:2], scale=1.0 / D))
                    act.sem_inc(free[b], 1)
                    act.sem_inc(s_root, 1)
                elif kind == "ug":
                    B.filled(act, *job)
                    own(fn(sigB[:, 2 * i:2 * i + 2, :], pair, ACT.Sigmoid))
                    act.sem_inc(free[b], 1)
                    act.sem_inc(s_sig, 1)
                elif kind == "f":
                    act.wait_ge(s_fe, 1)
                    own(fn(fx[0:DH, 2, :], fx[0:DH, 1, :], ACT.Exp))
                    own(fn(fx[0:DH, 2, :], fx[0:DH, 2, :], ACT.Ln, bias=1.0))
                    act.sem_inc(s_fl, 1)
                elif kind == "q":
                    B.filled(act, *job)
                    if i == 0:
                        act.wait_ge(s_poolB, 1)
                    z4 = qz.rearrange("p (c s) t -> p c s t", s=2)
                    own.mark(act.copy(z4[0:DH, 2 * i:2 * i + 2, 0, :], pair[0:DH]))
                    own(act.copy(z4[DH:P, 2 * i:2 * i + 2, 1, :], pair[DH:P]))
                    act.sem_inc(free[b], 1)
                    act.sem_inc(s_qkv, 1)
                elif kind == "k":
                    B.filled(act, *job)
                    own(act.copy(kB[:, 2 * i:2 * i + 2, :], pair))
                    act.sem_inc(free[b], 1)
                    act.sem_inc(s_qkv, 1)
                elif kind == "v":
                    B.filled(act, *job)
                    own(act.copy(vB[:, i, :], bank))
                    act.sem_inc(free[b], 1)
                    act.sem_inc(s_qkv, 1)
                elif kind == "gate":
                    B.filled(act, *job)
                    own(fn(gates[:, 2 * i:2 * i + 2, :], pair, ACT.Sigmoid))
                    act.sem_inc(free[b], 1)
                    act.sem_inc(s_gate, 1)
                elif kind == "s":
                    act.wait_ge(s_nm, HA + i + 1)
                    if i >= 2:
                        B.filled(act, "dT", i - 2)
                    nm = smallB[:, 2 * (i % 2):2 * (i % 2) + 2]
                    z = smallB[:, 4 + 2 * (i % 2):6 + 2 * (i % 2)]
                    for t, keys in ((0, slice(0, T)), (1, slice(T, 3 * P))):
                        own.mark(fn(pB[i % 2][:, keys], ps[:, b, keys], ACT.Exp, bias=nm[:, t:t + 1],
                                    scale=DH ** -0.5, accum_out=z[:, t:t + 1]))
                    own.settle()
                    act.sem_inc(free[b], 1)
                    act.sem_inc(s_exp, 1)
                elif kind == "o":
                    B.filled(act, *job)
                    h = slice(0, DH) if i % 2 == 0 else slice(DH, P)
                    own(act.copy(attnB[h, i // 2, :], ps[h, b, 0:T]))
                    act.sem_inc(free[b], 1)
                    act.sem_inc(s_o, 1)
                elif kind == "mean":
                    act.wait_ge(s_cen, 1)
                    fn(sqB, conv, ACT.Square).then_inc(s_csq, 1)
                elif kind == "var":
                    B.filled(act, *job)
                    own(fn(invB, ps[:, b, 0:T], ACT.Sqrt, bias=eps[:, 1:2], scale=1.0 / CW))
                    act.sem_inc(free[b], 1)
                    act.sem_inc(s_croot, 1)
                    act.wait_ge(s_cn, 1)
                    for c in range(KC):
                        last = fn(conv[:, c, :], conv[:, c, :], ACT.Silu, bias=col("conv_ln_b", c),
                                  scale=col("conv_ln_g", c))
                    last.then_inc(s_silu2, 1)
                elif kind == "wo" and i == 3:
                    act.wait_ge(s_x1, 4 + 4)
                    fn(xsqB, xT, ACT.Square).then_inc(s_sq, 1)
                elif kind == "route":
                    act.wait_ge(s_rmax, i + 1)
                    fn(chosen, logits[:, 0:E], ACT.Exp, bias=smallM[:, 0:1]).then_inc(s_rexp, 1)
                elif kind == "xg":
                    B.filled(act, *job)
                    own(act.copy(xg[:, 4 * i:4 * i + 4, :], bank.rearrange("p (a b) -> p a b", b=P)))
                    act.sem_inc(free[b], 1)
                    act.sem_inc(s_xg, 1)
                elif kind == "h3r":
                    B.filled(act, *job)
                    own(act.copy(h3_rows[:, i // 2, (i % 2) * 512:(i % 2 + 1) * 512], bank))
                    act.sem_inc(free[b], 1)
                    act.sem_inc(s_h3r, 1)
                elif kind == "x3r":
                    B.filled(act, *job)
                    own(act.copy(x3_rows[:, i // 2, (i % 2) * 512:(i % 2 + 1) * 512], bank))
                    act.sem_inc(free[b], 1)
                    act.sem_inc(s_x3r, 1)
                elif kind == "g2r":
                    B.filled(act, *job)
                    own(act.copy(g2_row[:, i * 512:(i + 1) * 512], bank))
                    act.sem_inc(free[b], 1)
                    act.sem_inc(s_x3r, 1)

            act.wait_ge(s_slots, 1)
            total = act.value_load(total_i[0:1, 0:1].bitcast(I32), min_val=E, max_val=MAX_PASSES)
            with act.Fori(0, total) as q:
                own.enter(q, 6)

                def copy_out(job, dst, src, done):
                    X.filled(act, q, job)
                    own(act.copy(dst, src))
                    act.sem_inc(x_free[EXPERT_BANK[job] - 4], 1)
                    act.sem_inc(done, 1)

                def tokens(half, job):
                    copy_out(job, xg[:, 4 * half:4 * half + 4, :],
                             ps[:, EXPERT_BANK[job], :].rearrange("p (a b) -> p a b", b=P), s_xg)

                copy_out("Zg", z_sb[:, 0, :], ps[:, EXPERT_BANK["Zg"], :], s_zc)
                copy_out("Zu", z_sb[:, 1, :], ps[:, EXPERT_BANK["Zu"], :], s_zc)
                act.wait_ge(s_g, q + 1)
                fn(sg_act, g_act, ACT.Sigmoid, scale=ALPHA).then_inc(s_sg, 1)
                tokens(0, "G0")
                tokens(1, "G1")
                copy_out("S", selgT, ps[:, EXPERT_BANK["S"], 0:T], s_selgT)
                copy_out("D", yg, ps[:, EXPERT_BANK["D"], :], s_yg)
                own.leave_open()
            act.wait_ge(s_y, 1)
            fn(smallM[:, 2:4], smallM[:, 2:4], ACT.Sqrt, bias=eps[:, 1:2], scale=1.0 / D).then_inc(s_yroot, 1)

        @block.vector
        def _(dve):
            own = Own(dve, s_v)
            ts, tt, stt = dve.tensor_scalar, dve.tensor_tensor, dve.scalar_tensor_tensor

            dve.wait_ge(s_cols, 16)
            dve.wait_ge(s_const, 1)
            def small_chains():
                for i in range(2):
                    own.mark(dve.tensor_tensor_reduce(lams[:, 2 * i, :], lams[:, 2 * i, :], lams[:, 2 * i + 1, :], 1.0,
                                                      0.0, ALU.mult, ALU.add, small[:, i:i + 1]))
                lam_r = col("rg_lambda", 0, CR)
                own(ts(sp[:, 2, :], lam_r, -1.0, None, ALU.mult))
                own(tt(sp[:, 0, :], sp[:, 2, :], lam_r, ALU.min))
                dve.sem_inc(s_spw, 1)
                dve.wait_ge(s_sp, 1)
                own(tt(small[:, 4:5], small[:, 2:3], small[:, 3:4], ALU.subtract))
                own(ts(small[:, 4:5], small[:, 4:5], LAM_INIT, None, ALU.add))
                lam = small[:, 4:5]
                own(ts(small[:, 5:6], col("subln_g"), 1.0 - LAM_INIT, None, ALU.mult))
                sub_g = small[:, 5:6]
                y, s_, s2, acc = sp[:, 1, :], sp[:, 3, :], sp[:, 4, :], sp[:, 5, :]
                own(ts(s_, y, 2.0, None, ALU.add))
                own(dve.reciprocal(s_, s_))
                own(tt(s_, s_, y, ALU.mult))
                own(tt(s2, s_, s_, ALU.mult))
                own(ts(acc, s2, 1.0 / 17, 1.0 / 15, ALU.mult, ALU.add))
                for k in (13, 11, 9, 7, 5, 3, 1):
                    own(tt(acc, acc, s2, ALU.mult))
                    own(ts(acc, acc, 1.0 / k, None, ALU.add))
                own(tt(acc, acc, s_, ALU.mult))
                own(ts(sp[:, 2, :], sp[:, 2, :], 0.0, None, ALU.max))
                own(stt(acc, acc, 2.0, sp[:, 2, :], ALU.mult, ALU.add))
                own(ts(acc, acc, 16.0, None, ALU.mult))
                return lam, sub_g, acc

            def ada(n):
                unit_loaded(dve, "w_ada", n)
                w = unit("w_ada", n).rearrange("p (c n) -> p c n", n=D)
                if n == 0:
                    dve.wait_ge(s_silu, 1)
                for j in range(4):
                    m = 4 * n + j
                    own.mark(dve.tensor_tensor_reduce(w[:, j, :], w[:, j, :], c_row, 1.0, 0.0, ALU.mult, ALU.add,
                                                      mod[:, m:m + 1]))
                own.settle()
                dve.sem_inc(unit_used("w_ada", n), 1)

            def norm_h(coef):
                own(dve.reciprocal(rstd, rstd))
                for c in range(KD):
                    stt(hT[:, c, :], xT[:, c, :], coef(c), rstd, ALU.mult, ALU.mult).then_inc(s_h, 1)

            def top16(values, best, where, n):
                for half in range(2):
                    s = slice(8 * half, 8 * half + 8)
                    for r in range(n):
                        own.mark(dve.max(best[:, r, s], values[:, r, :]))
                    own.settle_apart()
                    for r in range(n):
                        own.mark(dve.max_index(where[:, r, s], best[:, r, s], values[:, r, :]))
                    own.settle_apart()
                    if half == 0:
                        for r in range(n):
                            own.mark(dve.match_replace(values[:, r, :], best[:, r, s], values[:, r, :], -3e38))
                        own.settle_apart()

            n_best = 2 + 20 + 5 + 1

            def best_keys(pair):
                flat = all_scores.rearrange("p r k -> p (r k)")[:, bass.ds(pair * (4 * PK), 4 * PK)]
                own.mark(dve.tensor_copy(pair_scores.rearrange("p r k -> p (r k)"), flat))
                own.settle_apart()
                top16(pair_scores, top, top_i.bitcast(U32), 4)
                own(dve.tensor_copy(top_f, top_i.bitcast(U32)))

            n_route = 28 + 6

            def route(pair):
                four = [P, 2, TOPK, TOPK]

                def of_half(x, c):
                    return x.rearrange("p (h c) k -> p h c k", c=2)[:, :, c, :]

                own.mark(tt(cand.rearrange("p h (x y) -> p h x y", y=TOPK), of_half(top, 0).unsqueeze(3).to_broadcast(four),
                       of_half(top, 1).unsqueeze(2).to_broadcast(four), ALU.add))
                own.settle_apart()
                top16(cand, top_s, pos.bitcast(U32), 2)
                own(dve.tensor_copy(soft[:, 0:2], top_s[:, :, 0]))
                own(tt(top_s, top_s, soft[:, 0:2].unsqueeze(2).to_broadcast([P, 2, TOPK]), ALU.subtract))
                dve.sem_inc(s_soft_in, 1)
                hot4 = hot.rearrange("p (h k) x -> p h k x", k=TOPK)
                for op, arg, c, dst in ((ALU.logical_shift_right, 4, 0, i1_of), (ALU.bitwise_and, 15, 1, i2_of)):
                    own(ts(half_pos.bitcast(U32), pos.bitcast(U32), arg, None, op))
                    own(dve.tensor_copy(half_f, half_pos.bitcast(U32)))
                    own(tt(hot4, half_f.unsqueeze(3).to_broadcast(four),
                           iota16.unsqueeze(1).unsqueeze(1).to_broadcast(four), ALU.is_equal))
                    own(tt(hot4, hot4, of_half(top_f, c).unsqueeze(2).to_broadcast(four), ALU.mult))
                    own(dve.tensor_reduce(dst, hot4, AX, ALU.add))
                own(stt(i1_of, i1_of, float(PK), i2_of, ALU.mult, ALU.add))
                own(dve.tensor_copy(route_idx.bitcast(U32), i1_of))
                dve.sem_inc(s_route, 1)
                dve.wait_ge(s_soft, pair + 1)
                own(dve.tensor_reduce(soft[:, 2:4], top_s, AX, ALU.add))
                own(dve.reciprocal(soft[:, 2:4], soft[:, 2:4]))
                own(tt(route_g, top_s, soft[:, 2:4].unsqueeze(2).to_broadcast([P, 2, TOPK]), ALU.mult))

            ada_at = {("q", 0): 0, ("q", 2): 1, ("k", 0): 2, ("k", 2): 3, ("v", 0): 4, ("v", 2): 5,
                      ("yr", 1): 6, ("yr", 3): 7, ("gate", 0): 8, ("gate", 2): 9, ("gate", 4): 10, ("gate", 6): 11}
            for job in plan_first():
                kind, i = job[0], job[1] if len(job) > 1 else 0
                b = A.bank(*job)
                bank = ps[:, b, :]
                pair = bank.rearrange("p (a b) -> p a b", b=T)
                if job in ada_at:
                    ada(ada_at[job])
                if kind == "ss1":
                    dve.wait_ge(s_x, 16)
                    dve.wait_ge(s_root, 1)
                    norm_h(lambda c: col("norm1_g", c))
                    dve.wait_ge(s_par, 16 * 6)
                    lam, sub_g, decay_rate = small_chains()
                elif kind == "ss2":
                    dve.wait_ge(s_root, 2)
                    dve.wait_ge(full[A.bank("gate", 7)], A.number[("gate", 7)] // N_BANKS + 1)
                    norm_h(lambda c: col("norm2_g", c))
                elif kind == "xr":
                    dve.wait_ge(s_xr, i + 1)
                    if i >= 3:
                        A.filled(dve, "rg", 2 * (i - 3) + 1)
                    for tap in range(TAPS1):
                        for j in range(2):
                            c = 2 * i + j
                            src = xr[i % 2][:, j, tap:tap + T]
                            w = col("conv_w", c * TAPS1 + tap)
                            if tap == 0:
                                own.mark(ts(xc[i % 3][:, j, :], src, w, col("conv_b", c), ALU.mult, ALU.add))
                            else:
                                own.mark(stt(xc[i % 3][:, j, :], src, w, xc[i % 3][:, j, :], ALU.mult, ALU.add))
                        own.settle()
                    dve.sem_inc(s_xc, 1)
                elif kind == "rg" and i % 2 == 1:
                    n = i // 2
                    dve.wait_ge(s_ri, n + 1)
                    for j in range(2):
                        own.mark(ts(decay[:, j, :], ri[:, 0, j, :], decay_rate[:, 2 * n + j:2 * n + j + 1], None,
                                    ALU.mult))
                    own.settle()
                    dve.sem_inc(s_dec, 1)
                    coef = [1.0, -1.0 / 2, 1.0 / 6, -1.0 / 24, 1.0 / 120, -1.0 / 720]
                    own(ts(poly, decay, coef[5], None, ALU.mult))
                    for k in (4, 3, 2, 1, 0):
                        own(stt(poly, poly, coef[k], decay, ALU.add, ALU.mult))
                    own(tt(ri[:, 1], ri[:, 1], xc[n % 3], ALU.mult))
                    mask = ri[:, 0].bitcast(U32)
                    own(ts(mask, decay, 0.25, None, ALU.is_gt))
                    dve.wait_ge(s_expw, n + 1)
                    own(tt(decay, e_w, e_w, ALU.mult))
                    own(ts(decay, decay, -1.0, 1.0, ALU.mult, ALU.add))
                    own(dve.copy_predicated(poly, mask, decay))
                    own(ts(poly, poly, 1e-34, None, ALU.max))
                    dve.sem_inc(s_poly, 1)
                    dve.wait_ge(s_mult, n + 1)
                    own(tt(decay, poly, ri[:, 1], ALU.mult))
                    dve.sem_inc(s_rnn_free, 1)
                    for j in range(2):
                        own.mark(dve.tensor_tensor_scan(rnnT[:, 2 * n + j, :], e_w[:, j, :], decay[:, j, :], 0.0,
                                                        ALU.mult, ALU.add))
                    own.settle()
                elif kind == "yr":
                    dve.wait_ge(s_gel, i + 1)
                    own(tt(rnnT[:, 2 * i:2 * i + 2, :], rnnT[:, 2 * i:2 * i + 2, :], gelu_y, ALU.mult))
                    dve.sem_inc(s_gel_free, 1)
                elif kind in ("ssq", "ssk"):
                    n = i + (4 if kind == "ssk" else 0)
                    dst = (qT if kind == "ssq" else kT)[:, 2 * i:2 * i + 2, :]
                    bz = A.bank(kind[2], i)
                    dve.wait_ge(s_qroot, n + 1)
                    own(dve.reciprocal(inv, inv))
                    own(stt(dst, ps[:, bz, :].rearrange("p (a b) -> p a b", b=T), col(kind[2] + "_norm_g"), inv,
                            ALU.mult, ALU.mult))
                    dve.sem_inc(free[bz], 1)
                    dve.sem_inc(s_qroot_free, 1)
                elif kind == "s1":
                    b0 = A.bank("s0", i)
                    nm = small[:, 8 + 8 * (i % 2):12 + 8 * (i % 2)]
                    z = small[:, 12 + 8 * (i % 2):16 + 8 * (i % 2)]
                    A.filled(dve, "s0", i)
                    A.filled(dve, *job)
                    for bc in (b0, b):
                        diagonal = ps[:, bc, P:3 * P].rearrange("p (a b) -> p a b", b=P)
                        own.mark(dve.memset(diagonal[0:DH, :, DH:P], NEG))
                    own.settle()
                    for c, bc in ((0, b0), (1, b)):
                        own.mark(dve.tensor_reduce(nm[:, c:c + 1], ps[:, bc, 0:T], AX, ALU.max))
                        own.mark(dve.tensor_reduce(nm[:, 2 + c:3 + c], ps[:, bc, T:3 * P], AX, ALU.max))
                    own.settle()
                    own(ts(nm, nm, -DH ** -0.5, None, ALU.mult))
                    dve.sem_inc(s_nm, 1)
                    dve.wait_ge(s_exp, i + 1)
                    own(dve.reciprocal(z, z))
                    zl = small[:, 24 + 2 * (i % 2):26 + 2 * (i % 2)]
                    own.mark(ts(zl[:, 0:1], z[:, 1:2], lam, None, ALU.mult))
                    own(ts(zl[:, 1:2], z[:, 3:4], lam, None, ALU.mult))
                    buf = probs[i % 2]
                    halves = ((slice(0, T), z[:, 0:1], zl[:, 0:1]), (slice(T, 3 * P), z[:, 2:3], zl[:, 1:2]))
                    for keys, _, l in halves:
                        own.mark(ts(buf[:, 1, keys], buf[:, 1, keys], l, None, ALU.mult))
                    own.settle()
                    for keys, r, _ in halves:
                        own.mark(stt(buf[:, 0, keys], buf[:, 0, keys], r, buf[:, 1, keys], ALU.mult, ALU.subtract))
                    own.settle()
                    dve.sem_inc(s_diff, 1)
                elif kind == "dT":
                    A.filled(dve, *job)
                    if i >= 2:
                        A.filled(dve, "o", i - 2)
                    own(dve.tensor_copy(dT[i % 2], ps[:, b, 0:3 * P]))
                    dve.sem_inc(free[b], 1)
                    dve.sem_inc(s_dT, 1)
                elif kind == "osum":
                    bo = A.bank("o", i)
                    dve.wait_ge(s_oroot, i + 1)
                    own(dve.reciprocal(oinv, oinv))
                    own(stt(qT[:, i, :], ps[:, bo, 0:T], sub_g, oinv, ALU.mult, ALU.mult))
                    dve.sem_inc(free[bo], 1)
                    dve.sem_inc(s_o, 1)
                elif kind in ("brr", "bra"):
                    if i == 0:
                        dve.wait_ge(s_gate, KD)
                    g = 2 * i + (KD if kind == "brr" else 0)
                    dst = kT[:, 2 * i:2 * i + 2, :]
                    A.filled(dve, *job)
                    if kind == "brr":
                        own(tt(dst, pair, gates[:, g:g + 2, :], ALU.mult))
                        dve.sem_inc(free[b], 1)
                    else:
                        own(tt(sq, pair, gates[:, g:g + 2, :], ALU.mult))
                        dve.sem_inc(free[b], 1)
                        own(tt(dst, dst, sq, ALU.add))
                        dve.sem_inc(s_mrg, 1)
                elif kind == "wo":
                    A.filled(dve, *job)
                    own(tt(xT[:, 2 * i:2 * i + 2, :], pair, xT[:, 2 * i:2 * i + 2, :], ALU.add))
                    dve.sem_inc(free[b], 1)
                    dve.sem_inc(s_x1, 1)

            own(tt(mod, mod, col("b_ada", 0, 6 * KD), ALU.add))
            own.mark(stt(scale1, mod[:, KD:2 * KD], 1.0, col("norm1_g_2", 0, KD), ALU.add, ALU.mult))
            own(stt(scale2, mod[:, 4 * KD:5 * KD], 1.0, col("norm2_g_2", 0, KD), ALU.add, ALU.mult))

            dve.sem_inc(s_dot, 8)
            dve.wait_ge(s_iota, 1)
            own(dve.memset(all_scores[:, 4 * n_pairs:, :], 0.0))
            dve.wait_ge(s_ps, 1)
            best_keys(0)
            route(0)
            for tile in range(TT):
                dve.wait_ge(s_h2r, 2 * (tile + 1))
                with dve.Fori(0, PH // 2) as i:
                    own.enter(i, n_best + n_route)
                    for par in range(2):
                        g = tile * PH + par
                        for k in range(TOPK):
                            dve.wait_ge(u_full[k % 8], i * 64 + 16 * (2 * g + k // 8 + 1))
                            dve.tensor_tensor_reduce(u_rows[k % 8], u_rows[k % 8], h2_rows[:, tile, :], 1.0, 0.0,
                                                     ALU.mult, ALU.add, dots[:, par, k:k + 1]).then_inc(s_dot, 1)
                        dve.wait_ge(s_dot, i * 32 + TOPK * (g + 1) + 8)
                        dve.sem_inc(s_dots, 1)
                        dve.wait_ge(s_act, i * 2 + g + 1)
                        tt(wts[:, par, :], dots[:, par, :], route_g[:, par, :], ALU.mult).then_inc(s_wts, 1)
                        if par == 0:
                            dve.wait_ge(s_ps, n_pairs)
                            best_keys(i + tile * PH // 2 + 1)
                    dve.wait_ge(s_taken, i * 2 + tile * PH + 2)
                    route(i + tile * PH // 2 + 1)
                own.leave(PH // 2)

            def norm_hB(scale, shift):
                own(dve.reciprocal(rstd, rstd))
                for c in range(KD):
                    own.mark(stt(hT[:, c, :], xT[:, c, :], scale[:, c:c + 1], rstd, ALU.mult, ALU.mult))
                own.settle()
                for c in range(KD):
                    own.mark(ts(hT[:, c, :], hT[:, c, :], mod[:, shift + c:shift + c + 1], None, ALU.add))
                own.settle()
                dve.sem_inc(s_h, 1)

            def select(dst, e, part, gated):
                numbers = slots4[:, bass.ds(part * P, P)]
                for t in range(TT):
                    at_e = bass.ds(e, 1)
                    if gated:
                        own.mark(ts(dst[:, t, :], numbers, slot_of[:, t, at_e], gate_rows[:, t, at_e], ALU.is_equal,
                                    ALU.mult))
                    else:
                        own.mark(ts(dst[:, t, :], numbers, slot_of[:, t, at_e], None, ALU.is_equal))
                own.settle()

            taps = [(tap, c) for tap in range(TAPS2) for c in range(KC)]
            for job in plan_second():
                kind, i = job[0], job[1] if len(job) > 1 else 0
                b = B.bank(*job)
                bank = ps[:, b, :]
                pair = bank.rearrange("p (a b) -> p a b", b=T)
                if kind == "ss3":
                    dve.wait_ge(s_x2, 4)
                    dve.wait_ge(s_root, 2 + 1)
                    norm_hB(scale1, 0)
                elif kind == "ss4":
                    dve.wait_ge(s_root, 2 + 2)
                    norm_hB(scale2, 3 * KD)
                elif kind == "uv":
                    B.filled(dve, *job)
                    dve.wait_ge(s_sig, i + 1)
                    own(tt(pad[:, 2 * i:2 * i + 2, TAPS2 - 1:], pair, sigB[:, 2 * i:2 * i + 2, :], ALU.mult))
                    dve.sem_inc(free[b], 1)
                elif kind == "f":
                    B.filled(dve, *job)
                    x, y, l, w = (fx[0:DH, j, :] for j in range(4))
                    own(ts(x, ps[0:DH, b, 0:T], col("b_forget")[0:DH], None, ALU.add))
                    dve.sem_inc(free[b], 1)
                    own(ts(y, x, -1.0, None, ALU.mult))
                    own(tt(y, x, y, ALU.min))
                    dve.sem_inc(s_fe, 1)
                    own(ts(x, x, 0.0, None, ALU.min))
                    dve.wait_ge(s_fl, 1)
                    own(tt(x, x, l, ALU.subtract))
                    own(dve.memset(w, 1.0))
                    own(dve.tensor_tensor_scan(y, w, x, 0.0, ALU.mult, ALU.add))
                    own(ts(y, y, DH ** 0.5, None, ALU.mult))
                    dve.wait_ge(s_poolB, 1)
                    own.mark(ts(f_right[0:32, :], y[0:32, :], -1.0, None, ALU.mult))
                    own.mark(dve.tensor_copy(f_left[0:32], ident[0:32, 0:HB].unsqueeze(2).to_broadcast([32, HB, T])))
                    own.mark(tt(f_left[32:64], fx[32:64, 1, :].unsqueeze(1).to_broadcast([32, HB, T]),
                                ident[32:64, 32:32 + HB].unsqueeze(2).to_broadcast([32, HB, T]), ALU.mult))
                    own.settle()
                    dve.sem_inc(s_fm, 1)
                elif kind == "s":
                    nm = smallB[:, 2 * (i % 2):2 * (i % 2) + 2]
                    z = smallB[:, 4 + 2 * (i % 2):6 + 2 * (i % 2)]
                    B.filled(dve, *job)
                    diagonal = ps[:, b, P:3 * P].rearrange("p (a b) -> p a b", b=P)
                    own(tt(diagonal, diagonal, cmask.unsqueeze(1).to_broadcast([P, 2, P]), ALU.add))
                    own.mark(dve.tensor_reduce(nm[:, 0:1], ps[:, b, 0:T], AX, ALU.max))
                    own(dve.tensor_reduce(nm[:, 1:2], ps[:, b, T:3 * P], AX, ALU.max))
                    own(ts(nm, nm, -DH ** -0.5, None, ALU.mult))
                    dve.sem_inc(s_nm, 1)
                    for tap, c in taps[16 * i:16 * i + 16]:
                        src = pad[:, c, tap:tap + T]
                        w = col("conv_w_2", c * TAPS2 + tap)
                        if tap == 0:
                            own.mark(ts(conv[:, c, :], src, w, col("conv_b_2", c), ALU.mult, ALU.add))
                        else:
                            own.mark(stt(conv[:, c, :], src, w, conv[:, c, :], ALU.mult, ALU.add))
                        if c == KC - 1:
                            own.settle()
                    if i == HB - 1:
                        dve.sem_inc(s_conv, 1)
                    dve.wait_ge(s_exp, HA + i + 1)
                    own(dve.reciprocal(z, z))
                    for t, keys in ((0, slice(0, T)), (1, slice(T, 3 * P))):
                        own.mark(ts(pB[i % 2][:, keys], pB[i % 2][:, keys], z[:, t:t + 1], None, ALU.mult))
                    own.settle()
                    dve.sem_inc(s_diff, 1)
                elif kind == "dT":
                    B.filled(dve, *job)
                    if i >= 2:
                        B.filled(dve, "o", i - 2)
                    own(dve.tensor_copy(pTB[i % 2], ps[:, b, 0:3 * P]))
                    dve.sem_inc(free[b], 1)
                    dve.sem_inc(s_dT, 1)
                elif kind == "mean":
                    B.filled(dve, *job)
                    own(ts(meanB, ps[:, b, 0:T], 1.0 / CW, None, ALU.mult))
                    dve.sem_inc(free[b], 1)
                    own(tt(conv, conv, meanB.unsqueeze(1).to_broadcast([P, KC, T]), ALU.subtract))
                    dve.sem_inc(s_cen, 1)
                elif kind == "var":
                    dve.wait_ge(s_croot, 1)
                    dve.wait_ge(s_csq, 1)
                    own(dve.reciprocal(invB, invB))
                    own(tt(conv, conv, invB.unsqueeze(1).to_broadcast([P, KC, T]), ALU.mult))
                    dve.sem_inc(s_cn, 1)
                elif kind in ("bra", "brc"):
                    if i == 0:
                        dve.wait_ge(s_gate, KD + KD)
                    g = 2 * i + (KD if kind == "bra" else 0)
                    dst = mixed[:, 2 * i:2 * i + 2, :]
                    B.filled(dve, *job)
                    if kind == "bra":
                        own(tt(dst, pair, gates[:, g:g + 2, :], ALU.mult))
                        dve.sem_inc(free[b], 1)
                    else:
                        own(tt(sigB[:, 0:2, :], pair, gates[:, g:g + 2, :], ALU.mult))
                        dve.sem_inc(free[b], 1)
                        own(tt(dst, dst, sigB[:, 0:2, :], ALU.add))
                        dve.sem_inc(s_mrg, 1)
                elif kind == "wo":
                    B.filled(dve, *job)
                    for j in range(2):
                        c = 2 * i + j
                        own.mark(stt(xT[:, c, :], ps[:, b, j * T:(j + 1) * T], mod[:, 2 * KD + c:2 * KD + c + 1],
                                     xT[:, c, :], ALU.mult, ALU.add))
                    own.settle()
                    dve.sem_inc(free[b], 1)
                    dve.sem_inc(s_x1, 1)
                    if i == 3:
                        own(tt(g2_diag, ident.unsqueeze(1).to_broadcast([P, KD, P]),
                               mod[:, 5 * KD:6 * KD].unsqueeze(2).to_broadcast([P, KD, P]), ALU.mult))
                        dve.sem_inc(s_g2d, 1)
                elif kind == "route":
                    B.filled(dve, *job)
                    own.mark(dve.memset(logits[:, E:E + 4], 3e38))
                    own(tt(logits[:, 0:E], ps[:, b, 0:E], b_route, ALU.add))
                    dve.sem_inc(free[b], 1)
                    own(dve.max(m8, logits))
                    own(dve.match_replace(logits_r, m8, logits, -3e38))
                    own(ts(smallM[:, 0:1], m8[:, 4:5], -1.0, None, ALU.mult))
                    dve.sem_inc(s_rmax, 1)
                    dve.wait_ge(s_rexp, i + 1)
                    own(tt(logits_r[:, 0:E], logits_r[:, 0:E], logits[:, 0:E], ALU.not_equal))
                    own(tt(chosen, chosen, logits_r[:, 0:E], ALU.mult))
                    own(dve.tensor_reduce(smallM[:, 1:2], chosen, AX, ALU.add))
                    own(dve.reciprocal(smallM[:, 1:2], smallM[:, 1:2]))
                    own(ts(gate_rows[:, i, :], chosen, smallM[:, 1:2], None, ALU.mult))
                    dve.sem_inc(s_gr, 1)
                    if i == TT - 1:
                        own(ts(picked, gate_rows, 0.0, None, ALU.is_gt))
                        dve.sem_inc(s_pick, 1)
                elif kind == "rank":
                    B.filled(dve, *job)
                    dve.wait_ge(s_poolM, 1)
                    rank = ps[:, b, 0:2 * E].rearrange("p (a b) -> p a b", b=E)
                    own(stt(slot_of, rank, 1.0, picked, ALU.add, ALU.mult))
                    own(ts(slot_of, slot_of, -1.0, None, ALU.add))
                    count = n_pass[:, 3, :]
                    own(dve.tensor_copy(count, ps[:, b, 2 * E:3 * E]))
                    dve.sem_inc(free[b], 1)
                    own(ts(n_pass[:, 0, :], count, NS + 0.5, 1.0, ALU.is_gt, ALU.add))
                    for limit in (2 * NS, 3 * NS):
                        own(stt(n_pass[:, 0, :], count, limit + 0.5, n_pass[:, 0, :], ALU.is_gt, ALU.add))
                    own(dve.memset(n_pass[:, 2, :], 1.0))
                    own(dve.tensor_tensor_scan(n_pass[:, 1, :], n_pass[:, 2, :], n_pass[:, 0, :], 0.0, ALU.mult,
                                               ALU.add))
                    own(tt(n_pass[:, 2, :], n_pass[:, 1, :], n_pass[:, 0, :], ALU.subtract))
                    own(dve.tensor_copy(total_i[:, 0:1].bitcast(I32), n_pass[:, 1, E - 1:E]))
                    own(ts(count, n_pass[:, 1, :], -1.0, None, ALU.add))
                    own(dve.tensor_copy(last_of.bitcast(I32), count))
                    nq = [P, MAX_PASSES + 1, E]
                    own(tt(hit, n_pass[:, 1, :].unsqueeze(1).to_broadcast(nq), of_pass, ALU.is_le))
                    own(dve.tensor_reduce(table[:, 0, :], hit, AX, ALU.add))
                    own(ts(table[:, 0, :], table[:, 0, :], float(E - 1), None, ALU.min))
                    own(dve.tensor_copy(expert_of.bitcast(I32), table[:, 0, :]))
                    own(tt(hit, n_pass[:, 2, :].unsqueeze(1).to_broadcast(nq), of_pass, ALU.is_le))
                    own(tt(hit, hit, n_pass[:, 2, :].unsqueeze(1).to_broadcast(nq), ALU.mult))
                    own(dve.tensor_reduce(table[:, 1, :], hit, AX, ALU.max))
                    own(tt(table[:, 2, :], of_pass[:, :, 0], table[:, 1, :], ALU.subtract))
                    own(ts(table[:, 2, :], table[:, 2, :], 3.0, None, ALU.min))
                    own(dve.tensor_copy(part_of.bitcast(I32), table[:, 2, :]))
                    dve.sem_inc(s_slots, 1)
                    select(sel, 0, 0, False)
                    dve.sem_inc(s_sel, 1)
                elif kind == "gT":
                    B.filled(dve, *job)
                    own(dve.tensor_copy(gT[0:E, :], ps[0:E, b, 0:T]))
                    dve.sem_inc(free[b], 1)
                    dve.sem_inc(s_gT, 1)

            own(dve.tensor_copy(bias_now, b1[:, 0, :]))
            select(selg, 0, 0, True)
            dve.sem_inc(s_selg, 1)
            total = dve.value_load(total_i[0:1, 0:1].bitcast(I32), min_val=E, max_val=MAX_PASSES)
            with dve.Fori(0, total) as q:
                own.enter(q, 2 + 6 + 1 + 2)
                e = dve.value_load(expert_of[0:1, bass.ds(q + 1, 1)].bitcast(I32), min_val=0, max_val=E - 1)
                part = dve.value_load(part_of[0:1, bass.ds(q + 1, 1)].bitcast(I32), min_val=0, max_val=3)
                dve.wait_ge(s_xg, q * 2 + 2)
                select(sel, e, part, False)
                dve.sem_inc(s_sel, 1)
                g, u = g_act, u_act
                for n, (dst, job) in enumerate(((g, "Tg"), (u, "Tu"))):
                    bank = EXPERT_BANK[job]
                    bias = bias_now[:, n * KD:(n + 1) * KD].rearrange("p (h j) -> p j h", h=2)
                    X.filled(dve, q, job)
                    own(tt(dst.rearrange("p j (h s) -> p j h s", h=2),
                           ps[:, bank, :].rearrange("p (j h s) -> p j h s", j=4, h=2),
                           bias.unsqueeze(3).to_broadcast([P, 4, 2, NS]), ALU.add))
                    dve.sem_inc(x_free[bank - 4], 1)
                    if n == 0:
                        own(ts(g, g, LIMIT, None, ALU.min))
                        dve.sem_inc(s_g, 1)
                own(ts(u, u, LIMIT, -LIMIT, ALU.min, ALU.max))
                own(stt(u, u, 1.0, g, ALU.add, ALU.mult))
                dve.wait_ge(s_sg, q + 1)
                dve.wait_ge(s_yg, q + 1)
                own(tt(hm, u, sg_act, ALU.mult))
                dve.sem_inc(s_hm, 1)
                own(dve.tensor_copy(bias_now, b1[:, bass.ds(e, 1), :].rearrange("p e c -> p (e c)")))
                dve.wait_ge(s_selgT, q + 2)
                select(selg, e, part, True)
                dve.sem_inc(s_selg, 1)
                own.leave_open()
            end = Own(dve, s_vend)

            dve.wait_ge(s_fin, 1)
            dve.wait_ge(s_row, 16)
            for t in range(TT):
                for half in range(2):
                    h = slice(half * 512, (half + 1) * 512)
                    end(tt(y_rows[:, t, h], ps[:, 2 * t + half, :], g2_row[:, h], ALU.mult))
                end(tt(y_rows[:, t, :], y_rows[:, t, :], x3_rows[:, t, :], ALU.add))
                end(dve.tensor_tensor_reduce(x3_rows[:, t, :], y_rows[:, t, :], y_rows[:, t, :], 1.0, 0.0, ALU.mult,
                                             ALU.add, smallM[:, 2 + t:3 + t]))
            dve.sem_inc(s_y, 1)
            dve.wait_ge(s_yroot, 1)
            end(dve.reciprocal(smallM[:, 2:4], smallM[:, 2:4]))
            for t in range(TT):
                stt(y_rows[:, t, :], y_rows[:, t, :], smallM[:, 2 + t:3 + t], final_row, ALU.mult, ALU.mult)\
                    .then_inc(s_yn, 1)


def _units(w, columns):
    k, n = w.shape
    return np.ascontiguousarray(w.reshape(k // P, P, n // columns, columns).transpose(2, 1, 0, 3)).reshape(
        n // columns, P, k // P * columns)


def _chunks(v):
    return v.reshape(-1, P).T


def _layout(i):
    a = {}
    a["xT"] = np.ascontiguousarray(i["x"][0].T.reshape(KD, P, T).transpose(1, 0, 2))
    w_in = i["w_in"][0]
    a["w_in"] = _units(w_in, 512)
    a["w_br_rnn"] = _units(i["w_br_rnn"][0], 256)
    for name in ("w_br_attn", "w_out", "w_peer_q"):
        a[name] = _units(i[name][0], 512)
    a["sub_keys"] = np.ascontiguousarray(i["peer_sub_keys"][0].reshape(2 * PH, PK, P).transpose(2, 0, 1)).reshape(
        1, P, 2 * PH * PK)
    a["w_ada"] = np.ascontiguousarray(i["w_ada_2"][0].T.reshape(12, 4, P, D).transpose(0, 2, 1, 3)).reshape(
        12, P, 4 * D)
    a["peer_u"], a["peer_v"] = i["peer_u"][0], i["peer_v"][0]
    w = i["w_in_2"][0]
    a["w_in_2"] = np.concatenate([_units(w[:, 0:2560], 512), _units(w[:, 2568:], 512)])
    w_f = np.zeros((P, KD, DH), np.float32)
    for s in (0, 32):
        w_f[:, :, s:s + HB] = w[:, 2560:2568].reshape(KD, P, HB).transpose(1, 0, 2)
    a["w_f"] = w_f
    a["w_router"] = np.ascontiguousarray(i["w_router_2"][0].reshape(KD, P, E).transpose(1, 0, 2))
    a["w_attn_out_2"] = _units(i["w_attn_out_2"][0], D)
    a["w_conv_out_2"] = _units(i["w_conv_out_2"][0], D)
    a["w_out_2"] = _units(i["w_out_2"][0], 512)
    a["b_router"] = i["b_router_2"][0]
    a["b_exp_in"] = np.ascontiguousarray(i["b_exp_in_2"][0].reshape(E, 2 * KD, P).transpose(2, 0, 1))
    a["b_exp_out"] = i["b_exp_out_2"][0]
    a["final_g"] = i["final_g_2"]
    a["w_exp"] = w_exp = np.empty((E, 6, P, SLOT), np.float32)
    up = i["w_exp_in_2"][0].reshape(E, KD, P, 4, 512)
    w_exp[:, 0:4] = up.transpose(0, 3, 2, 1, 4).reshape(E, 4, P, SLOT)
    w_exp[:, 4:6] = i["w_exp_out_2"][0].reshape(E, 2, 4, P, D).transpose(0, 1, 3, 2, 4).reshape(E, 2, P, SLOT)
    gates = np.zeros((P, 2, CR, P), np.float32)
    for g, name in enumerate(("w_rg_a", "w_rg_x")):
        w = i[name][0].reshape(CR, 2, DH, DH)
        for s in range(2):
            gates[s * DH:(s + 1) * DH, g, :, s * DH:(s + 1) * DH] = w[:, s].transpose(1, 0, 2)
    a["w_rg"] = gates
    for name in ("lambda_q1", "lambda_k1", "lambda_q2", "lambda_k2"):
        a[name] = i[name][0]
    a["c_2"] = i["c_2"][0]
    cols = np.zeros((P, N_COLS), np.float32)

    def put(name, v):
        s, n = COLS[name]
        cols[0:v.shape[0], s:s + n] = v

    for name, key in (("norm1_g", "norm1_g"), ("b_gate", "b_gate"), ("conv_b", "conv_b"), ("b_rg_a", "b_rg_a"),
                      ("b_rg_x", "b_rg_x"), ("rg_lambda", "rg_lambda"), ("norm2_g", "norm2_g"), ("b_ada", "b_ada_2"),
                      ("norm1_g_2", "norm1_g_2"), ("conv_b_2", "conv_b_2"), ("conv_ln_g", "conv_ln_g_2"),
                      ("conv_ln_b", "conv_ln_b_2"), ("norm2_g_2", "norm2_g_2"), ("subln_g", "subln_g")):
        put(name, _chunks(i[key][0]))
    for name in ("q_norm_g", "k_norm_g"):
        put(name, np.concatenate([i[name][0], i[name][0]])[:, None])
    put("conv_w", i["conv_w"][0].reshape(TAPS1, CR, P).transpose(2, 1, 0).reshape(P, CR * TAPS1))
    put("conv_w_2", i["conv_w_2"][0].reshape(TAPS2, KC, P).transpose(2, 1, 0).reshape(P, KC * TAPS2))
    put("b_forget", i["b_forget_2"][0][:, None])
    cols[32:32 + HB, COLS["b_forget"][0]] = i["b_forget_2"][0]
    a["cols"] = cols
    return a


def kernel(**inputs):
    import concourse.bacc as bacc
    from concourse.bass_utils import run_bass_kernel_spmd

    nc = bacc.Bacc("TRN2", target_bir_lowering=False, num_devices=1)
    arrays, aps = {}, {}
    for name, v in _layout(inputs).items():
        arrays[f"in_{name}"] = v
        aps[name] = nc.dram_tensor(f"in_{name}", v.shape, F32, kind="ExternalInput").ap()
    out = nc.dram_tensor("out", (T, D), F32, kind="ExternalOutput").ap()
    build_program(nc, aps, out)
    r = run_bass_kernel_spmd(nc, [arrays], core_ids=[0])
    return r.results[0]["out"].reshape(1, T, D)
```
